# Optimizing a Trainium2 kernel written in Bass

```python
import math
import jax, jax.numpy as jnp
from jax import lax
import numpy as np

D_MODEL = 1024
BATCH = 1
SEQ = 512
DEPTH = 2

CHUNK = 64
Q_BLOCK = 128
HEAD_DIM = 64
A_HEADS = 4
A_V_DIM = 2 * HEAD_DIM
B_HEADS = 8
B_KV_HEADS = 2
B_GROUP = B_HEADS // B_KV_HEADS
WINDOW = 128
W_CHUNKS = WINDOW // CHUNK
BAND = (W_CHUNKS + 1) * CHUNK
C_HEADS = 8
IDX_HEADS = 4
IDX_DIM = 32
TOPK_MAX = 256
NUM_BUCKETS = 32
MAX_DISTANCE = 1024
REL_HEADS = A_HEADS + B_HEADS + C_HEADS
N_BRANCH = 3
BRANCH_WIDTH = 512
N_GROUPS = 4
EXPERTS_PER_GROUP = 4
N_EXPERTS = N_GROUPS * EXPERTS_PER_GROUP
TOP_E = 2
EXPERT_FF = 256
EPS = 1e-6
NEG = -1e30

COL_SIZES = (A_HEADS * 2 * HEAD_DIM, A_HEADS * 2 * HEAD_DIM, A_HEADS * A_V_DIM,
             B_HEADS * HEAD_DIM, B_KV_HEADS * HEAD_DIM, B_KV_HEADS * HEAD_DIM,
             C_HEADS * HEAD_DIM, HEAD_DIM, HEAD_DIM,
             IDX_HEADS * IDX_DIM, IDX_DIM, IDX_HEADS)
IN_COLS = sum(COL_SIZES)

kernel_name = 'hybrid_chunk_causal_block'

def rms_norm(x, g):
    xf = x.astype(jnp.float32)
    y = xf * lax.rsqrt(jnp.mean(xf * xf, axis=-1, keepdims=True) + EPS)
    return (y * g.astype(jnp.float32)).astype(x.dtype)

def t5_bucket(rel):
    half = NUM_BUCKETS // 2
    max_exact = half // 2
    n = jnp.abs(rel)
    n_f = jnp.maximum(n, 1).astype(jnp.float32)
    large = max_exact + (jnp.log(n_f / max_exact) / math.log(MAX_DISTANCE / max_exact)
                         * (half - max_exact)).astype(jnp.int32)
    large = jnp.minimum(large, half - 1)
    return jnp.where(rel > 0, half, 0) + jnp.where(n < max_exact, n, large)

def band_chunks(t, n_chunks):
    tc = t.reshape(t.shape[0], n_chunks, CHUNK, *t.shape[2:])
    pad = [(0, 0), (W_CHUNKS, 0)] + [(0, 0)] * (tc.ndim - 2)
    tp = jnp.pad(tc, pad)
    return jnp.concatenate([tp[:, i:i + n_chunks] for i in range(W_CHUNKS + 1)], axis=2)

def diff_attention(q, k, v, bias_tab, q_g, k_g, lam_par, subln_g, lambda_init):
    bsz, seq = q.shape[0], q.shape[1]
    n_blocks = seq // Q_BLOCK
    q = rms_norm(q, q_g) * (HEAD_DIM ** -0.5)
    k = rms_norm(k, k_g)
    lp = lam_par.astype(jnp.float32)
    lam = jnp.exp(jnp.sum(lp[0] * lp[1])) - jnp.exp(jnp.sum(lp[2] * lp[3])) + lambda_init
    q_blocks = jnp.moveaxis(q.reshape(bsz, n_blocks, Q_BLOCK, A_HEADS, 2, HEAD_DIM), 1, 0)
    starts = jnp.arange(n_blocks, dtype=jnp.int32) * Q_BLOCK
    key_pos = jnp.arange(seq, dtype=jnp.int32)

    def one_block(args):
        qb, start = args
        q_pos = start + jnp.arange(Q_BLOCK, dtype=jnp.int32)
        bias = bias_tab[t5_bucket(key_pos[None, :] - q_pos[:, None])]
        allowed = (key_pos[None, :] // CHUNK) <= (q_pos[:, None] // CHUNK)
        s = jnp.einsum('bqhmd,bkhmd->bhmqk', qb, k).astype(jnp.float32)
        s = s + jnp.transpose(bias, (2, 0, 1)).astype(jnp.float32)[None, :, None]
        s = jnp.where(allowed, s, NEG)
        p = jax.nn.softmax(s, axis=-1)
        p = p[:, :, 0] - lam * p[:, :, 1]
        return jnp.einsum('bhqk,bkhe->bqhe', p.astype(v.dtype), v)

    out = lax.map(one_block, (q_blocks, starts))
    out = jnp.moveaxis(out, 0, 1).reshape(bsz, seq, A_HEADS, A_V_DIM)
    out = rms_norm(out, subln_g) * (1.0 - lambda_init)
    return out.reshape(bsz, seq, A_HEADS * A_V_DIM)

def sliding_sink_attention(q, k, v, bias_tab, q_g, k_g, sinks):
    bsz, seq = q.shape[0], q.shape[1]
    n_chunks = seq // CHUNK
    q = rms_norm(q, q_g) * (HEAD_DIM ** -0.5)
    k = rms_norm(k, k_g)
    q = q.reshape(bsz, n_chunks, CHUNK, B_KV_HEADS, B_GROUP, HEAD_DIM)
    k_band = band_chunks(k, n_chunks)
    v_band = band_chunks(v, n_chunks)
    k_off = jnp.arange(BAND, dtype=jnp.int32) - W_CHUNKS * CHUNK
    q_off = jnp.arange(CHUNK, dtype=jnp.int32)
    bias = bias_tab[t5_bucket(k_off[None, :] - q_off[:, None])]
    bias = jnp.transpose(bias.reshape(CHUNK, BAND, B_KV_HEADS, B_GROUP), (2, 3, 0, 1)).astype(jnp.float32)
    valid = (jnp.arange(n_chunks, dtype=jnp.int32)[:, None] * CHUNK + k_off[None, :]) >= 0
    s = jnp.einsum('bcqhgd,bckhd->bchgqk', q, k_band).astype(jnp.float32) + bias
    s = jnp.where(valid[None, :, None, None, None, :], s, NEG)
    sink = sinks.astype(jnp.float32).reshape(B_KV_HEADS, B_GROUP)[None, None, :, :, None, None]
    m = jnp.maximum(jnp.max(s, axis=-1, keepdims=True), sink)
    e = jnp.exp(s - m)
    p = e / (jnp.sum(e, axis=-1, keepdims=True) + jnp.exp(sink - m))
    out = jnp.einsum('bchgqk,bckhd->bcqhgd', p.astype(v.dtype), v_band)
    return out.reshape(bsz, seq, B_HEADS * HEAD_DIM)

def dsa_attention(q, k, v, q_idx, k_idx, w_idx, bias_tab, q_g, k_g):
    bsz, seq = q.shape[0], q.shape[1]
    n_blocks = seq // Q_BLOCK
    top_k = min(TOPK_MAX, seq // 4)
    q = rms_norm(q, q_g) * (HEAD_DIM ** -0.5)
    k = rms_norm(k, k_g)
    w_idx = w_idx.astype(jnp.float32) * (IDX_HEADS ** -0.5 * IDX_DIM ** -0.5)

    def blocks(t):
        return jnp.moveaxis(t.reshape(bsz, n_blocks, Q_BLOCK, *t.shape[2:]), 1, 0)

    starts = jnp.arange(n_blocks, dtype=jnp.int32) * Q_BLOCK
    key_chunk = jnp.arange(seq, dtype=jnp.int32) // CHUNK
    gather = jax.vmap(lambda table, idx: table[idx])

    def one_block(args):
        qb, qib, wib, start = args
        q_pos = start + jnp.arange(Q_BLOCK, dtype=jnp.int32)
        q_chunk = q_pos // CHUNK
        logits = jnp.einsum('bqhd,bkd->bqhk', qib, k_idx).astype(jnp.float32)
        score = jnp.einsum('bqhk,bqh->bqk', jax.nn.relu(logits), wib)
        score = jnp.where(key_chunk[None, None, :] <= q_chunk[None, :, None], score, NEG)
        _, sel = lax.top_k(score, top_k)
        k_sel = gather(k, sel)
        v_sel = gather(v, sel)
        bias = bias_tab[t5_bucket(sel - q_pos[None, :, None])]
        ok = (sel // CHUNK) <= q_chunk[None, :, None]
        s = jnp.einsum('bqhd,bqkd->bqhk', qb, k_sel).astype(jnp.float32)
        s = s + jnp.swapaxes(bias, -1, -2).astype(jnp.float32)
        s = jnp.where(ok[:, :, None, :], s, NEG)
        p = jax.nn.softmax(s, axis=-1)
        return jnp.einsum('bqhk,bqkd->bqhd', p.astype(v.dtype), v_sel)

    out = lax.map(one_block, (blocks(q), blocks(q_idx), blocks(w_idx), starts))
    return jnp.moveaxis(out, 0, 1).reshape(bsz, seq, C_HEADS * HEAD_DIM)

def hybrid_mixer(h, rel_bias, w_in, qk_g, lam_par, subln_g, sinks, w_branch, w_gate, b_gate, w_out, lambda_init):
    bsz, seq = h.shape[0], h.shape[1]
    proj = h @ w_in
    split_points = np.cumsum(COL_SIZES)[:-1].tolist()
    aq, ak, av, bq, bk, bv, cq, ck, cv, iq, ik, iw = jnp.split(proj, split_points, axis=-1)
    oa = diff_attention(aq.reshape(bsz, seq, A_HEADS, 2, HEAD_DIM),
                        ak.reshape(bsz, seq, A_HEADS, 2, HEAD_DIM),
                        av.reshape(bsz, seq, A_HEADS, A_V_DIM),
                        rel_bias[:, :A_HEADS], qk_g[0, 0], qk_g[0, 1], lam_par, subln_g, lambda_init)
    ob = sliding_sink_attention(bq.reshape(bsz, seq, B_HEADS, HEAD_DIM),
                                bk.reshape(bsz, seq, B_KV_HEADS, HEAD_DIM),
                                bv.reshape(bsz, seq, B_KV_HEADS, HEAD_DIM),
                                rel_bias[:, A_HEADS:A_HEADS + B_HEADS], qk_g[1, 0], qk_g[1, 1], sinks)
    oc = dsa_attention(cq.reshape(bsz, seq, C_HEADS, HEAD_DIM), ck, cv,
                       iq.reshape(bsz, seq, IDX_HEADS, IDX_DIM), ik, iw,
                       rel_bias[:, A_HEADS + B_HEADS:], qk_g[2, 0], qk_g[2, 1])
    branches = jnp.stack([oa, ob, oc], axis=2)
    y = jnp.einsum('bsnw,nwd->bsnd', branches, w_branch)
    gates = jax.nn.sigmoid(h @ w_gate + b_gate).reshape(bsz, seq, N_BRANCH, D_MODEL)
    return jnp.sum(gates * y, axis=2) @ w_out

def hier_moe(h, w_rg, b_rg, w_re, b_re, w_g, w_u, w_d):
    bsz, seq = h.shape[0], h.shape[1]
    g_logits = (h @ w_rg + b_rg).astype(jnp.float32)
    g_prob = jax.nn.softmax(g_logits, axis=-1)
    _, g_sel = lax.top_k(g_logits, 1)
    p_group = jnp.take_along_axis(g_prob, g_sel, axis=-1)
    e_logits = (h @ w_re + b_re).astype(jnp.float32).reshape(bsz, seq, N_GROUPS, EXPERTS_PER_GROUP)
    e_in_group = jnp.take_along_axis(e_logits, g_sel[..., None], axis=2)[:, :, 0]
    e_val, e_sel = lax.top_k(e_in_group, TOP_E)
    weights = jax.nn.softmax(e_val, axis=-1) * p_group
    expert_id = g_sel * EXPERTS_PER_GROUP + e_sel
    gate = jnp.sum(jax.nn.one_hot(expert_id, N_EXPERTS, dtype=jnp.float32) * weights[..., None], axis=2)
    hid = jax.nn.silu(jnp.einsum('bsd,edf->bsef', h, w_g)) * jnp.einsum('bsd,edf->bsef', h, w_u)
    hid = hid * gate[..., None].astype(hid.dtype)
    return jnp.einsum('bsef,efd->bsd', hid, w_d)

def setup_inputs(seed: int = 0) -> dict:
    key = jax.random.key(seed)
    ks = jax.random.split(key, 20)

    def nrm(k, shape, scale):
        return jax.random.normal(k, shape, jnp.float32) * scale

    return {
        'x': nrm(ks[0], (BATCH, SEQ, D_MODEL), 1.0),
        'rel_bias': nrm(ks[1], (NUM_BUCKETS, REL_HEADS), 0.5),
        'norm_mix_g': 1.0 + nrm(ks[2], (DEPTH, D_MODEL), 0.05),
        'w_in': nrm(ks[3], (DEPTH, D_MODEL, IN_COLS), D_MODEL ** -0.5),
        'qk_norm_g': 1.0 + nrm(ks[4], (DEPTH, N_BRANCH, 2, HEAD_DIM), 0.05),
        'diff_lambda': nrm(ks[5], (DEPTH, 4, HEAD_DIM), 0.1),
        'diff_subln_g': 1.0 + nrm(ks[6], (DEPTH, A_V_DIM), 0.05),
        'sinks': nrm(ks[7], (DEPTH, B_HEADS), 0.5),
        'w_branch': nrm(ks[8], (DEPTH, N_BRANCH, BRANCH_WIDTH, D_MODEL), BRANCH_WIDTH ** -0.5),
        'w_gate': nrm(ks[9], (DEPTH, D_MODEL, N_BRANCH * D_MODEL), D_MODEL ** -0.5),
        'b_gate': nrm(ks[10], (DEPTH, N_BRANCH * D_MODEL), 0.02),
        'w_out': nrm(ks[11], (DEPTH, D_MODEL, D_MODEL), D_MODEL ** -0.5),
        'norm_ffn_g': 1.0 + nrm(ks[12], (DEPTH, D_MODEL), 0.05),
        'w_router_group': nrm(ks[13], (DEPTH, D_MODEL, N_GROUPS), D_MODEL ** -0.5),
        'b_router_group': nrm(ks[14], (DEPTH, N_GROUPS), 0.01),
        'w_router_expert': nrm(ks[15], (DEPTH, D_MODEL, N_EXPERTS), D_MODEL ** -0.5),
        'b_router_expert': nrm(ks[16], (DEPTH, N_EXPERTS), 0.01),
        'w_ff_gate': nrm(ks[17], (DEPTH, N_EXPERTS, D_MODEL, EXPERT_FF), D_MODEL ** -0.5),
        'w_ff_up': nrm(ks[18], (DEPTH, N_EXPERTS, D_MODEL, EXPERT_FF), D_MODEL ** -0.5),
        'w_ff_down': nrm(ks[19], (DEPTH, N_EXPERTS, EXPERT_FF, D_MODEL), EXPERT_FF ** -0.5),
    }

def reference(x, rel_bias, norm_mix_g, w_in, qk_norm_g, diff_lambda, diff_subln_g, sinks,
              w_branch, w_gate, b_gate, w_out, norm_ffn_g, w_router_group, b_router_group,
              w_router_expert, b_router_expert, w_ff_gate, w_ff_up, w_ff_down):
    for l in range(DEPTH):
        lambda_init = 0.8 - 0.6 * math.exp(-0.3 * l)
        h = rms_norm(x, norm_mix_g[l])
        x = x + hybrid_mixer(h, rel_bias, w_in[l], qk_norm_g[l], diff_lambda[l], diff_subln_g[l],
                             sinks[l], w_branch[l], w_gate[l], b_gate[l], w_out[l], lambda_init)
        h = rms_norm(x, norm_ffn_g[l])
        x = x + hier_moe(h, w_router_group[l], b_router_group[l], w_router_expert[l], b_router_expert[l],
                         w_ff_gate[l], w_ff_up[l], w_ff_down[l])
    return x


_drawn_inputs = setup_inputs


def setup_inputs(seed=0):
    import zlib

    import numpy as np

    out = dict(_drawn_inputs(seed))
    spreads = {}
    factors = {'sinks': 8.0, 'b_gate': 2.763, 'b_router_group': 3.116, 'b_router_expert': 3.148}
    for name, (base, spread) in spreads.items():
        noise = np.random.default_rng([zlib.crc32(name.encode()), seed]).standard_normal(out[name].shape)
        drawn = base * np.exp(spread * noise) if base else spread * noise
        out[name] = __import__('jax').numpy.asarray(drawn.astype(out[name].dtype))
    for name, factor in factors.items():
        out[name] = (out[name] * factor).astype(out[name].dtype)
    return out
```

```python
import math
from contextlib import ExitStack

import numpy as np

import concourse.bass as bass
from concourse import mybir

F32 = mybir.dt.float32
F32R = mybir.dt.float32r
ALU = mybir.AluOpType
ACT = mybir.ActivationFunctionType
AX = mybir.AxisListType

P = 128
D_MODEL, SEQ, DEPTH = 1024, 512, 2
CHUNK, HD = 64, 64
A_HEADS, B_HEADS, B_KV, C_HEADS = 4, 8, 2, 8
IDX_HEADS, IDX_DIM = 4, 32
TOP_K = min(256, SEQ // 4)
N_BUCKETS, MAX_DIST = 32, 1024
REL_HEADS = A_HEADS + B_HEADS + C_HEADS
N_BRANCH, WIDTH = 3, 512
N_GROUPS, PER_GROUP = 4, 4
N_EXPERTS = N_GROUPS * PER_GROUP
FF = 256
EPS = 1e-6
NEG = -1e30
LOWEST = -3e38
TAKEN_BELOW = -2e38

TT = SEQ // P
KT = D_MODEL // P
RAW_SLOTS = 3
UNIT_KT = 2
SPAN = 640

P_CHUNKS = [("I", 2816, 292), ("Aq", 0, 512), ("Ak", 512, 512), ("Av", 1024, 512),
            ("Bq", 1536, 512), ("Bkv", 2048, 256), ("Cq", 2304, 512)]
UNITS_K = KT // UNIT_KT
T_BLOCKS = {"I": 3, "Aq": 4, "Ak": 4, "Av": 0, "Bq": 4, "Bkv": 2, "Cq": 4}

ROW_MIX, ROW_FFN, ROW_BGATE, ROW_QK, ROW_SUBLN, N_ROWS = 0, 8, 16, 40, 46, 47


class Branch:

    def __init__(self, n, name, heads, lag, per_block, fill, first_head, first_job, first_fill, groups):
        self.n, self.name, self.heads, self.lag, self.per_block = n, name, heads, lag, per_block
        self.fill, self.first_head, self.first_job = fill, first_head, first_job
        self.jobs = heads * TT
        self.blocks = self.jobs // per_block
        self.slots = self.jobs + lag + 3
        self.t_index, self.o_index = {}, {}
        at = first_fill
        for s in range(self.slots):
            if 0 <= s - lag < self.jobs:
                self.t_index[s - lag] = at
                at += 1
            b = self.block_turned(s)
            if b is not None:
                self.o_index[b] = at
                at += 1
        self.end_fill = at
        self.dense = groups

    def block_turned(self, s):
        b, r = divmod(s - self.lag - 3 + 1, self.per_block)
        return b - 1 if r == 0 and 1 <= b <= self.blocks else None

    def block_scaled(self, s):
        b, r = divmod(s - self.lag - 2 + 1, self.per_block)
        return b - 1 if r == 0 and 1 <= b <= self.blocks else None

    def groups_of(self, s):
        return range(self.fill * s, self.fill * (s + 1)) if s < self.jobs else range(0)

    def job(self, j):
        h, i = divmod(j, TT)
        if self.name == "B":
            tiles = [i - 1, i] if i else [0]
        else:
            tiles = list(range(i + 1))
        nk = P * len(tiles)
        return h, i, SEQ - nk, nk, tiles


def gate_chunk(n, c):
    return len(P_CHUNKS) + 4 * n + c


def y_chunk(n, c):
    return len(P_CHUNKS) + 4 * n + 2 + c


OUT_CHUNK = len(P_CHUNKS) + 4 * N_BRANCH
N_CHUNKS = OUT_CHUNK + 2
GATE_GROUPS = 2 * 4 * KT
Y_GROUPS = 2 * 4 * (WIDTH // P)
P_FILLS = sum(T_BLOCKS.values())


def make_branches():
    a = Branch(0, "A", A_HEADS, 1, TT, 4, 0, 0, P_FILLS, [("gate", 0)])
    b = Branch(1, "B", B_HEADS, 2, 2 * TT, 3, A_HEADS, a.jobs, a.end_fill, [("y", 0), ("gate", 1)])
    c = Branch(2, "C", C_HEADS, 2, 2 * TT, 3, A_HEADS + B_HEADS, a.jobs + b.jobs, b.end_fill,
               [("y", 1), ("gate", 2)])
    return [a, b, c]


def dense_groups(dense):
    out = []
    for kind, n in dense:
        units = UNITS_K if kind == "gate" else WIDTH // P // UNIT_KT
        for c in range(2):
            for u in range(units):
                for t in range(4):
                    for k in range(UNIT_KT):
                        out.append((kind, n, c, u, t, k, u == 0 and k == 0,
                                    u == units - 1 and k == UNIT_KT - 1, t == 3 and k == UNIT_KT - 1))
    return out


def unit_list():
    out = [("in", i, u) for i in range(len(P_CHUNKS)) for u in range(UNITS_K)]
    for n in range(N_BRANCH):
        out += [("gate", n, c, u) for c in range(2) for u in range(UNITS_K)]
        out += [("y", n, c, u) for c in range(2) for u in range(WIDTH // P // UNIT_KT)]
    out += [("out", c, u) for c in range(2) for u in range(UNITS_K)]
    return out


def hybrid_block(nc, x, rel_bias, norm_mix_g, w_in, qk_norm_g, diff_lambda, diff_subln_g, sinks, w_branch,
                 w_gate, b_gate, w_out, norm_ffn_g, w_router_group, b_router_group, w_router_expert,
                 b_router_expert, w_ff_gate, w_ff_up, w_ff_down, bucket_onehot, identity, flip, layer_consts,
                 out):
    units = unit_list()
    unit_at = {u: n for n, u in enumerate(units)}
    branches = make_branches()
    n_jobs = sum(b.jobs for b in branches)
    ctx = ExitStack()

    def sb(name, shape, dt=F32):
        return ctx.enter_context(nc.sbuf_tensor(name, shape, dt))

    def sem(name):
        return ctx.enter_context(nc.semaphore(name))

    with ctx:
        X = sb("X", [P, TT, D_MODEL])
        gT = X[:, :, :].rearrange("p t (a n) -> p (t a) n", a=2)
        hT_hi = sb("hT_hi", [P, KT, SEQ], F32R)
        hT_lo = sb("hT_lo", [P, KT, SEQ], F32R)
        raw = sb("raw", [P, RAW_SLOTS, UNIT_KT, 512])
        w_hi = sb("w_hi", [P, 2, UNIT_KT, 512], F32R)
        w_lo = sb("w_lo", [P, 2, UNIT_KT, 512], F32R)
        ptmp = sb("ptmp", [P, TT, 512])
        sq = sb("sq", [P, 2, 512])
        aqT = sb("aqT", [P, 4, SEQ])
        akT = sb("akT", [P, 4, SEQ])
        bqT = sb("bqT", [P, 4, SEQ])
        bkT = sb("bkT", [P, 2, SEQ])
        cqT = sb("cqT", [P, 4, SEQ])
        ckT = sb("ckT", [P, SEQ])
        iqT = sb("iqT", [P, SEQ])
        ikT = sb("ikT", [P, SEQ])
        av = sb("av", [P, TT, 512])
        bv = sb("bv", [P, TT, B_KV * HD])
        cv = sb("cv", [P, TT, HD])
        iw = sb("iw", [P, TT, IDX_HEADS])
        bias = sb("bias", [P, 2, SEQ])
        score = sb("score", [P, P * (2 + 3 + 4)])
        top8 = sb("top8", [P, 8])
        mixed = sb("mixed", [P, KT, SEQ])
        xn = mixed[:, :, :].rearrange("p (t a) n -> p t (a n)", a=2)
        ytmp = sb("ytmp", [P, SEQ])
        bias_sel = ytmp
        oT_hi = sb("oT_hi", [P, 4, SEQ], F32R)
        oT_lo = sb("oT_lo", [P, 4, SEQ], F32R)
        o_rows = sb("o_rows", [P, 2, TT, P])
        probs = sb("probs", [P, 4, SEQ])
        pT = sb("pT", [P, 2, SEQ])
        ident = sb("ident", [P, P])
        prow = sb("prow", [N_ROWS, P])
        pcol = sb("pcol", [P, N_ROWS])
        q_gain = sb("q_gain", [P, N_BRANCH])
        sub_gain = sb("sub_gain", [P, 1])
        lam_rows = sb("lam_rows", [P, 4 * HD])
        lam_sum = sb("lam_sum", [P, 2])
        lam_exp = sb("lam_exp", [P, 2])
        lam_dif = sb("lam_dif", [P, 1])
        neg_lam = sb("neg_lam", [P, 1])
        lconst = sb("lconst", [P, 2])
        sink_row = sb("sink_row", [P, B_HEADS])
        half_neg = sb("half_neg", [P, 32])
        row_ss = sb("row_ss", [P, 2, TT])
        row_ms = sb("row_ms", [P, 2, TT])
        row_rs = sb("row_rs", [P, 2, TT])
        head_ss = sb("head_ss", [P, 2, 32])
        head_ms = sb("head_ms", [P, 2, 32])
        head_rs = sb("head_rs", [P, 2, 32])
        o_ss = sb("o_ss", [P, 2, TT])
        o_ms = sb("o_ms", [P, 2, TT])
        o_rs = sb("o_rs", [P, 2, TT])
        job_max = sb("job_max", [P, 4, 2])
        job_neg = sb("job_neg", [P, 4, 2])
        job_sum = sb("job_sum", [P, 4, 2])
        job_sink = sb("job_sink", [P, 4])
        job_den = sb("job_den", [P, 4])
        job_inv = sb("job_inv", [P, 4, 2])
        job_mix = sb("job_mix", [P, 4])
        wr = sb("wr", [P, KT, 20])
        wr_hi = sb("wr_hi", [P, KT, 20], F32R)
        wr_lo = sb("wr_lo", [P, KT, 20], F32R)
        br = sb("br", [P, 20])
        rt = sb("rt", [P, 16, 16])
        logit = sb("logit", [P, TT, 20])
        ein = sb("ein", [P, TT, 4, 4])
        gate16 = sb("gate16", [P, N_EXPERTS, TT])
        gate_cur = sb("gate_cur", [P, TT])

        banks = [ctx.enter_context(nc.psum_tensor(f"bank{i}", [P, 512], F32)) for i in range(8)]
        G = banks[0:4]
        S = banks[4:6]
        T = banks[6:8]
        O = banks[7]

        xs = nc.dram_tensor("residual_dram", (SEQ, D_MODEL), F32, kind="Internal").ap()
        toep = nc.dram_tensor("toeplitz_dram", (REL_HEADS, SPAN), F32, kind="Internal").ap()
        bias_dram = nc.dram_tensor("bias_dram", (REL_HEADS, P, SEQ), F32, kind="Internal").ap()

        pre_x = sem("pre_x")
        pre_c = sem("pre_c")
        pre_mm = sem("pre_mm")
        pre_row = sem("pre_row")
        pre_toep = sem("pre_toep")
        pre_in = [sem("pre_in0"), sem("pre_in1")]
        pre_flip = sem("pre_flip")
        pre_cp = sem("pre_cp")
        pre_set = sem("pre_set")
        pre_out = [sem("pre_out0"), sem("pre_out1")]
        pre_half = sem("pre_half")
        par = sem("par")
        raw_in = [sem(f"raw_in{i}") for i in range(RAW_SLOTS)]
        split_hi = sem("split_hi")
        split_done = sem("split_done")
        unit_used = sem("unit_used")
        par_turned = sem("par_turned")
        pcol_ready = sem("pcol_ready")
        lam_summed = sem("lam_summed")
        lam_exped = sem("lam_exped")
        gains_ready = sem("gains_ready")
        ss_done = sem("ss_done")
        ms_done = sem("ms_done")
        rs_done = sem("rs_done")
        xn_done = sem("xn_done")
        nt_done = sem("nt_done")
        nhi_done = sem("nhi_done")
        nlo_done = sem("nlo_done")
        g_done = sem("g_done")
        g_free = sem("g_free")
        chunk_copied = sem("chunk_copied")
        squared = sem("squared")
        reduced = sem("reduced")
        cms_done = sem("cms_done")
        crs_done = sem("crs_done")
        chunk_normed = sem("chunk_normed")
        t_done = sem("t_done")
        t_free = sem("t_free")
        idx_done = sem("idx_done")
        relu_done = sem("relu_done")
        relu_used = sem("relu_used")
        s_done = sem("s_done")
        soft_done = sem("soft_done")
        exp_done = sem("exp_done")
        p_ready = sem("p_ready")
        pv_done = sem("pv_done")
        o_free = sem("o_free")
        oms_done = sem("oms_done")
        ors_done = sem("ors_done")
        o_scaled = sem("o_scaled")
        ohi_done = sem("ohi_done")
        bias_in = [sem("bias_in0"), sem("bias_in1")]
        x_back = sem("x_back")
        dve = sem("dve")
        wrhi_done = sem("wrhi_done")
        wr_split = sem("wr_split")
        log_done = sem("log_done")
        rexp_in = sem("rexp_in")
        rexp_out = sem("rexp_out")
        layer_out = sem("layer_out")
        layer_sems = [par, *raw_in, split_hi, split_done, unit_used, par_turned, pcol_ready, lam_summed, lam_exped,
                      gains_ready, ss_done, ms_done, rs_done, xn_done, nt_done, nhi_done, nlo_done, g_done, g_free,
                      chunk_copied, squared, reduced, cms_done, crs_done, chunk_normed, t_done, t_free, idx_done,
                      relu_done, relu_used, s_done, soft_done, exp_done, p_ready, pv_done, o_free, oms_done,
                      ors_done, o_scaled, ohi_done, *bias_in, x_back, dve, wrhi_done, wr_split, log_done, rexp_in,
                      rexp_out, layer_out]
        e_raw = [sem(f"e_raw{i}") for i in range(RAW_SLOTS)]
        e_hi = sem("e_hi")
        e_split = sem("e_split")
        e_used = sem("e_used")
        e_gu = sem("e_gu")
        e_silu = sem("e_silu")
        e_dve = sem("e_dve")
        e_hid = sem("e_hid")
        e_down = sem("e_down")
        e_free = sem("e_free")
        expert_sems = [*e_raw, e_hi, e_split, e_used, e_gu, e_silu, e_dve, e_hid, e_down, e_free]
        expert_end = [sem("expert_done"), sem("expert_go"), sem("expert_ack")]
        layer_end = [sem("layer_done"), sem("layer_go"), sem("layer_ack")]

        def meet_and_clear(sp, point, sems):
            meet_done, meet_go, meet_ack = point
            sp.wait_ge(meet_done, 4)
            for s in sems:
                sp.sem_clear(s)
            sp.sem_clear(meet_done)
            sp.sem_inc(meet_go, 1)
            sp.wait_ge(meet_ack, 4)
            sp.sem_clear(meet_go)
            sp.sem_clear(meet_ack)

        def meet(eng, point):
            meet_done, meet_go, meet_ack = point
            eng.drain()
            eng.sem_inc(meet_done, 1)
            eng.wait_ge(meet_go, 1)
            eng.sem_inc(meet_ack, 1)

        def layer_of(w, l):
            return w[bass.ds(l, 1)]

        def unit_source(unit, l):
            kind = unit[0]
            if kind == "in":
                _, c0, w = P_CHUNKS[unit[1]]
                src, u = layer_of(w_in, l)[:, :, c0:c0 + w], unit[2]
            elif kind == "gate":
                _, n, c, u = unit
                c0 = n * D_MODEL + c * 512
                src = layer_of(w_gate, l)[:, :, c0:c0 + 512]
            elif kind == "y":
                _, n, c, u = unit
                src = w_branch.rearrange("l n w d -> (l n) w d")[bass.ds(l * N_BRANCH + n, 1), :, c * 512:c * 512 + 512]
            else:
                _, c, u = unit
                src = layer_of(w_out, l)[:, :, c * 512:c * 512 + 512]
            src = src[:, u * UNIT_KT * P:(u + 1) * UNIT_KT * P, :]
            return src.rearrange("a (k p) n -> p (a k) n", p=P)

        chunk_names = list(dict.fromkeys(u[:-1] for u in units))

        def unit_end(n):
            k = chunk_names.index(units[n][:-1])
            if n + 1 == len(units) or units[n + 1][:-1] != units[n][:-1]:
                return True, 4 * (k + 1)
            return False, n + 1 - k

        E_UNITS = [("gu", u) for u in range(UNITS_K)] + [("down", c) for c in range(2)]

        def expert_raw_value(n):
            return sum(32 if E_UNITS[m][0] == "gu" else 16 for m in range(n % RAW_SLOTS, n + 1, RAW_SLOTS))

        block = ctx.enter_context(nc.Block())

        @block.sync
        def _(sp):
            sp.dma_start(X[:, :, :], x.rearrange("b (t p) d -> p (b t) d", p=P)).then_inc(pre_x, 16)
            sp.dma_start(ident[:, :], identity).then_inc(pre_c, 16)
            sp.dma_start(probs[:, 0, 0:P], flip).then_inc(pre_c, 16)
            sp.dma_start(probs[0:N_BUCKETS, 1, 0:REL_HEADS], rel_bias).then_inc(pre_c, 16)
            sp.dma_start(aqT[0:N_BUCKETS, 0:2, 0:SPAN // 2],
                         bucket_onehot.rearrange("b (a n) -> b a n", a=2)).then_inc(pre_c, 16)
            sp.wait_ge(pre_x, 16)
            sp.dma_start(xs.rearrange("(t p) d -> p t d", p=P), X[:, :, :]).then_inc(pre_x, 16)
            sp.wait_ge(pre_row, 2)
            sp.dma_start(toep.rearrange("h (a n) -> h a n", a=2),
                         akT[0:REL_HEADS, 0:2, 0:SPAN // 2]).then_inc(pre_toep, 16)
            sp.wait_ge(pre_toep, 16)
            for h in range(REL_HEADS + 2):
                if h < REL_HEADS:
                    if h >= 2:
                        sp.wait_ge(pre_flip, h - 1)
                    row = toep[h:h + 1, 0:SEQ]
                    shifted = bass.AP(row.tensor, row.offset, [[1, P], [1, SEQ]])
                    sp.dma_start(bqT[:, h % 2, :], shifted).then_inc(pre_in[h % 2], 16)
                if h >= 2:
                    sp.wait_ge(pre_set, h - 1)
                    sp.dma_start(bias_dram[h - 2], cqT[:, h % 2, :]).then_inc(pre_out[h % 2], 16)
            sp.wait_ge(pre_out[0], 16 * REL_HEADS // 2)
            sp.wait_ge(pre_out[1], 16 * REL_HEADS // 2)
            sp.wait_ge(pre_x, 32)
            sp.sem_inc(pre_half, 1)
            with sp.Fori(0, DEPTH) as l:
                sp.dma_start(prow[ROW_MIX:ROW_MIX + 8, :],
                             layer_of(norm_mix_g, l).rearrange("a (r c) -> (a r) c", c=P)).then_inc(par, 16)
                sp.dma_start(prow[ROW_FFN:ROW_FFN + 8, :],
                             layer_of(norm_ffn_g, l).rearrange("a (r c) -> (a r) c", c=P)).then_inc(par, 16)
                sp.dma_start(prow[ROW_BGATE:ROW_BGATE + 24, :],
                             layer_of(b_gate, l).rearrange("a (r c) -> (a r) c", c=P)).then_inc(par, 16)
                for half in range(2):
                    sp.dma_start(prow[ROW_QK:ROW_QK + 6, half * HD:(half + 1) * HD],
                                 layer_of(qk_norm_g, l).rearrange("a n b d -> (a n b) d")).then_inc(par, 16)
                sp.dma_start(prow[ROW_SUBLN:ROW_SUBLN + 1, :], layer_of(diff_subln_g, l)).then_inc(par, 16)
                for unit in range(RAW_SLOTS):
                    w = P_CHUNKS[units[unit][1]][2]
                    sp.dma_start(raw[:, unit, :, 0:w], unit_source(units[unit], l)).then_inc(raw_in[unit], 16)
                sp.dma_start(lam_rows[:, :],
                             layer_of(diff_lambda, l).rearrange("a r d -> a (r d)").broadcast_to([P, 4 * HD])
                             ).then_inc(par, 16)
                sp.dma_start(sink_row[:, :], layer_of(sinks, l).broadcast_to([P, B_HEADS])).then_inc(par, 16)
                sp.dma_start(lconst[:, :], layer_of(layer_consts, l).broadcast_to([P, 2])).then_inc(par, 16)
                sp.dma_start(br[:, 0:4], layer_of(b_router_group, l).broadcast_to([P, 4])).then_inc(par, 16)
                sp.dma_start(br[:, 4:20], layer_of(b_router_expert, l).broadcast_to([P, 16])).then_inc(par, 16)
                sp.dma_start(wr[:, :, 0:4],
                             layer_of(w_router_group, l).rearrange("a (k p) n -> p (a k) n", p=P)).then_inc(par, 16)
                sp.dma_start(wr[:, :, 4:20],
                             layer_of(w_router_expert, l).rearrange("a (k p) n -> p (a k) n", p=P)).then_inc(par, 16)
                for n in range(RAW_SLOTS, len(units)):
                    w = P_CHUNKS[units[n][1]][2] if units[n][0] == "in" else 512
                    sp.wait_ge(split_done, n - RAW_SLOTS + 1)
                    sp.dma_start(raw[:, n % RAW_SLOTS, :, 0:w],
                                 unit_source(units[n], l)).then_inc(raw_in[n % RAW_SLOTS], 16)
                sp.wait_ge(split_done, len(units))
                with sp.Fori(0, N_EXPERTS) as e:
                    le = l * N_EXPERTS + e
                    for n, (kind, u) in enumerate(E_UNITS):
                        if n >= RAW_SLOTS:
                            sp.wait_ge(e_split, n - RAW_SLOTS + 1)
                        dst = raw[:, n % RAW_SLOTS]
                        if kind == "gu":
                            for half, w in enumerate((w_ff_gate, w_ff_up)):
                                src = w.rearrange("l e d f -> (l e) d f")[bass.ds(le, 1),
                                                                          u * UNIT_KT * P:(u + 1) * UNIT_KT * P, :]
                                sp.dma_start(dst[:, :, half * FF:(half + 1) * FF],
                                             src.rearrange("a (k p) n -> p (a k) n", p=P)
                                             ).then_inc(e_raw[n % RAW_SLOTS], 16)
                        else:
                            src = w_ff_down.rearrange("l e f d -> (l e) f d")[bass.ds(le, 1), :, u * 512:u * 512 + 512]
                            sp.dma_start(dst, src.rearrange("a (k p) n -> p (a k) n", p=P)
                                         ).then_inc(e_raw[n % RAW_SLOTS], 16)
                    meet_and_clear(sp, expert_end, expert_sems)
                sp.wait_ge(layer_end[0], 4)
                sp.dma_start(xs.rearrange("(t p) d -> p t d", p=P), X[:, :, :]).then_inc(layer_out, 16)
                sp.wait_ge(layer_out, 16)
                meet_and_clear(sp, layer_end, layer_sems)
            sp.dma_start(out.rearrange("b (t p) d -> p (b t) d", p=P), X[:, :, :]).then_inc(pre_x, 16)
            sp.wait_ge(pre_x, 48)

        @block.gpsimd
        def _(pool):
            nc.gpsimd.memset(half_neg[:, :], -0.5).then_inc(pre_half, 1)

            def pow_step(dst, src, n):
                return nc.gpsimd.tensor_tensor(dst, src, half_neg[:, 0:n], ALU.pow)

            def split(n):
                w = P_CHUNKS[units[n][1]][2] if units[n][0] == "in" else 512
                slot, two = n % RAW_SLOTS, n % 2
                pool.wait_ge(raw_in[slot], 16 * (n // RAW_SLOTS + 1))
                if n >= 2:
                    last_of_chunk, value = unit_end(n - 2)
                    pool.wait_ge(g_done if last_of_chunk else unit_used, value)
                nc.gpsimd.tensor_scalar(w_hi[:, two, :, 0:w], raw[:, slot, :, 0:w], 1.0, 0.0,
                                        ALU.mult, ALU.add).then_inc(split_hi, 1)
                pool.wait_ge(split_hi, n + 1)
                nc.gpsimd.tensor_tensor(w_lo[:, two, :, 0:w], raw[:, slot, :, 0:w],
                                        w_hi[:, two, :, 0:w].bitcast(F32), ALU.subtract).then_inc(split_done, 1)

            pool.wait_ge(pre_half, 2)
            normed = [i for i, (name, _, _) in enumerate(P_CHUNKS) if name != "Av"]
            with pool.Fori(0, DEPTH) as l:
                split(0)
                split(1)
                pool.wait_ge(ms_done, 1)
                pow_step(row_rs[:, 0, :], row_ms[:, 0, :], TT).then_inc(rs_done, 1)
                n_gate0 = unit_at[("gate", 0, 0, 0)]
                powed = 0
                for n in range(2, len(units)):
                    split(n)
                    if n < n_gate0 + 4 and n % UNITS_K == 1 and n // UNITS_K - 1 in normed:
                        c = n // UNITS_K - 1
                        w = 8 * TT if P_CHUNKS[c][0] in ("Aq", "Ak", "Bq", "Cq") else 2 * TT
                        if P_CHUNKS[c][0] == "I":
                            w = TT
                        pool.wait_ge(cms_done, normed.index(c) + 1)
                        pow_step(head_rs[:, c % 2, 0:w], head_ms[:, c % 2, 0:w], w).then_inc(crs_done, 1)
                    for b in range(4):
                        if n == n_gate0 + min(2 * b + 4, 9):
                            pool.wait_ge(oms_done, b + 1)
                            pow_step(o_rs[:, b % 2, :], o_ms[:, b % 2, :], TT).then_inc(ors_done, 1)
                pool.wait_ge(ms_done, 2)
                pow_step(row_rs[:, 1, :], row_ms[:, 1, :], TT).then_inc(rs_done, 1)
                with pool.Fori(0, N_EXPERTS) as e:
                    for n in range(len(E_UNITS)):
                        slot, two = n % RAW_SLOTS, n % 2
                        pool.wait_ge(e_raw[slot], expert_raw_value(n))
                        if n >= 2:
                            pool.wait_ge(e_used, n - 1)
                        nc.gpsimd.tensor_scalar(w_hi[:, two], raw[:, slot], 1.0, 0.0,
                                                ALU.mult, ALU.add).then_inc(e_hi, 1)
                        pool.wait_ge(e_hi, n + 1)
                        nc.gpsimd.tensor_tensor(w_lo[:, two], raw[:, slot], w_hi[:, two].bitcast(F32),
                                                ALU.subtract).then_inc(e_split, 1)
                    meet(pool, expert_end)
                meet(pool, layer_end)

        @block.tensor
        def _(pe):
            def three(out_ap, s_hi, s_lo, m_hi, m_lo, start, stop):
                nc.tensor.matmul(out_ap, s_hi, m_lo, start=start, stop=False)
                nc.tensor.matmul(out_ap, s_lo, m_hi, start=False, stop=False)
                return nc.tensor.matmul(out_ap, s_hi, m_hi, start=False, stop=stop)

            pe.wait_ge(pre_c, 64)
            for a in range(2):
                nc.tensor.matmul(G[a][0:REL_HEADS, 0:SPAN // 2], probs[0:N_BUCKETS, 1, 0:REL_HEADS],
                                 aqT[0:N_BUCKETS, a, 0:SPAN // 2], start=True, stop=True).then_inc(pre_mm, 1)
            for h in range(REL_HEADS):
                pe.wait_ge(pre_in[h % 2], 16 * (h // 2 + 1))
                if h >= 2:
                    pe.wait_ge(pre_cp, h - 1)
                nc.tensor.matmul(S[h % 2][:, :], probs[:, 0, 0:P], bqT[:, h % 2, :],
                                 start=True, stop=True).then_inc(pre_flip, 1)

            def norm_turns(which):
                for dt in range(KT):
                    pe.wait_ge(xn_done, TT * (which + 1))
                    if dt >= 4:
                        pe.wait_ge(nlo_done, KT * which + dt - 3)
                    for t in range(TT):
                        last = nc.tensor.transpose(G[dt % 4][:, t * P:(t + 1) * P],
                                                   xn[:, t, dt * P:(dt + 1) * P], ident[:, :])
                    last.then_inc(nt_done, 1)

            def rows_chunk(k, first_unit, width, lhs_hi, lhs_lo):
                for u in range(UNITS_K):
                    n = first_unit + u
                    pe.wait_ge(split_done, n + 1)
                    for t in range(TT):
                        if u == 0 and k > 0:
                            pe.wait_ge(g_free, 4 * (k - 1) + t + 1)
                        for kk in range(UNIT_KT):
                            kt = u * UNIT_KT + kk
                            last = three(G[t][:, 0:width], lhs_hi[:, kt, t * P:(t + 1) * P],
                                         lhs_lo[:, kt, t * P:(t + 1) * P], w_hi[:, n % 2, kk, 0:width],
                                         w_lo[:, n % 2, kk, 0:width], kt == 0, kt == KT - 1)
                        if u == UNITS_K - 1 and t < TT - 1:
                            last.then_inc(g_done, 1)
                    if u < UNITS_K - 1:
                        last.then_inc(unit_used, 1)
                last.then_inc(g_done, 1)

            fills = [0]

            def chunk_turns(c):
                name = P_CHUNKS[c][0]
                if T_BLOCKS[name]:
                    pe.wait_ge(chunk_normed, sum(1 for m in range(c + 1) if T_BLOCKS[P_CHUNKS[m][0]]))
                for b in range(T_BLOCKS[name]):
                    n = fills[0]
                    if n >= 2:
                        pe.wait_ge(t_free, n - 1)
                    for t in range(TT):
                        last = nc.tensor.transpose(T[n % 2][:, t * P:(t + 1) * P],
                                                   ptmp[:, t, b * P:(b + 1) * P], ident[:, :])
                    last.then_inc(t_done, 1)
                    fills[0] += 1

            def index_logits():
                pe.wait_ge(t_free, T_BLOCKS["I"])
                n = 0
                for i in range(1, TT):
                    for h in range(IDX_HEADS):
                        if n >= 2:
                            pe.wait_ge(relu_done, n - 1)
                        r = slice(IDX_DIM * h, IDX_DIM * (h + 1))
                        nc.tensor.matmul(S[n % 2][:, 0:P * (i + 1)], iqT[r, i * P:(i + 1) * P],
                                         ikT[r, 0:P * (i + 1)], start=True, stop=True).then_inc(idx_done, 1)
                        n += 1

            def dense_step(group):
                kind, n, c, u, t, kk, first, last_of_bank, last_of_unit = group
                unit = unit_at[(kind, n, c, u)]
                k = gate_chunk(n, c) if kind == "gate" else y_chunk(n, c)
                if t == 0 and kk == 0:
                    pe.wait_ge(split_done, unit + 1)
                    if kind == "y" and c == 0 and u == 0:
                        pe.wait_ge(ohi_done, 2 * 4 * (n + 1))
                if first:
                    pe.wait_ge(g_free, 4 * (k - 1) + t + 1)
                hi, lo = (hT_hi, hT_lo) if kind == "gate" else (oT_hi, oT_lo)
                kt = u * UNIT_KT + kk
                last = three(G[t][:, :], w_hi[:, unit % 2, kk, t * P:(t + 1) * P],
                             w_lo[:, unit % 2, kk, t * P:(t + 1) * P], hi[:, kt, :], lo[:, kt, :], first,
                             last_of_bank)
                if last_of_bank:
                    last.then_inc(g_done, 1)
                elif last_of_unit:
                    last.then_inc(unit_used, 1)

            def scores(br_, j):
                h, i, _, nk, tiles = br_.job(j)
                k0 = tiles[0] * P
                job = br_.first_job + j
                if br_.name == "A":
                    pe.wait_ge(soft_done, job) if job else None
                    for m in range(2):
                        r = slice(HD * m, HD * (m + 1))
                        last = nc.tensor.matmul(S[m][:, 0:nk], aqT[r, h, i * P:(i + 1) * P],
                                                akT[r, h, k0:k0 + nk], start=True, stop=True)
                else:
                    pe.wait_ge(soft_done, br_.first_job + max(j - 1, 0))
                    r = slice(HD * (h % 2), HD * (h % 2 + 1))
                    q, k = (bqT, bkT[:, h // (B_HEADS // B_KV), :]) if br_.name == "B" else (cqT, ckT[:, :])
                    last = nc.tensor.matmul(S[j % 2][:, 0:nk], q[r, h // 2, i * P:(i + 1) * P],
                                            k[r, k0:k0 + nk], start=True, stop=True)
                last.then_inc(s_done, 1)

            def prob_of(br_, j):
                return probs[:, 2 * (j % 2), :] if br_.name == "A" else probs[:, j % 4, :]

            def turn_probs(br_, j):
                _, _, _, nk, tiles = br_.job(j)
                pe.wait_ge(p_ready, br_.first_job + j + 1)
                pe.wait_ge(t_free, br_.t_index[j])
                for b in range(len(tiles)):
                    last = nc.tensor.transpose(T[0][:, b * P:(b + 1) * P],
                                               prob_of(br_, j)[:, b * P:(b + 1) * P], ident[:, :])
                last.then_inc(t_done, 1)

            def times_values(br_, j):
                h, _, _, _, tiles = br_.job(j)
                job = br_.first_job + j
                pe.wait_ge(t_free, br_.t_index[j] + 1)
                if job:
                    pe.wait_ge(o_free, job)
                for b, kt in enumerate(tiles):
                    if br_.name == "A":
                        v = av[:, kt, h * P:(h + 1) * P]
                    elif br_.name == "B":
                        g = h // (B_HEADS // B_KV)
                        v = bv[:, kt, g * HD:(g + 1) * HD]
                    else:
                        v = cv[:, kt, :]
                    w = v.shape[-1]
                    last = nc.tensor.matmul(O[:, (job % 4) * P:(job % 4) * P + w], pT[:, j % 2, b * P:(b + 1) * P], v,
                                            start=(b == 0), stop=(b == len(tiles) - 1))
                last.then_inc(pv_done, 1)

            def turn_rows(br_, b):
                if br_.name == "A":
                    pe.wait_ge(o_scaled, b + 1)
                else:
                    pe.wait_ge(o_free, br_.first_job + br_.per_block * (b + 1))
                pe.wait_ge(t_free, br_.o_index[b])
                for t in range(TT):
                    last = nc.tensor.transpose(T[0][:, t * P:(t + 1) * P], o_rows[:, b % 2, t, :], ident[:, :])
                last.then_inc(t_done, 1)

            def attention(br_):
                groups = dense_groups(br_.dense)
                for s in range(br_.slots):
                    if s < br_.jobs:
                        scores(br_, s)
                    if 0 <= s - br_.lag < br_.jobs:
                        turn_probs(br_, s - br_.lag)
                    if 0 <= s - br_.lag - 1 < br_.jobs:
                        times_values(br_, s - br_.lag - 1)
                    if br_.block_turned(s) is not None:
                        turn_rows(br_, br_.block_turned(s))
                    for g in br_.groups_of(s):
                        dense_step(groups[g])

            pe.wait_ge(pre_half, 2)
            with pe.Fori(0, DEPTH) as l:
                fills[0] = 0
                pe.wait_ge(par, 16 * 13)
                nc.tensor.transpose(G[0][:, 0:N_ROWS], prow[:, :], ident[0:N_ROWS, 0:N_ROWS]).then_inc(par_turned, 1)
                pe.wait_ge(pcol_ready, 1)
                norm_turns(0)
                pe.wait_ge(nlo_done, KT)
                for c in range(len(P_CHUNKS)):
                    rows_chunk(c, c * UNITS_K, P_CHUNKS[c][2], hT_hi, hT_lo)
                    if c >= 1:
                        chunk_turns(c - 1)
                    if c == 1:
                        index_logits()
                chunk_turns(len(P_CHUNKS) - 1)
                pe.wait_ge(t_free, P_FILLS)
                for br_ in branches:
                    attention(br_)
                for group in dense_groups([("y", 2)]):
                    dense_step(group)
                pe.wait_ge(g_free, 4 * OUT_CHUNK)
                for c in range(2):
                    rows_chunk(OUT_CHUNK + c, unit_at[("out", c, 0)], 512, hT_hi, hT_lo)
                pe.wait_ge(g_free, 4 * N_CHUNKS)
                norm_turns(1)
                pe.wait_ge(nlo_done, 2 * KT)
                pe.wait_ge(wr_split, 1)
                for t in range(TT):
                    for kt in range(KT):
                        last = three(S[0][:, t * 20:(t + 1) * 20], hT_hi[:, kt, t * P:(t + 1) * P],
                                     hT_lo[:, kt, t * P:(t + 1) * P], wr_hi[:, kt, :], wr_lo[:, kt, :],
                                     kt == 0, kt == KT - 1)
                last.then_inc(log_done, 1)
                with pe.Fori(0, N_EXPERTS) as e:
                    for n in range(UNITS_K):
                        pe.wait_ge(e_split, n + 1)
                        for t in range(4):
                            for kk in range(UNIT_KT):
                                kt = n * UNIT_KT + kk
                                last = three(G[t][:, :], w_hi[:, n % 2, kk, t * P:(t + 1) * P],
                                             w_lo[:, n % 2, kk, t * P:(t + 1) * P], hT_hi[:, kt, :], hT_lo[:, kt, :],
                                             kt == 0, kt == KT - 1)
                        last.then_inc(e_used, 1)
                    pe.wait_ge(e_used, UNITS_K)
                    pe.sem_inc(e_gu, 1)
                    pe.wait_ge(e_hid, 2)
                    for c in range(2):
                        n = UNITS_K + c
                        pe.wait_ge(e_split, n + 1)
                        for t in range(TT):
                            if c == 1:
                                pe.wait_ge(e_free, t + 1)
                            for kk in range(FF // P):
                                last = three(banks[4 + t][:, :], oT_hi[:, kk, t * P:(t + 1) * P],
                                             oT_lo[:, kk, t * P:(t + 1) * P], w_hi[:, n % 2, kk, :],
                                             w_lo[:, n % 2, kk, :], kk == 0, kk == FF // P - 1)
                            last.then_inc(e_down, 1)
                        if c == 0:
                            pe.wait_ge(e_down, TT)
                            pe.sem_inc(e_used, 1)
                    meet(pe, expert_end)
                meet(pe, layer_end)

        @block.scalar
        def _(act):
            def norm_rows(which):
                for t in range(TT):
                    if which + t:
                        act.wait_ge(ss_done, TT * which + t)
                    nc.scalar.activation(ptmp[:, 0:2, :].rearrange("p a n -> p (a n)"), X[:, t, :], ACT.Square,
                                         accum_out=row_ss[:, which, t:t + 1]).then_inc(ss_done, 1)

            def norm_hi(which, row):
                for dt in range(KT):
                    act.wait_ge(nt_done, KT * which + dt + 1)
                    nc.scalar.activation(hT_hi[:, dt, :], G[dt % 4][:, :], ACT.Copy,
                                         scale=pcol[:, row + dt:row + dt + 1]).then_inc(nhi_done, 1)

            n_sq = [0]
            n_copy = [0]
            fills = [0]

            def chunk_out(c):
                name = P_CHUNKS[c][0]
                fills_before = sum(T_BLOCKS[P_CHUNKS[m][0]] for m in range(c))
                for t in range(TT):
                    act.wait_ge(g_done, 4 * c + t + 1)
                    if t == 0 and fills_before and T_BLOCKS[name]:
                        act.wait_ge(t_done, fills_before)
                    ps = G[t]
                    if name == "Av":
                        nc.scalar.activation(av[:, t, :], ps[:, :], ACT.Copy).then_inc(g_free, 1)
                        continue
                    if name == "I":
                        nc.scalar.activation(ptmp[:, t, 384:448], ps[:, 0:64], ACT.Copy)
                        nc.scalar.activation(cv[:, t, :], ps[:, 64:128], ACT.Copy)
                        nc.scalar.activation(ptmp[:, t, 128:256], ps[:, 128:256], ACT.Copy)
                        nc.scalar.activation(ptmp[:, t, 256:384].rearrange("p (r d) -> p r d", r=4),
                                             ps[:, 256:288].unsqueeze(1).broadcast_to([P, 4, IDX_DIM]), ACT.Copy)
                        nc.scalar.activation(iw[:, t, :], ps[:, 288:292], ACT.Copy).then_inc(chunk_copied, 1)
                        w = 64
                    elif name == "Bkv":
                        nc.scalar.activation(bv[:, t, :], ps[:, 128:256], ACT.Copy)
                        nc.scalar.activation(ptmp[:, t, 256:384], ps[:, 0:128], ACT.Copy).then_inc(chunk_copied, 1)
                        w = 128
                    else:
                        nc.scalar.activation(ptmp[:, t, :], ps[:, :], ACT.Copy).then_inc(chunk_copied, 1)
                        w = 512
                    n_copy[0] += 1
                    if n_sq[0] >= 2:
                        act.wait_ge(reduced, n_sq[0] - 1)
                    nc.scalar.activation(sq[:, n_sq[0] % 2, 0:w], ps[:, 0:w], ACT.Square).then_inc(squared, 1)
                    n_sq[0] += 1
                    act.wait_ge(squared, n_sq[0])
                    act.wait_ge(chunk_copied, n_copy[0])
                    act.sem_inc(g_free, 1)

            def turned_out(c):
                name = P_CHUNKS[c][0]
                for b in range(T_BLOCKS[name]):
                    n = fills[0]
                    act.wait_ge(t_done, n + 1)
                    src = T[n % 2][:, :]
                    k_gain = {"A": 1, "B": 3, "C": 5}
                    if name == "I":
                        dst, gain = [(ckT[:, :], pcol[:, ROW_QK + 5:ROW_QK + 6]), (iqT[:, :], 1.0), (ikT[:, :], 1.0)][b]
                    elif name == "Bkv":
                        dst, gain = bkT[:, b, :], pcol[:, ROW_QK + 3:ROW_QK + 4]
                    elif name == "Ak":
                        dst, gain = akT[:, b, :], pcol[:, ROW_QK + 1:ROW_QK + 2]
                    else:
                        q = "ABC".index(name[0])
                        dst, gain = (aqT, bqT, cqT)[q][:, b, :], q_gain[:, q:q + 1]
                    nc.scalar.activation(dst, src, ACT.Copy, scale=gain).then_inc(t_free, 1)
                    fills[0] += 1

            def index_relu():
                n = 0
                for i in range(1, TT):
                    for h in range(IDX_HEADS):
                        act.wait_ge(idx_done, n + 1)
                        if n >= 4:
                            act.wait_ge(relu_used, n - 3)
                        nc.scalar.activation(probs[:, n % 4, 0:P * (i + 1)], S[n % 2][:, 0:P * (i + 1)],
                                             ACT.Relu).then_inc(relu_done, 1)
                        n += 1

            def load_bias(gh):
                act.dma_start(bias[:, gh % 2, :], bias_dram[gh]).then_inc(bias_in[gh % 2], 16)

            def exps(br_, j):
                h, i, _, nk, _ = br_.job(j)
                job = br_.first_job + j
                gh = br_.first_head + h
                act.wait_ge(soft_done, job + 1)
                if i == 0 and 1 <= gh < REL_HEADS - 1:
                    load_bias(gh + 1)
                st = j % 4
                for m in range(2 if br_.name == "A" else 1):
                    p = probs[:, 2 * (j % 2) + m, 0:nk] if br_.name == "A" else probs[:, j % 4, 0:nk]
                    last = nc.scalar.activation(p, p, ACT.Exp, bias=job_neg[:, st, m:m + 1],
                                                accum_out=job_sum[:, st, m:m + 1])
                if br_.name == "B":
                    last = nc.scalar.activation(job_sink[:, st:st + 1], sink_row[:, h:h + 1], ACT.Exp,
                                                bias=job_neg[:, st, 0:1])
                last.then_inc(exp_done, 1)

            def attention(br_):
                groups = dense_groups(br_.dense)
                for s in range(br_.slots):
                    if s < br_.jobs:
                        exps(br_, s)
                    if 0 <= s - br_.lag < br_.jobs:
                        j = s - br_.lag
                        _, _, _, nk, _ = br_.job(j)
                        act.wait_ge(t_done, br_.t_index[j] + 1)
                        if br_.first_job + j >= 2:
                            act.wait_ge(pv_done, br_.first_job + j - 1)
                        nc.scalar.activation(pT[:, j % 2, 0:nk], T[0][:, 0:nk], ACT.Copy).then_inc(t_free, 1)
                    b = br_.block_turned(s)
                    if b is not None:
                        act.wait_ge(t_done, br_.o_index[b] + 1)
                        if b == 0 and br_.n > 0:
                            act.wait_ge(g_done, 4 * (y_chunk(br_.n - 1, 1) + 1))
                        gain = sub_gain[:, 0:1] if br_.name == "A" else 1.0
                        nc.scalar.activation(oT_hi[:, b, :], T[0][:, :], ACT.Copy, scale=gain).then_inc(ohi_done, 1)
                    for g in br_.groups_of(s):
                        kind, n, c, _, t, _, _, last_of_bank, _ = groups[g]
                        if kind == "gate" and last_of_bank:
                            act.wait_ge(g_done, 4 * gate_chunk(n, c) + t + 1)
                            row = ROW_BGATE + n * KT + c * 4 + t
                            nc.scalar.activation(gT[:, c * 4 + t, :], G[t][:, :], ACT.Sigmoid,
                                                 bias=pcol[:, row:row + 1]).then_inc(g_free, 1)

            for a in range(2):
                act.wait_ge(pre_mm, a + 1)
                nc.scalar.activation(akT[0:REL_HEADS, a, 0:SPAN // 2], G[a][0:REL_HEADS, 0:SPAN // 2],
                                     ACT.Copy).then_inc(pre_row, 1)
            for h in range(REL_HEADS):
                act.wait_ge(pre_flip, h + 1)
                if h >= 2:
                    act.wait_ge(pre_out[h % 2], 16 * (h // 2))
                nc.scalar.activation(cqT[:, h % 2, :], S[h % 2][:, :], ACT.Copy).then_inc(pre_cp, 1)
            act.wait_ge(pre_half, 2)
            with act.Fori(0, DEPTH) as l:
                n_sq[0] = n_copy[0] = fills[0] = 0
                load_bias(0)
                load_bias(1)
                norm_rows(0)
                act.wait_ge(lam_summed, 1)
                nc.scalar.activation(lam_exp[:, :], lam_sum[:, :], ACT.Exp).then_inc(lam_exped, 1)
                act.wait_ge(gains_ready, 1)
                norm_hi(0, ROW_MIX)
                for c in range(len(P_CHUNKS)):
                    if c >= 1:
                        turned_out(c - 1)
                    chunk_out(c)
                    if c == 1:
                        index_relu()
                turned_out(len(P_CHUNKS) - 1)
                for br_ in branches:
                    attention(br_)
                act.wait_ge(g_free, 4 * OUT_CHUNK)
                act.dma_start(X[:, :, :], xs.rearrange("(t p) d -> p t d", p=P)).then_inc(x_back, 16)
                act.wait_ge(g_free, 4 * N_CHUNKS)
                norm_rows(1)
                norm_hi(1, ROW_FFN)
                act.wait_ge(rexp_in, 1)
                nc.scalar.activation(rt[:, 0:2, :], rt[:, 0:2, :], ACT.Exp).then_inc(rexp_out, 1)
                with act.Fori(0, N_EXPERTS) as e:
                    act.wait_ge(e_gu, 1)
                    for f in range(2):
                        nc.scalar.activation(ptmp[:, f, :], G[f][:, :], ACT.Silu).then_inc(e_silu, 1)
                    meet(act, expert_end)
                meet(act, layer_end)

        @block.vector
        def _(v):
            links = [0]

            def link(ins):
                links[0] += 1
                ins.then_inc(dve, 1)
                v.wait_ge(dve, links[0])

            def norm_scale(which):
                v.wait_ge(ss_done, TT * (which + 1))
                nc.vector.tensor_scalar(row_ms[:, which, :], row_ss[:, which, :], 1.0 / D_MODEL, EPS, ALU.mult,
                                        ALU.add).then_inc(ms_done, 1)
                v.wait_ge(rs_done, which + 1)
                for t in range(TT):
                    nc.vector.tensor_scalar(xn[:, t, :], X[:, t, :], row_rs[:, which, t:t + 1], None,
                                            ALU.mult).then_inc(xn_done, 1)

            def norm_lo(which, row):
                for dt in range(KT):
                    v.wait_ge(nhi_done, KT * which + dt + 1)
                    nc.vector.scalar_tensor_tensor(hT_lo[:, dt, :], G[dt % 4][:, :], pcol[:, row + dt:row + dt + 1],
                                                   hT_hi[:, dt, :].bitcast(F32), ALU.mult,
                                                   ALU.subtract).then_inc(nlo_done, 1)

            n_red = [0]
            n_cms = [0]

            def chunk_stats(c):
                name = P_CHUNKS[c][0]
                heads = {"I": 1, "Bkv": 2}.get(name, 8)
                ss = head_ss[:, c % 2, 0:heads * TT].rearrange("p (t g) -> p t g", t=TT)
                for t in range(TT):
                    v.wait_ge(squared, n_red[0] + 1)
                    nc.vector.tensor_reduce(ss[:, t, :],
                                            sq[:, n_red[0] % 2, 0:heads * HD].rearrange("p (g d) -> p g d", d=HD),
                                            AX.X, ALU.add).then_inc(reduced, 1)
                    n_red[0] += 1
                v.wait_ge(reduced, n_red[0])
                nc.vector.tensor_scalar(head_ms[:, c % 2, 0:heads * TT], head_ss[:, c % 2, 0:heads * TT],
                                        1.0 / HD, EPS, ALU.mult, ALU.add).then_inc(cms_done, 1)
                n_cms[0] += 1

            def chunk_scale(c):
                name = P_CHUNKS[c][0]
                heads = {"I": 1, "Bkv": 2}.get(name, 8)
                v.wait_ge(crs_done, n_cms[0])
                v.wait_ge(chunk_copied, TT * n_cms[0])
                rs = head_rs[:, c % 2, 0:heads * TT]
                if heads == 8:
                    rows = ptmp[:, :, :].rearrange("p t (g d) -> p (t g) d", d=HD)
                    nc.vector.tensor_tensor(rows, rows, rs.unsqueeze(2).broadcast_to([P, 8 * TT, HD]),
                                            ALU.mult).then_inc(chunk_normed, 1)
                    return
                scale = rs.rearrange("p (t g) -> p t g", t=TT).unsqueeze(3).broadcast_to([P, TT, heads, HD])
                first = 384 if name == "I" else 256
                rows = ptmp[:, :, first:first + heads * HD].rearrange("p t (g d) -> p t g d", d=HD)
                for twin in range(2):
                    dst = ptmp[:, :, 0:heads * P].rearrange("p t (g r d) -> p t g r d", r=2, d=HD)[:, :, :, twin, :]
                    last = nc.vector.tensor_tensor(dst, rows, scale, ALU.mult)
                last.then_inc(chunk_normed, 1)

            block_at = {1: 0, 2: 2 * P, 3: 5 * P}

            def index_scores():
                w_scale = IDX_HEADS ** -0.5 * IDX_DIM ** -0.5
                link(nc.vector.tensor_scalar(iw[:, :, :], iw[:, :, :], w_scale, None, ALU.mult))
                n = 0
                for i in range(1, TT):
                    nk = P * (i + 1)
                    dst = score[:, block_at[i]:block_at[i] + nk]
                    for h in range(IDX_HEADS):
                        v.wait_ge(relu_done, n + 1)
                        w = iw[:, i, h:h + 1]
                        if h == 0:
                            nc.vector.tensor_scalar(dst, probs[:, n % 4, 0:nk], w, 0.0, ALU.mult,
                                                    ALU.add).then_inc(relu_used, 1)
                        else:
                            nc.vector.scalar_tensor_tensor(dst, probs[:, n % 4, 0:nk], w, dst, ALU.mult,
                                                           ALU.add).then_inc(relu_used, 1)
                        n += 1
                        v.wait_ge(relu_used, n)
                    link(nc.vector.memset(score[0:CHUNK, block_at[i] + nk - CHUNK:block_at[i] + nk], NEG))

            def top_round(i, r):
                nk = P * (i + 1)
                s = score[:, block_at[i]:block_at[i] + nk]
                link(nc.vector.max(top8[:, :], s))
                link(nc.vector.match_replace(s, top8[:, :], s, LOWEST))
                if r == TOP_K // 8 - 1:
                    link(nc.vector.tensor_scalar(s, s, TAKEN_BELOW, NEG, ALU.is_ge, ALU.mult))

            rounds = [(i, r) for i in range(1, TT) for r in range(TOP_K // 8)]

            def soft(br_, j):
                h, i, c0, nk, _ = br_.job(j)
                job, gh, st = br_.first_job + j, br_.first_head + h, j % 4
                tile_bias = bias[:, gh % 2, c0:c0 + nk]
                if i == 0:
                    v.wait_ge(bias_in[gh % 2], 16 * (gh // 2 + 1))
                if br_.name == "C" and i > 0:
                    link(nc.vector.tensor_tensor(bias_sel[:, 0:nk], tile_bias, score[:, block_at[i]:block_at[i] + nk],
                                                 ALU.add))
                    tile_bias = bias_sel[:, 0:nk]
                v.wait_ge(s_done, job + 1)
                if br_.name == "A":
                    if j >= 2:
                        v.wait_ge(t_done, br_.t_index[j - 2] + 1)
                    for m in range(2):
                        last = nc.vector.tensor_tensor_reduce(probs[:, 2 * (j % 2) + m, 0:nk], S[m][:, 0:nk],
                                                              tile_bias, 1.0, LOWEST, ALU.add, ALU.max,
                                                              job_max[:, st, m:m + 1])
                    link(last)
                    nc.vector.tensor_scalar(job_neg[:, st, :], job_max[:, st, :], -1.0, None,
                                            ALU.mult).then_inc(soft_done, 1)
                    return
                if j >= 4:
                    v.wait_ge(t_done, br_.t_index[j - 4] + 1)
                least = sink_row[:, h:h + 1] if br_.name == "B" else LOWEST
                link(nc.vector.tensor_tensor_reduce(probs[:, j % 4, 0:nk], S[j % 2][:, 0:nk], tile_bias, 1.0, least,
                                                    ALU.add, ALU.max, job_max[:, st, 0:1]))
                nc.vector.tensor_scalar(job_neg[:, st, 0:1], job_max[:, st, 0:1], -1.0, None,
                                        ALU.mult).then_inc(soft_done, 1)

            def post(br_, j):
                _, _, _, nk, _ = br_.job(j)
                job, st = br_.first_job + j, j % 4
                v.wait_ge(exp_done, job + 1)
                if br_.name == "A":
                    link(nc.vector.reciprocal(job_inv[:, st, :], job_sum[:, st, :]))
                    link(nc.vector.tensor_scalar(job_mix[:, st:st + 1], job_sum[:, st, 0:1], job_inv[:, st, 1:2],
                                                 neg_lam[:, 0:1], ALU.mult, ALU.mult))
                    nc.vector.scalar_tensor_tensor(probs[:, 2 * (j % 2), 0:nk], probs[:, 2 * (j % 2) + 1, 0:nk],
                                                   job_mix[:, st:st + 1], probs[:, 2 * (j % 2), 0:nk], ALU.mult,
                                                   ALU.add).then_inc(p_ready, 1)
                elif br_.name == "B":
                    link(nc.vector.tensor_tensor(job_den[:, st:st + 1], job_sum[:, st, 0:1], job_sink[:, st:st + 1],
                                                 ALU.add))
                    nc.vector.reciprocal(job_inv[:, st, 0:1], job_den[:, st:st + 1]).then_inc(p_ready, 1)
                else:
                    nc.vector.reciprocal(job_inv[:, st, 0:1], job_sum[:, st, 0:1]).then_inc(p_ready, 1)

            def rows_out(br_, j):
                h, i, _, _, _ = br_.job(j)
                job, st = br_.first_job + j, j % 4
                b = j // br_.per_block
                v.wait_ge(pv_done, job + 1)
                v.wait_ge(p_ready, job + 1)
                if j % br_.per_block == 0 and b >= 2:
                    v.wait_ge(t_done, br_.o_index[b - 2] + 1)
                w = P if br_.name == "A" else HD
                c0 = 0 if br_.name == "A" else HD * (h % 2)
                nc.vector.tensor_scalar(o_rows[:, b % 2, i, c0:c0 + w], O[:, (job % 4) * P:(job % 4) * P + w],
                                        job_inv[:, st, 0:1], None, ALU.mult).then_inc(o_free, 1)
                if br_.name == "A" and i == TT - 1:
                    v.wait_ge(o_free, job + 1)
                    for t in range(TT):
                        last = nc.vector.tensor_tensor_reduce(sq[:, 0, t * P:(t + 1) * P], o_rows[:, b % 2, t, :],
                                                              o_rows[:, b % 2, t, :], 1.0, 0.0, ALU.mult, ALU.add,
                                                              o_ss[:, b % 2, t:t + 1])
                    link(last)
                    nc.vector.tensor_scalar(o_ms[:, b % 2, :], o_ss[:, b % 2, :], 1.0 / P, EPS, ALU.mult,
                                            ALU.add).then_inc(oms_done, 1)

            def scale_rows(b):
                v.wait_ge(ors_done, b + 1)
                nc.vector.tensor_tensor(o_rows[:, b % 2], o_rows[:, b % 2],
                                        o_rs[:, b % 2, :].unsqueeze(2).broadcast_to([P, TT, P]),
                                        ALU.mult).then_inc(o_scaled, 1)

            def turned_lo(br_, b):
                n = 4 * br_.n + b
                v.wait_ge(ohi_done, 2 * n + 1)
                if br_.name == "A":
                    nc.vector.scalar_tensor_tensor(oT_lo[:, b, :], T[0][:, :], sub_gain[:, 0:1],
                                                   oT_hi[:, b, :].bitcast(F32), ALU.mult,
                                                   ALU.subtract).then_inc(ohi_done, 1)
                else:
                    nc.vector.tensor_tensor(oT_lo[:, b, :], T[0][:, :], oT_hi[:, b, :].bitcast(F32),
                                            ALU.subtract).then_inc(ohi_done, 1)
                v.wait_ge(ohi_done, 2 * n + 2)
                v.sem_inc(t_free, 1)

            def branch_out(n, c, t):
                dt = 4 * c + t
                k = y_chunk(n, c)
                v.wait_ge(g_done, 4 * k + t + 1)
                v.wait_ge(g_free, 4 * gate_chunk(n, c) + t + 1)
                if n == 0:
                    nc.vector.tensor_tensor(mixed[:, dt, :], G[t][:, :], gT[:, dt, :], ALU.mult).then_inc(g_free, 1)
                    return
                link(nc.vector.tensor_tensor(ytmp[:, :], G[t][:, :], gT[:, dt, :], ALU.mult))
                if n == 1:
                    nc.vector.tensor_tensor(mixed[:, dt, :], mixed[:, dt, :], ytmp[:, :], ALU.add).then_inc(g_free, 1)
                    v.wait_ge(g_free, 4 * k + t + 1)
                    return
                link(nc.vector.tensor_tensor(mixed[:, dt, :], mixed[:, dt, :], ytmp[:, :], ALU.add))
                link(nc.vector.tensor_copy(hT_hi[:, dt, :], mixed[:, dt, :]))
                nc.vector.tensor_tensor(hT_lo[:, dt, :], mixed[:, dt, :], hT_hi[:, dt, :].bitcast(F32),
                                        ALU.subtract).then_inc(g_free, 1)

            def attention(br_):
                groups = dense_groups(br_.dense)
                for s in range(br_.slots):
                    if s < br_.jobs:
                        soft(br_, s)
                    if 0 <= s - br_.lag - 1 < br_.jobs:
                        rows_out(br_, s - br_.lag - 1)
                    if br_.name == "A" and br_.block_scaled(s) is not None:
                        scale_rows(br_.block_scaled(s))
                    if br_.block_turned(s) is not None:
                        turned_lo(br_, br_.block_turned(s))
                    j = s - br_.lag + 1
                    if 0 <= j < br_.jobs:
                        post(br_, j)
                    for g in br_.groups_of(s):
                        kind, n, c, _, t, _, _, last_of_bank, _ = groups[g]
                        if kind == "y" and last_of_bank:
                            branch_out(n, c, t)

            def first_only(flags, n):
                taken = rt[:, 14, :].rearrange("p (t g) -> p t g", g=4)
                link(nc.vector.memset(taken, 0.0))
                link(nc.vector.tensor_copy(taken[:, :, 1:2], flags[:, :, 0:1]))
                link(nc.vector.tensor_tensor(taken[:, :, 2:3], flags[:, :, 0:1], flags[:, :, 1:2], ALU.max))
                link(nc.vector.tensor_tensor(taken[:, :, 3:4], taken[:, :, 2:3], flags[:, :, 2:3], ALU.max))
                link(nc.vector.tensor_tensor(flags, flags, taken, ALU.is_gt))

            def route():
                v.wait_ge(log_done, 1)
                link(nc.vector.tensor_tensor(logit[:, :, :], S[0][:, 0:TT * 20].rearrange("p (t n) -> p t n", t=TT),
                                             br[:, :].unsqueeze(1).broadcast_to([P, TT, 20]), ALU.add))
                four = lambda n: rt[:, n, :].rearrange("p (t g) -> p t g", g=4)
                one = lambda n: rt[:, n, 0:TT]
                wide = lambda n: one(n).unsqueeze(2).broadcast_to([P, TT, 4])
                gl = logit[:, :, 0:4]
                link(nc.vector.tensor_reduce(one(2), gl, AX.X, ALU.max))
                link(nc.vector.tensor_tensor(four(0), gl, wide(2), ALU.subtract))
                link(nc.vector.tensor_tensor(four(3), gl, wide(2), ALU.is_equal))
                first_only(four(3), 4)
                el = logit[:, :, 4:20].rearrange("p t (g e) -> p t e g", g=4)
                link(nc.vector.tensor_tensor(ein[:, :, :, :], el, four(3).unsqueeze(2).broadcast_to([P, TT, 4, 4]),
                                             ALU.mult))
                link(nc.vector.tensor_reduce(four(4), ein[:, :, :, :], AX.X, ALU.add))
                link(nc.vector.tensor_reduce(one(5), four(4), AX.X, ALU.max))
                link(nc.vector.tensor_tensor(four(6), four(4), wide(5), ALU.is_equal))
                first_only(four(6), 4)
                link(nc.vector.scalar_tensor_tensor(four(7), four(6), LOWEST, four(4), ALU.mult, ALU.add))
                link(nc.vector.tensor_reduce(one(8), four(7), AX.X, ALU.max))
                link(nc.vector.tensor_tensor(four(9), four(7), wide(8), ALU.is_equal))
                first_only(four(9), 4)
                link(nc.vector.memset(rt[:, 1, :], 0.0))
                nc.vector.tensor_tensor(rt[:, 1, 0:TT], one(8), one(5), ALU.subtract).then_inc(rexp_in, 1)
                v.wait_ge(rexp_out, 1)
                link(nc.vector.tensor_reduce(one(10), four(0), AX.X, ALU.add))
                link(nc.vector.tensor_scalar(one(11), rt[:, 1, 0:TT], 1.0, None, ALU.add))
                link(nc.vector.tensor_tensor(one(12), one(10), one(11), ALU.mult))
                link(nc.vector.reciprocal(one(12), one(12)))
                link(nc.vector.tensor_tensor(one(13), one(12), rt[:, 1, 0:TT], ALU.mult))
                link(nc.vector.tensor_tensor(four(6), four(6), wide(12), ALU.mult))
                link(nc.vector.tensor_tensor(four(9), four(9), wide(13), ALU.mult))
                link(nc.vector.tensor_tensor(four(6), four(6), four(9), ALU.add))
                for g in range(N_GROUPS):
                    dst = gate16[:, g * 4:(g + 1) * 4, :].rearrange("p e t -> p t e")
                    link(nc.vector.tensor_tensor(dst, four(6), four(3)[:, :, g:g + 1].broadcast_to([P, TT, 4]),
                                                 ALU.mult))

            for h in range(REL_HEADS):
                v.wait_ge(pre_cp, h + 1)
                last = nc.vector.memset(cqT[0:CHUNK, h % 2, SEQ - CHUNK:SEQ], NEG)
                if A_HEADS <= h < A_HEADS + B_HEADS:
                    last = nc.vector.memset(cqT[CHUNK:P, h % 2, SEQ - 2 * P:SEQ - 2 * P + CHUNK], NEG)
                last.then_inc(pre_set, 1)
            v.wait_ge(pre_half, 2)
            with v.Fori(0, DEPTH) as l:
                links[0] = n_red[0] = n_cms[0] = 0
                v.wait_ge(par_turned, 1)
                nc.vector.tensor_copy(pcol[:, :], G[0][:, 0:N_ROWS]).then_inc(pcol_ready, 1)
                norm_scale(0)
                v.wait_ge(par, 16 * 13)
                v.wait_ge(pcol_ready, 1)
                link(nc.vector.tensor_copy(wr_hi[:, :, :], wr[:, :, :]))
                nc.vector.tensor_tensor(wr_lo[:, :, :], wr[:, :, :], wr_hi[:, :, :].bitcast(F32),
                                        ALU.subtract).then_inc(wr_split, 1)
                for m in range(2):
                    last = nc.vector.tensor_tensor_reduce(sq[:, m, 0:HD], lam_rows[:, 2 * m * HD:(2 * m + 1) * HD],
                                                          lam_rows[:, (2 * m + 1) * HD:(2 * m + 2) * HD], 1.0, 0.0,
                                                          ALU.mult, ALU.add, lam_sum[:, m:m + 1])
                last.then_inc(lam_summed, 1)
                link(nc.vector.tensor_scalar(q_gain[:, :], pcol[:, ROW_QK:ROW_QK + 6:2], HD ** -0.5, None, ALU.mult))
                link(nc.vector.tensor_tensor(sub_gain[:, :], pcol[:, ROW_SUBLN:ROW_SUBLN + 1], lconst[:, 1:2],
                                             ALU.mult))
                v.wait_ge(lam_exped, 1)
                link(nc.vector.tensor_tensor(lam_dif[:, :], lam_exp[:, 1:2], lam_exp[:, 0:1], ALU.subtract))
                nc.vector.tensor_tensor(neg_lam[:, :], lam_dif[:, :], lconst[:, 0:1],
                                        ALU.subtract).then_inc(gains_ready, 1)
                v.wait_ge(gains_ready, 1)
                norm_lo(0, ROW_MIX)
                at = 0
                for c in range(len(P_CHUNKS)):
                    if P_CHUNKS[c][0] != "Av":
                        chunk_stats(c)
                    if c == 1:
                        index_scores()
                    if P_CHUNKS[c][0] != "Av":
                        chunk_scale(c)
                    if c >= 2:
                        n = -(-(len(rounds) - at) // (len(P_CHUNKS) - c))
                        for i, r in rounds[at:at + n]:
                            top_round(i, r)
                        at += n
                for br_ in branches:
                    attention(br_)
                for group in dense_groups([("y", 2)]):
                    if group[7]:
                        branch_out(2, group[2], group[4])
                v.wait_ge(x_back, 16)
                for c in range(2):
                    for t in range(TT):
                        v.wait_ge(g_done, 4 * (OUT_CHUNK + c) + t + 1)
                        rows = X[:, t, c * 512:(c + 1) * 512]
                        nc.vector.tensor_tensor(rows, G[t][:, :], rows, ALU.add).then_inc(g_free, 1)
                v.wait_ge(g_free, 4 * N_CHUNKS)
                norm_scale(1)
                norm_lo(1, ROW_FFN)
                route()
                with v.Fori(0, N_EXPERTS) as e:
                    nc.vector.tensor_copy(gate_cur[:, :], gate16[:, bass.ds(e, 1), :].rearrange("p a t -> p (a t)")
                                          ).then_inc(e_dve, 1)
                    for f in range(2):
                        v.wait_ge(e_silu, f + 1)
                        nc.vector.tensor_tensor(ptmp[:, 2 + f, :], ptmp[:, f, :], G[2 + f][:, :],
                                                ALU.mult).then_inc(e_dve, 1)
                        v.wait_ge(e_dve, 2 + 2 * f)
                        nc.vector.tensor_copy(oT_hi[:, f, :], ptmp[:, 2 + f, :]).then_inc(e_dve, 1)
                        v.wait_ge(e_dve, 3 + 2 * f)
                        nc.vector.tensor_tensor(oT_lo[:, f, :], ptmp[:, 2 + f, :], oT_hi[:, f, :].bitcast(F32),
                                                ALU.subtract).then_inc(e_hid, 1)
                    for c in range(2):
                        for t in range(TT):
                            v.wait_ge(e_down, TT * c + t + 1)
                            rows = X[:, t, c * 512:(c + 1) * 512]
                            nc.vector.scalar_tensor_tensor(rows, banks[4 + t][:, :], gate_cur[:, t:t + 1], rows,
                                                           ALU.mult, ALU.add).then_inc(e_free, 1)
                    meet(v, expert_end)
                meet(v, layer_end)


def distance_buckets():
    rel = np.arange(SPAN) - (SEQ - 1)
    half = N_BUCKETS // 2
    exact = half // 2
    n = np.abs(rel)
    n_f = np.maximum(n, 1).astype(np.float32)
    large = exact + (np.log(n_f / np.float32(exact)) / np.float32(math.log(MAX_DIST / exact))
                     * np.float32(half - exact)).astype(np.int32)
    large = np.minimum(large, half - 1)
    bucket = np.where(rel > 0, half, 0) + np.where(n < exact, n, large)
    return (bucket[None, :] == np.arange(N_BUCKETS)[:, None]).astype(np.float32)


_INS = ["x", "rel_bias", "norm_mix_g", "w_in", "qk_norm_g", "diff_lambda", "diff_subln_g", "sinks", "w_branch",
        "w_gate", "b_gate", "w_out", "norm_ffn_g", "w_router_group", "b_router_group", "w_router_expert",
        "b_router_expert", "w_ff_gate", "w_ff_up", "w_ff_down"]


def kernel(**inputs):
    import concourse.bacc as bacc
    from concourse.bass_utils import run_bass_kernel_spmd

    nc = bacc.Bacc("TRN2", target_bir_lowering=False, num_devices=1)
    arrays, args = {}, []
    constants = {
        "bucket_onehot": distance_buckets(),
        "identity": np.eye(P, dtype=np.float32),
        "flip": np.ascontiguousarray(np.eye(P, dtype=np.float32)[::-1]),
        "layer_consts": np.array([[i, 1.0 - i] for i in (0.8 - 0.6 * math.exp(-0.3 * l) for l in range(DEPTH))],
                                 np.float32),
    }
    for name in _INS + list(constants):
        a = np.ascontiguousarray(inputs[name] if name in inputs else constants[name])
        arrays[f"in_{name}"] = a
        args.append(nc.dram_tensor(f"in_{name}", a.shape, mybir.dt.from_np(a.dtype), kind="ExternalInput").ap())
    args.append(nc.dram_tensor("out_rows", (1, SEQ, D_MODEL), F32, kind="ExternalOutput").ap())
    hybrid_block(nc, *args)
    r = run_bass_kernel_spmd(nc, [arrays], core_ids=[0])
    return r.results[0]["out_rows"]
```

```python
import math
from contextlib import ExitStack

import numpy as np

import concourse.bass as bass
from concourse import mybir

F32 = mybir.dt.float32
F32R = mybir.dt.float32r
I32 = mybir.dt.int32
ALU = mybir.AluOpType
ACT = mybir.ActivationFunctionType
AX = mybir.AxisListType

P = 128
D_MODEL, SEQ, DEPTH = 1024, 512, 2
CHUNK, HD = 64, 64
A_HEADS, B_HEADS, B_KV, C_HEADS = 4, 8, 2, 8
IDX_HEADS, IDX_DIM = 4, 32
TOP_K = min(256, SEQ // 4)
N_BUCKETS, MAX_DIST = 32, 1024
REL_HEADS = A_HEADS + B_HEADS + C_HEADS
N_BRANCH, WIDTH = 3, 512
N_GROUPS, PER_GROUP = 4, 4
N_EXPERTS = N_GROUPS * PER_GROUP
FF = 256
EPS = 1e-6
NEG = -1e30
LOWEST = -3e38
TAKEN_BELOW = -2e38

TT = SEQ // P
KT = D_MODEL // P
RAW_SLOTS = 3
UNIT_KT = 2
SPAN = 640
CAPACITY = P
RING = 6
PIECES = 3

P_CHUNKS = [("I", 2816, 292), ("Aq", 0, 512), ("Ak", 512, 512), ("Av", 1024, 512),
            ("Bq", 1536, 512), ("Bkv", 2048, 256), ("Cq", 2304, 512)]
UNITS_K = KT // UNIT_KT
T_BLOCKS = {"I": 3, "Aq": 4, "Ak": 4, "Av": 0, "Bq": 4, "Bkv": 2, "Cq": 4}

ROW_MIX, ROW_FFN, ROW_BGATE, ROW_QK, ROW_SUBLN, N_ROWS = 0, 8, 16, 40, 46, 47


class Branch:

    def __init__(self, n, name, heads, lag, per_block, fill, first_head, first_job, first_fill, groups):
        self.n, self.name, self.heads, self.lag, self.per_block = n, name, heads, lag, per_block
        self.fill, self.first_head, self.first_job = fill, first_head, first_job
        self.jobs = heads * TT
        self.blocks = self.jobs // per_block
        self.slots = self.jobs + lag + 3
        self.t_index, self.o_index = {}, {}
        at = first_fill
        for s in range(self.slots):
            if 0 <= s - lag < self.jobs:
                self.t_index[s - lag] = at
                at += 1
            b = self.block_turned(s)
            if b is not None:
                self.o_index[b] = at
                at += 1
        self.end_fill = at
        self.dense = groups

    def block_turned(self, s):
        b, r = divmod(s - self.lag - 3 + 1, self.per_block)
        return b - 1 if r == 0 and 1 <= b <= self.blocks else None

    def block_scaled(self, s):
        b, r = divmod(s - self.lag - 2 + 1, self.per_block)
        return b - 1 if r == 0 and 1 <= b <= self.blocks else None

    def groups_of(self, s):
        return range(self.fill * s, self.fill * (s + 1)) if s < self.jobs else range(0)

    def job(self, j):
        h, i = divmod(j, TT)
        if self.name == "B":
            tiles = [i - 1, i] if i else [0]
        else:
            tiles = list(range(i + 1))
        nk = P * len(tiles)
        return h, i, SEQ - nk, nk, tiles


def gate_chunk(n, c):
    return len(P_CHUNKS) + 4 * n + c


def y_chunk(n, c):
    return len(P_CHUNKS) + 4 * n + 2 + c


OUT_CHUNK = len(P_CHUNKS) + 4 * N_BRANCH
N_CHUNKS = OUT_CHUNK + 2
GATE_GROUPS = 2 * 4 * KT
Y_GROUPS = 2 * 4 * (WIDTH // P)
P_FILLS = sum(T_BLOCKS.values())


def make_branches():
    a = Branch(0, "A", A_HEADS, 1, TT, 4, 0, 0, P_FILLS, [("gate", 0)])
    b = Branch(1, "B", B_HEADS, 2, 2 * TT, 3, A_HEADS, a.jobs, a.end_fill, [("y", 0), ("gate", 1)])
    c = Branch(2, "C", C_HEADS, 2, 2 * TT, 3, A_HEADS + B_HEADS, a.jobs + b.jobs, b.end_fill,
               [("y", 1), ("gate", 2)])
    return [a, b, c]


def dense_groups(dense):
    out = []
    for kind, n in dense:
        units = UNITS_K if kind == "gate" else WIDTH // P // UNIT_KT
        for c in range(2):
            for u in range(units):
                for t in range(4):
                    for k in range(UNIT_KT):
                        out.append((kind, n, c, u, t, k, u == 0 and k == 0,
                                    u == units - 1 and k == UNIT_KT - 1, t == 3 and k == UNIT_KT - 1))
    return out


def unit_list():
    out = [("in", i, u) for i in range(len(P_CHUNKS)) for u in range(UNITS_K)]
    for n in range(N_BRANCH):
        out += [("gate", n, c, u) for c in range(2) for u in range(UNITS_K)]
        out += [("y", n, c, u) for c in range(2) for u in range(WIDTH // P // UNIT_KT)]
    out += [("out", c, u) for c in range(2) for u in range(UNITS_K)]
    return out


def hybrid_block(nc, x, rel_bias, norm_mix_g, w_in, qk_norm_g, diff_lambda, diff_subln_g, sinks, w_branch,
                 w_gate, b_gate, w_out, norm_ffn_g, w_router_group, b_router_group, w_router_expert,
                 b_router_expert, w_ff_gate, w_ff_up, w_ff_down, bucket_onehot, identity, flip, before,
                 expert_ids, token_ids, spill_rows, layer_consts, out):
    units = unit_list()
    unit_at = {u: n for n, u in enumerate(units)}
    branches = make_branches()
    n_jobs = sum(b.jobs for b in branches)
    ctx = ExitStack()

    def sb(name, shape, dt=F32):
        return ctx.enter_context(nc.sbuf_tensor(name, shape, dt))

    def sem(name):
        return ctx.enter_context(nc.semaphore(name))

    with ctx:
        X = sb("X", [P, TT, D_MODEL])
        gT = X[:, :, :].rearrange("p t (a n) -> p (t a) n", a=2)
        hT_hi = sb("hT_hi", [P, KT, SEQ], F32R)
        hT_lo = sb("hT_lo", [P, KT, SEQ], F32R)
        raw = sb("raw", [P, RAW_SLOTS, UNIT_KT, 512])
        w_hi = sb("w_hi", [P, 2, UNIT_KT, 512], F32R)
        w_lo = sb("w_lo", [P, 2, UNIT_KT, 512], F32R)
        ptmp = sb("ptmp", [P, TT, 512])
        sq = sb("sq", [P, 2, 512])
        work = sb("work", [P, RING, 4, SEQ])
        aqT, akT, bqT, cqT, av = (work[:, i] for i in range(5))
        bkT, ckT, iqT = work[:, 5, 0:2], work[:, 5, 2], work[:, 5, 3]
        ikT = sb("ikT", [P, SEQ])
        bv = sb("bv", [P, TT, B_KV * HD])
        cv = sb("cv", [P, TT, HD])
        iw = sb("iw", [P, TT, IDX_HEADS])
        bias = sb("bias", [P, 2, SEQ])
        score = sb("score", [P, P * (2 + 3 + 4)])
        top8 = sb("top8", [P, 8])
        mixed = sb("mixed", [P, KT, SEQ])
        xn = mixed[:, :, :].rearrange("p (t a) n -> p t (a n)", a=2)
        ytmp = sb("ytmp", [P, SEQ])
        bias_sel = ytmp
        oT_hi = sb("oT_hi", [P, 4, SEQ], F32R)
        oT_lo = sb("oT_lo", [P, 4, SEQ], F32R)
        o_rows = sb("o_rows", [P, 2, TT, P])
        probs = sb("probs", [P, 4, SEQ])
        pT = sb("pT", [P, 2, SEQ])
        ident = sb("ident", [P, P])
        prow = sb("prow", [N_ROWS, P])
        pcol = sb("pcol", [P, N_ROWS])
        q_gain = sb("q_gain", [P, N_BRANCH])
        sub_gain = sb("sub_gain", [P, 1])
        lam_rows = sb("lam_rows", [P, 4 * HD])
        lam_sum = sb("lam_sum", [P, 2])
        lam_exp = sb("lam_exp", [P, 2])
        lam_dif = sb("lam_dif", [P, 1])
        neg_lam = sb("neg_lam", [P, 1])
        lconst = sb("lconst", [P, 2])
        sink_row = sb("sink_row", [P, B_HEADS])
        half_neg = sb("half_neg", [P, 32])
        row_ss = sb("row_ss", [P, 2, TT])
        row_ms = sb("row_ms", [P, 2, TT])
        row_rs = sb("row_rs", [P, 2, TT])
        head_ss = sb("head_ss", [P, 2, 32])
        head_ms = sb("head_ms", [P, 2, 32])
        head_rs = sb("head_rs", [P, 2, 32])
        o_ss = sb("o_ss", [P, 2, TT])
        o_ms = sb("o_ms", [P, 2, TT])
        o_rs = sb("o_rs", [P, 2, TT])
        job_max = sb("job_max", [P, 4, 2])
        job_neg = sb("job_neg", [P, 4, 2])
        job_sum = sb("job_sum", [P, 4, 2])
        job_sink = sb("job_sink", [P, 4])
        job_den = sb("job_den", [P, 4])
        job_inv = sb("job_inv", [P, 4, 2])
        job_mix = sb("job_mix", [P, 4])
        wr = sb("wr", [P, KT, 20])
        wr_hi = sb("wr_hi", [P, KT, 20], F32R)
        wr_lo = sb("wr_lo", [P, KT, 20], F32R)
        br = sb("br", [P, 20])
        gate_cur = sb("gate_cur", [P, TT])
        rt = score[:, 0:256].rearrange("p (a n) -> p a n", a=16)
        logit = score[:, 256:336].rearrange("p (t n) -> p t n", t=TT)
        ein = score[:, 336:400].rearrange("p (t g e) -> p t g e", t=TT, g=4)
        gate16 = score[:, 400:464].rearrange("p (e t) -> p e t", t=TT)
        pick = score[:, 464:592].rearrange("p (k t e) -> p k t e", k=2, t=TT)
        both = score[:, 592:656].rearrange("p (t e) -> p t e", t=TT)
        pick_left = score[:, 720:848].rearrange("p (k t e) -> p k t e", k=2, t=TT)
        prod = score[:, 656:720].rearrange("p (t e) -> p t e", t=TT)
        upper = sb("upper", [P, P])
        ones = sb("ones", [P, P])
        eids = sb("eids", [P, N_EXPERTS])
        spill = sb("spill", [P, 2, TT])
        tokens = sb("tokens", [P, TT], I32)
        rank = sb("rank", [P, 2, TT])
        eid = sb("eid", [P, 2, TT])
        fits = sb("fits", [P, 2, TT])
        row = sb("row", [P, 2, TT])
        table_row = sb("table_row", [P, 2, TT], I32)
        y_row = sb("y_row", [P, 2, TT], I32)
        weight = sb("weight", [P, 2, TT])
        left = sb("left", [P, 2, TT])
        spilled = sb("spilled", [P, N_EXPERTS])
        spilled_int = sb("spilled_int", [P, N_EXPERTS], I32)
        slot_token = sb("slot_token", [P, N_EXPERTS], I32)

        gather_rows = probs[:, :, :].rearrange("p (b a) n -> p b (a n)", b=2)
        et = ptmp[:, :, :].rearrange("p (b a) n -> p b (a n)", b=2)
        gain_row = bias[:, :, :].rearrange("p a n -> p (a n)")

        banks = [ctx.enter_context(nc.psum_tensor(f"bank{i}", [P, 512], F32)) for i in range(8)]
        G = banks[0:4]
        S = banks[4:6]
        T = banks[6:8]
        O = banks[7]

        xs = nc.dram_tensor("residual_dram", (SEQ, D_MODEL), F32, kind="Internal").ap()
        toep = nc.dram_tensor("toeplitz_dram", (REL_HEADS, SPAN), F32, kind="Internal").ap()
        bias_dram = nc.dram_tensor("bias_dram", (REL_HEADS, P, SEQ), F32, kind="Internal").ap()

        xn_dram = nc.dram_tensor("normed_dram", (SEQ, D_MODEL), F32, kind="Internal").ap()
        y_dram = nc.dram_tensor("expert_rows_dram", (N_EXPERTS * CAPACITY, D_MODEL), F32, kind="Internal").ap()
        table = nc.dram_tensor("slot_table_dram", (N_EXPERTS * CAPACITY + 2 * SEQ, 1), I32, kind="Internal").ap()

        pre_x = sem("pre_x")
        pre_c = sem("pre_c")
        pre_mm = sem("pre_mm")
        pre_row = sem("pre_row")
        pre_toep = sem("pre_toep")
        pre_in = [sem("pre_in0"), sem("pre_in1")]
        pre_flip = sem("pre_flip")
        pre_cp = sem("pre_cp")
        pre_set = sem("pre_set")
        pre_out = [sem("pre_out0"), sem("pre_out1")]
        pre_half = sem("pre_half")
        pre_zero = sem("pre_zero")
        par = sem("par")
        raw_in = [sem(f"raw_in{i}") for i in range(RAW_SLOTS)]
        split_hi = sem("split_hi")
        split_done = sem("split_done")
        unit_used = sem("unit_used")
        par_turned = sem("par_turned")
        pcol_ready = sem("pcol_ready")
        lam_summed = sem("lam_summed")
        lam_exped = sem("lam_exped")
        gains_ready = sem("gains_ready")
        ss_done = sem("ss_done")
        ms_done = sem("ms_done")
        rs_done = sem("rs_done")
        xn_done = sem("xn_done")
        nt_done = sem("nt_done")
        nhi_done = sem("nhi_done")
        nlo_done = sem("nlo_done")
        g_done = sem("g_done")
        g_free = sem("g_free")
        chunk_copied = sem("chunk_copied")
        squared = sem("squared")
        reduced = sem("reduced")
        cms_done = sem("cms_done")
        crs_done = sem("crs_done")
        chunk_normed = sem("chunk_normed")
        t_done = sem("t_done")
        t_free = sem("t_free")
        idx_done = sem("idx_done")
        relu_done = sem("relu_done")
        relu_used = sem("relu_used")
        s_done = sem("s_done")
        soft_done = sem("soft_done")
        exp_done = sem("exp_done")
        p_ready = sem("p_ready")
        pv_done = sem("pv_done")
        o_free = sem("o_free")
        oms_done = sem("oms_done")
        ors_done = sem("ors_done")
        o_scaled = sem("o_scaled")
        ohi_done = sem("ohi_done")
        bias_in = [sem("bias_in0"), sem("bias_in1")]
        x_back = sem("x_back")
        dve = sem("dve")
        wrhi_done = sem("wrhi_done")
        wr_split = sem("wr_split")
        log_done = sem("log_done")
        rexp_in = sem("rexp_in")
        rexp_out = sem("rexp_out")
        layer_out = sem("layer_out")
        gain_in = sem("gain_in")
        xn_out = sem("xn_out")
        picked = sem("picked")
        counted = sem("counted")
        over_summed = sem("over_summed")
        over_counted = sem("over_counted")
        rows_ready = sem("rows_ready")
        over_known = sem("over_known")
        scattered = sem("scattered")
        table_in = sem("table_in")
        piece_in = [sem(f"piece_in{i}") for i in range(RING)]
        first_half = sem("first_half")
        gathered = [sem("gathered0"), sem("gathered1")]
        et_turned = sem("et_turned")
        et_act = sem("et_act")
        et_dve = sem("et_dve")
        gu_done = sem("gu_done")
        silu_done = sem("silu_done")
        hid_done = sem("hid_done")
        hid_turned = sem("hid_turned")
        hidT_done = sem("hidT_done")
        down_done = sem("down_done")
        y_act = sem("y_act")
        y_dve = sem("y_dve")
        y_out = [sem(f"y_out{i}") for i in range(4)]
        y_back = [sem("y_back0"), sem("y_back1")]
        added = sem("added")
        layer_sems = [par, *raw_in, split_hi, split_done, unit_used, par_turned, pcol_ready, lam_summed, lam_exped,
                      gains_ready, ss_done, ms_done, rs_done, xn_done, nt_done, nhi_done, nlo_done, g_done, g_free,
                      chunk_copied, squared, reduced, cms_done, crs_done, chunk_normed, t_done, t_free, idx_done,
                      relu_done, relu_used, s_done, soft_done, exp_done, p_ready, pv_done, o_free, oms_done,
                      ors_done, o_scaled, ohi_done, *bias_in, x_back, dve, wrhi_done, wr_split, log_done, rexp_in,
                      rexp_out, layer_out, gain_in, xn_out, picked, counted, over_summed, over_counted,
                      rows_ready, over_known, scattered, table_in, *piece_in, first_half, *gathered, et_turned,
                      et_act, et_dve, gu_done, silu_done, hid_done, hid_turned, hidT_done, down_done, y_act, y_dve,
                      *y_out, *y_back, added]
        e_raw = [sem(f"e_raw{i}") for i in range(RAW_SLOTS)]
        e_hi = sem("e_hi")
        e_split = sem("e_split")
        e_used = sem("e_used")
        e_gu = sem("e_gu")
        e_silu = sem("e_silu")
        e_dve = sem("e_dve")
        e_hid = sem("e_hid")
        e_down = sem("e_down")
        e_free = sem("e_free")
        expert_sems = [*e_raw, e_hi, e_split, e_used, e_gu, e_silu, e_dve, e_hid, e_down, e_free]
        expert_end = [sem("expert_done"), sem("expert_go"), sem("expert_ack")]
        dense_start = [sem("dense_start_done"), sem("dense_start_go"), sem("dense_start_ack")]
        layer_end = [sem("layer_done"), sem("layer_go"), sem("layer_ack")]

        def meet_and_clear(sp, point, sems):
            meet_done, meet_go, meet_ack = point
            sp.wait_ge(meet_done, 4)
            for s in sems:
                sp.sem_clear(s)
            sp.sem_clear(meet_done)
            sp.sem_inc(meet_go, 1)
            sp.wait_ge(meet_ack, 4)
            sp.sem_clear(meet_go)
            sp.sem_clear(meet_ack)

        def meet(eng, point):
            meet_done, meet_go, meet_ack = point
            eng.drain()
            eng.sem_inc(meet_done, 1)
            eng.wait_ge(meet_go, 1)
            eng.sem_inc(meet_ack, 1)

        def layer_of(w, l):
            return w[bass.ds(l, 1)]

        def unit_source(unit, l):
            kind = unit[0]
            if kind == "in":
                _, c0, w = P_CHUNKS[unit[1]]
                src, u = layer_of(w_in, l)[:, :, c0:c0 + w], unit[2]
            elif kind == "gate":
                _, n, c, u = unit
                c0 = n * D_MODEL + c * 512
                src = layer_of(w_gate, l)[:, :, c0:c0 + 512]
            elif kind == "y":
                _, n, c, u = unit
                src = w_branch.rearrange("l n w d -> (l n) w d")[bass.ds(l * N_BRANCH + n, 1), :, c * 512:c * 512 + 512]
            else:
                _, c, u = unit
                src = layer_of(w_out, l)[:, :, c * 512:c * 512 + 512]
            src = src[:, u * UNIT_KT * P:(u + 1) * UNIT_KT * P, :]
            return src.rearrange("a (k p) n -> p (a k) n", p=P)

        chunk_names = list(dict.fromkeys(u[:-1] for u in units))

        def unit_end(n):
            k = chunk_names.index(units[n][:-1])
            if n + 1 == len(units) or units[n + 1][:-1] != units[n][:-1]:
                return True, 4 * (k + 1)
            return False, n + 1 - k

        E_UNITS = [("gu", u) for u in range(UNITS_K)] + [("down", c) for c in range(2)]

        def expert_raw_value(n):
            return sum(32 if E_UNITS[m][0] == "gu" else 16 for m in range(n % RAW_SLOTS, n + 1, RAW_SLOTS))

        block = ctx.enter_context(nc.Block())

        @block.sync
        def _(sp):
            sp.dma_start(X[:, :, :], x.rearrange("b (t p) d -> p (b t) d", p=P)).then_inc(pre_x, 16)
            sp.dma_start(ident[:, :], identity).then_inc(pre_c, 16)
            sp.dma_start(probs[:, 0, 0:P], flip).then_inc(pre_c, 16)
            sp.dma_start(probs[0:N_BUCKETS, 1, 0:REL_HEADS], rel_bias).then_inc(pre_c, 16)
            sp.dma_start(aqT[0:N_BUCKETS, 0:2, 0:SPAN // 2],
                         bucket_onehot.rearrange("b (a n) -> b a n", a=2)).then_inc(pre_c, 16)
            for dst, src in ((upper[:, :], before), (eids[:, :], expert_ids), (spill[:, :, :], spill_rows),
                             (tokens[:, :], token_ids)):
                sp.dma_start(dst, src).then_inc(pre_c, 16)
            sp.wait_ge(pre_x, 16)
            sp.dma_start(xs.rearrange("(t p) d -> p t d", p=P), X[:, :, :]).then_inc(pre_x, 16)
            sp.wait_ge(pre_row, 2)
            sp.dma_start(toep.rearrange("h (a n) -> h a n", a=2),
                         akT[0:REL_HEADS, 0:2, 0:SPAN // 2]).then_inc(pre_toep, 16)
            sp.wait_ge(pre_toep, 16)
            for h in range(REL_HEADS + 2):
                if h < REL_HEADS:
                    if h >= 2:
                        sp.wait_ge(pre_flip, h - 1)
                    row = toep[h:h + 1, 0:SEQ]
                    shifted = bass.AP(row.tensor, row.offset, [[1, P], [1, SEQ]])
                    sp.dma_start(bqT[:, h % 2, :], shifted).then_inc(pre_in[h % 2], 16)
                if h >= 2:
                    sp.wait_ge(pre_set, h - 1)
                    sp.dma_start(bias_dram[h - 2], cqT[:, h % 2, :]).then_inc(pre_out[h % 2], 16)
            sp.wait_ge(pre_out[0], 16 * REL_HEADS // 2)
            sp.wait_ge(pre_out[1], 16 * REL_HEADS // 2)
            sp.wait_ge(pre_zero, 1)
            sp.dma_start(table[0:N_EXPERTS * CAPACITY].rearrange("(s e) o -> s (e o)", e=N_EXPERTS),
                         slot_token[:, :]).then_inc(pre_toep, 16)
            sp.wait_ge(pre_toep, 32)
            sp.wait_ge(pre_c, 16 * 8)
            sp.wait_ge(pre_x, 32)
            sp.sem_inc(pre_half, 1)
            with sp.Fori(0, DEPTH) as l:
                sp.dma_start(prow[ROW_MIX:ROW_MIX + 8, :],
                             layer_of(norm_mix_g, l).rearrange("a (r c) -> (a r) c", c=P)).then_inc(par, 16)
                sp.dma_start(prow[ROW_FFN:ROW_FFN + 8, :],
                             layer_of(norm_ffn_g, l).rearrange("a (r c) -> (a r) c", c=P)).then_inc(par, 16)
                sp.dma_start(prow[ROW_BGATE:ROW_BGATE + 24, :],
                             layer_of(b_gate, l).rearrange("a (r c) -> (a r) c", c=P)).then_inc(par, 16)
                for half in range(2):
                    sp.dma_start(prow[ROW_QK:ROW_QK + 6, half * HD:(half + 1) * HD],
                                 layer_of(qk_norm_g, l).rearrange("a n b d -> (a n b) d")).then_inc(par, 16)
                sp.dma_start(prow[ROW_SUBLN:ROW_SUBLN + 1, :], layer_of(diff_subln_g, l)).then_inc(par, 16)
                for unit in range(RAW_SLOTS):
                    w = P_CHUNKS[units[unit][1]][2]
                    sp.dma_start(raw[:, unit, :, 0:w], unit_source(units[unit], l)).then_inc(raw_in[unit], 16)
                sp.dma_start(lam_rows[:, :],
                             layer_of(diff_lambda, l).rearrange("a r d -> a (r d)").broadcast_to([P, 4 * HD])
                             ).then_inc(par, 16)
                sp.dma_start(sink_row[:, :], layer_of(sinks, l).broadcast_to([P, B_HEADS])).then_inc(par, 16)
                sp.dma_start(lconst[:, :], layer_of(layer_consts, l).broadcast_to([P, 2])).then_inc(par, 16)
                sp.dma_start(br[:, 0:4], layer_of(b_router_group, l).broadcast_to([P, 4])).then_inc(par, 16)
                sp.dma_start(br[:, 4:20], layer_of(b_router_expert, l).broadcast_to([P, 16])).then_inc(par, 16)
                sp.dma_start(wr[:, :, 0:4],
                             layer_of(w_router_group, l).rearrange("a (k p) n -> p (a k) n", p=P)).then_inc(par, 16)
                sp.dma_start(wr[:, :, 4:20],
                             layer_of(w_router_expert, l).rearrange("a (k p) n -> p (a k) n", p=P)).then_inc(par, 16)
                for n in range(RAW_SLOTS, len(units)):
                    w = P_CHUNKS[units[n][1]][2] if units[n][0] == "in" else 512
                    sp.wait_ge(split_done, n - RAW_SLOTS + 1)
                    sp.dma_start(raw[:, n % RAW_SLOTS, :, 0:w],
                                 unit_source(units[n], l)).then_inc(raw_in[n % RAW_SLOTS], 16)
                for n in range(PIECES * N_EXPERTS):
                    e, part = divmod(n, PIECES)
                    if n == 0:
                        sp.wait_ge(pv_done, n_jobs)
                    if n >= RING:
                        used, per = ((first_half, 1), (gu_done, 1), (down_done, 2))[(n - RING) % PIECES]
                        sp.wait_ge(used, per * ((n - RING) // PIECES + 1))
                    slot = n % RING
                    if part < 2:
                        for half, w in enumerate((w_ff_gate, w_ff_up)):
                            src = layer_of(w, l)[:, e, part * 512:(part + 1) * 512, :]
                            sp.dma_start(work[:, slot, :, half * FF:(half + 1) * FF],
                                         src.rearrange("a (k p) n -> p (a k) n", p=P)).then_inc(piece_in[slot], 16)
                    else:
                        sp.dma_start(work[:, slot].rearrange("p (k c) n -> p k (c n)", k=2),
                                     layer_of(w_ff_down, l)[:, e].rearrange("a (k p) n -> p (a k) n", p=P)
                                     ).then_inc(piece_in[slot], 16)
                sp.wait_ge(over_known, 1)
                with sp.Fori(0, N_EXPERTS) as e:
                    over = sp.value_load(spilled_int[0:1, bass.ds(e, 1)], min_val=0, max_val=SEQ)
                    with sp.If(over > 0):
                        meet_and_clear(sp, dense_start, [])
                        le = l * N_EXPERTS + e
                        for n, (kind, u) in enumerate(E_UNITS):
                            if n >= RAW_SLOTS:
                                sp.wait_ge(e_split, n - RAW_SLOTS + 1)
                            dst = raw[:, n % RAW_SLOTS]
                            if kind == "gu":
                                for half, w in enumerate((w_ff_gate, w_ff_up)):
                                    src = w.rearrange("l e d f -> (l e) d f")[bass.ds(le, 1),
                                                                              u * UNIT_KT * P:(u + 1) * UNIT_KT * P, :]
                                    sp.dma_start(dst[:, :, half * FF:(half + 1) * FF],
                                                 src.rearrange("a (k p) n -> p (a k) n", p=P)
                                                 ).then_inc(e_raw[n % RAW_SLOTS], 16)
                            else:
                                src = w_ff_down.rearrange("l e f d -> (l e) f d")[bass.ds(le, 1), :, u * 512:u * 512 + 512]
                                sp.dma_start(dst, src.rearrange("a (k p) n -> p (a k) n", p=P)
                                             ).then_inc(e_raw[n % RAW_SLOTS], 16)
                        meet_and_clear(sp, expert_end, expert_sems)
                sp.wait_ge(layer_end[0], 4)
                sp.dma_start(xs.rearrange("(t p) d -> p t d", p=P), X[:, :, :]).then_inc(layer_out, 16)
                sp.wait_ge(layer_out, 16)
                meet_and_clear(sp, layer_end, layer_sems)
            sp.dma_start(out.rearrange("b (t p) d -> p (b t) d", p=P), X[:, :, :]).then_inc(pre_x, 16)
            sp.wait_ge(pre_x, 48)

        @block.gpsimd
        def _(pool):
            nc.gpsimd.memset(slot_token[:, :], 0).then_inc(pre_zero, 1)
            nc.gpsimd.memset(ones[:, :], 1.0)
            nc.gpsimd.memset(half_neg[:, :], -0.5).then_inc(pre_half, 1)

            def pow_step(dst, src, n):
                return nc.gpsimd.tensor_tensor(dst, src, half_neg[:, 0:n], ALU.pow)

            def split(n):
                w = P_CHUNKS[units[n][1]][2] if units[n][0] == "in" else 512
                slot, two = n % RAW_SLOTS, n % 2
                pool.wait_ge(raw_in[slot], 16 * (n // RAW_SLOTS + 1))
                if n >= 2:
                    last_of_chunk, value = unit_end(n - 2)
                    pool.wait_ge(g_done if last_of_chunk else unit_used, value)
                nc.gpsimd.tensor_scalar(w_hi[:, two, :, 0:w], raw[:, slot, :, 0:w], 1.0, 0.0,
                                        ALU.mult, ALU.add).then_inc(split_hi, 1)
                pool.wait_ge(split_hi, n + 1)
                nc.gpsimd.tensor_tensor(w_lo[:, two, :, 0:w], raw[:, slot, :, 0:w],
                                        w_hi[:, two, :, 0:w].bitcast(F32), ALU.subtract).then_inc(split_done, 1)

            pool.wait_ge(pre_half, 2)
            normed = [i for i, (name, _, _) in enumerate(P_CHUNKS) if name != "Av"]
            with pool.Fori(0, DEPTH) as l:
                split(0)
                split(1)
                pool.wait_ge(ms_done, 1)
                pow_step(row_rs[:, 0, :], row_ms[:, 0, :], TT).then_inc(rs_done, 1)
                n_gate0 = unit_at[("gate", 0, 0, 0)]
                powed = 0
                for n in range(2, len(units)):
                    split(n)
                    if n < n_gate0 + 4 and n % UNITS_K == 1 and n // UNITS_K - 1 in normed:
                        c = n // UNITS_K - 1
                        w = 8 * TT if P_CHUNKS[c][0] in ("Aq", "Ak", "Bq", "Cq") else 2 * TT
                        if P_CHUNKS[c][0] == "I":
                            w = TT
                        pool.wait_ge(cms_done, normed.index(c) + 1)
                        pow_step(head_rs[:, c % 2, 0:w], head_ms[:, c % 2, 0:w], w).then_inc(crs_done, 1)
                    for b in range(4):
                        if n == n_gate0 + min(2 * b + 4, 9):
                            pool.wait_ge(oms_done, b + 1)
                            pow_step(o_rs[:, b % 2, :], o_ms[:, b % 2, :], TT).then_inc(ors_done, 1)
                pool.wait_ge(ms_done, 2)
                pow_step(row_rs[:, 1, :], row_ms[:, 1, :], TT).then_inc(rs_done, 1)
                pool.wait_ge(rows_ready, 1)
                for k in range(2):
                    for t in range(TT):
                        nc.gpsimd.indirect_dma_start(
                            out=table, out_offset=bass.IndirectOffsetOnAxis(ap=table_row[:, k, t:t + 1], axis=0),
                            in_=tokens[:, t:t + 1], in_offset=None).then_inc(scattered, 16)
                pool.wait_ge(scattered, 16 * 2 * TT)
                pool.dma_start(slot_token[:, :],
                               table[0:N_EXPERTS * CAPACITY].rearrange("(s e) o -> s (e o)", e=N_EXPERTS)
                               ).then_inc(table_in, 16)
                pool.wait_ge(table_in, 16)
                pool.wait_ge(xn_out, 16)
                for e in range(N_EXPERTS):
                    if e >= 2:
                        pool.wait_ge(et_turned, 2 * (e - 1))
                    nc.gpsimd.indirect_dma_start(
                        out=gather_rows[:, e % 2, :], out_offset=None, in_=xn_dram,
                        in_offset=bass.IndirectOffsetOnAxis(ap=slot_token[:, e:e + 1], axis=0)
                    ).then_inc(gathered[e % 2], 16)
                for i in range(4):
                    pool.wait_ge(y_out[i], 16 * N_EXPERTS // 4)
                for t in range(TT):
                    if t >= 2:
                        pool.wait_ge(added, 2 * (t - 1))
                    for k in range(2):
                        nc.gpsimd.indirect_dma_start(
                            out=xn[:, 2 * (t % 2) + k, :], out_offset=None, in_=y_dram,
                            in_offset=bass.IndirectOffsetOnAxis(ap=y_row[:, k, t:t + 1], axis=0)
                        ).then_inc(y_back[t % 2], 16)
                pool.wait_ge(over_known, 1)
                with pool.Fori(0, N_EXPERTS) as e:
                    over = pool.value_load(spilled_int[0:1, bass.ds(e, 1)], min_val=0, max_val=SEQ)
                    with pool.If(over > 0):
                        meet(pool, dense_start)
                        for n in range(len(E_UNITS)):
                            slot, two = n % RAW_SLOTS, n % 2
                            pool.wait_ge(e_raw[slot], expert_raw_value(n))
                            if n >= 2:
                                pool.wait_ge(e_used, n - 1)
                            nc.gpsimd.tensor_scalar(w_hi[:, two], raw[:, slot], 1.0, 0.0,
                                                    ALU.mult, ALU.add).then_inc(e_hi, 1)
                            pool.wait_ge(e_hi, n + 1)
                            nc.gpsimd.tensor_tensor(w_lo[:, two], raw[:, slot], w_hi[:, two].bitcast(F32),
                                                    ALU.subtract).then_inc(e_split, 1)
                        meet(pool, expert_end)
                pool.drain()
                pool.dma_reset()
                meet(pool, layer_end)

        @block.tensor
        def _(pe):
            def three(out_ap, s_hi, s_lo, m_hi, m_lo, start, stop):
                nc.tensor.matmul(out_ap, s_hi, m_lo, start=start, stop=False)
                nc.tensor.matmul(out_ap, s_lo, m_hi, start=False, stop=False)
                return nc.tensor.matmul(out_ap, s_hi, m_hi, start=False, stop=stop)

            pe.wait_ge(pre_c, 16 * 8)
            for a in range(2):
                nc.tensor.matmul(G[a][0:REL_HEADS, 0:SPAN // 2], probs[0:N_BUCKETS, 1, 0:REL_HEADS],
                                 aqT[0:N_BUCKETS, a, 0:SPAN // 2], start=True, stop=True).then_inc(pre_mm, 1)
            for h in range(REL_HEADS):
                pe.wait_ge(pre_in[h % 2], 16 * (h // 2 + 1))
                if h >= 2:
                    pe.wait_ge(pre_cp, h - 1)
                nc.tensor.matmul(S[h % 2][:, :], probs[:, 0, 0:P], bqT[:, h % 2, :],
                                 start=True, stop=True).then_inc(pre_flip, 1)

            def norm_turns(which):
                for dt in range(KT):
                    pe.wait_ge(xn_done, TT * (which + 1))
                    if dt >= 4:
                        pe.wait_ge(nlo_done, KT * which + dt - 3)
                    for t in range(TT):
                        last = nc.tensor.transpose(G[dt % 4][:, t * P:(t + 1) * P],
                                                   xn[:, t, dt * P:(dt + 1) * P], ident[:, :])
                    last.then_inc(nt_done, 1)

            def rows_chunk(k, first_unit, width, lhs_hi, lhs_lo):
                for u in range(UNITS_K):
                    n = first_unit + u
                    pe.wait_ge(split_done, n + 1)
                    for t in range(TT):
                        if u == 0 and k > 0:
                            pe.wait_ge(g_free, 4 * (k - 1) + t + 1)
                        for kk in range(UNIT_KT):
                            kt = u * UNIT_KT + kk
                            last = three(G[t][:, 0:width], lhs_hi[:, kt, t * P:(t + 1) * P],
                                         lhs_lo[:, kt, t * P:(t + 1) * P], w_hi[:, n % 2, kk, 0:width],
                                         w_lo[:, n % 2, kk, 0:width], kt == 0, kt == KT - 1)
                        if u == UNITS_K - 1 and t < TT - 1:
                            last.then_inc(g_done, 1)
                    if u < UNITS_K - 1:
                        last.then_inc(unit_used, 1)
                last.then_inc(g_done, 1)

            fills = [0]

            def chunk_turns(c):
                name = P_CHUNKS[c][0]
                if T_BLOCKS[name]:
                    pe.wait_ge(chunk_normed, sum(1 for m in range(c + 1) if T_BLOCKS[P_CHUNKS[m][0]]))
                for b in range(T_BLOCKS[name]):
                    n = fills[0]
                    if n >= 2:
                        pe.wait_ge(t_free, n - 1)
                    for t in range(TT):
                        last = nc.tensor.transpose(T[n % 2][:, t * P:(t + 1) * P],
                                                   ptmp[:, t, b * P:(b + 1) * P], ident[:, :])
                    last.then_inc(t_done, 1)
                    fills[0] += 1

            def index_logits():
                pe.wait_ge(t_free, T_BLOCKS["I"])
                n = 0
                for i in range(1, TT):
                    for h in range(IDX_HEADS):
                        if n >= 2:
                            pe.wait_ge(relu_done, n - 1)
                        r = slice(IDX_DIM * h, IDX_DIM * (h + 1))
                        nc.tensor.matmul(S[n % 2][:, 0:P * (i + 1)], iqT[r, i * P:(i + 1) * P],
                                         ikT[r, 0:P * (i + 1)], start=True, stop=True).then_inc(idx_done, 1)
                        n += 1

            def dense_step(group):
                kind, n, c, u, t, kk, first, last_of_bank, last_of_unit = group
                unit = unit_at[(kind, n, c, u)]
                k = gate_chunk(n, c) if kind == "gate" else y_chunk(n, c)
                if t == 0 and kk == 0:
                    pe.wait_ge(split_done, unit + 1)
                    if kind == "y" and c == 0 and u == 0:
                        pe.wait_ge(ohi_done, 2 * 4 * (n + 1))
                if first:
                    pe.wait_ge(g_free, 4 * (k - 1) + t + 1)
                hi, lo = (hT_hi, hT_lo) if kind == "gate" else (oT_hi, oT_lo)
                kt = u * UNIT_KT + kk
                last = three(G[t][:, :], w_hi[:, unit % 2, kk, t * P:(t + 1) * P],
                             w_lo[:, unit % 2, kk, t * P:(t + 1) * P], hi[:, kt, :], lo[:, kt, :], first,
                             last_of_bank)
                if last_of_bank:
                    last.then_inc(g_done, 1)
                elif last_of_unit:
                    last.then_inc(unit_used, 1)

            def scores(br_, j):
                h, i, _, nk, tiles = br_.job(j)
                k0 = tiles[0] * P
                job = br_.first_job + j
                if br_.name == "A":
                    pe.wait_ge(soft_done, job) if job else None
                    for m in range(2):
                        r = slice(HD * m, HD * (m + 1))
                        last = nc.tensor.matmul(S[m][:, 0:nk], aqT[r, h, i * P:(i + 1) * P],
                                                akT[r, h, k0:k0 + nk], start=True, stop=True)
                else:
                    pe.wait_ge(soft_done, br_.first_job + max(j - 1, 0))
                    r = slice(HD * (h % 2), HD * (h % 2 + 1))
                    q, k = (bqT, bkT[:, h // (B_HEADS // B_KV), :]) if br_.name == "B" else (cqT, ckT)
                    last = nc.tensor.matmul(S[j % 2][:, 0:nk], q[r, h // 2, i * P:(i + 1) * P],
                                            k[r, k0:k0 + nk], start=True, stop=True)
                last.then_inc(s_done, 1)

            def prob_of(br_, j):
                return probs[:, 2 * (j % 2), :] if br_.name == "A" else probs[:, j % 4, :]

            def turn_probs(br_, j):
                _, _, _, nk, tiles = br_.job(j)
                pe.wait_ge(p_ready, br_.first_job + j + 1)
                pe.wait_ge(t_free, br_.t_index[j])
                for b in range(len(tiles)):
                    last = nc.tensor.transpose(T[0][:, b * P:(b + 1) * P],
                                               prob_of(br_, j)[:, b * P:(b + 1) * P], ident[:, :])
                last.then_inc(t_done, 1)

            def times_values(br_, j):
                h, _, _, _, tiles = br_.job(j)
                job = br_.first_job + j
                pe.wait_ge(t_free, br_.t_index[j] + 1)
                if job:
                    pe.wait_ge(o_free, job)
                for b, kt in enumerate(tiles):
                    if br_.name == "A":
                        v = av[:, kt, h * P:(h + 1) * P]
                    elif br_.name == "B":
                        g = h // (B_HEADS // B_KV)
                        v = bv[:, kt, g * HD:(g + 1) * HD]
                    else:
                        v = cv[:, kt, :]
                    w = v.shape[-1]
                    last = nc.tensor.matmul(O[:, (job % 4) * P:(job % 4) * P + w], pT[:, j % 2, b * P:(b + 1) * P], v,
                                            start=(b == 0), stop=(b == len(tiles) - 1))
                last.then_inc(pv_done, 1)

            def turn_rows(br_, b):
                if br_.name == "A":
                    pe.wait_ge(o_scaled, b + 1)
                else:
                    pe.wait_ge(o_free, br_.first_job + br_.per_block * (b + 1))
                pe.wait_ge(t_free, br_.o_index[b])
                for t in range(TT):
                    last = nc.tensor.transpose(T[0][:, t * P:(t + 1) * P], o_rows[:, b % 2, t, :], ident[:, :])
                last.then_inc(t_done, 1)

            def attention(br_):
                groups = dense_groups(br_.dense)
                for s in range(br_.slots):
                    if s < br_.jobs:
                        scores(br_, s)
                    if 0 <= s - br_.lag < br_.jobs:
                        turn_probs(br_, s - br_.lag)
                    if 0 <= s - br_.lag - 1 < br_.jobs:
                        times_values(br_, s - br_.lag - 1)
                    if br_.block_turned(s) is not None:
                        turn_rows(br_, br_.block_turned(s))
                    for g in br_.groups_of(s):
                        dense_step(groups[g])

            def turn_gathered(e):
                pe.wait_ge(gathered[e % 2], 16 * (e // 2 + 1))
                if e >= 1:
                    pe.wait_ge(et_act, e)
                    pe.wait_ge(et_dve, e)
                for a in range(2):
                    for q in range(4):
                        dt = 4 * a + q
                        last = nc.tensor.transpose(S[a][:, q * P:(q + 1) * P],
                                                   gather_rows[:, e % 2, dt * P:(dt + 1) * P], ident[:, :])
                    last.then_inc(et_turned, 1)

            def gate_up(e):
                pe.wait_ge(et_act, e + 1)
                pe.wait_ge(et_dve, e + 1)
                if e >= 2:
                    pe.wait_ge(hid_done, e - 1)
                for part in range(2):
                    n = PIECES * e + part
                    pe.wait_ge(piece_in[n % RING], 32 * (n // RING + 1))
                    for kk in range(4):
                        kt = 4 * part + kk
                        last = nc.tensor.matmul(G[e % 2][:, :], et[:, e % 2, kt * P:(kt + 1) * P],
                                                work[:, n % RING, kk, :], start=(kt == 0), stop=(kt == KT - 1))
                    last.then_inc(first_half if part == 0 else gu_done, 1)

            def turn_hidden(e):
                pe.wait_ge(hid_done, e + 1)
                if e >= 2:
                    pe.wait_ge(hidT_done, e - 1)
                for f in range(2):
                    last = nc.tensor.transpose(T[e % 2][:, f * P:(f + 1) * P],
                                               sq[:, e % 2, FF + f * P:FF + (f + 1) * P], ident[:, :])
                last.then_inc(hid_turned, 1)

            def down(e):
                n = PIECES * e + 2
                pe.wait_ge(hidT_done, e + 1)
                pe.wait_ge(piece_in[n % RING], 16 * (n // RING + 1))
                w = work[:, n % RING].rearrange("p (k c) n -> p k (c n)", k=2)
                for c in range(2):
                    if e >= 1:
                        pe.wait_ge((y_act, y_dve)[c], e)
                    for f in range(2):
                        last = nc.tensor.matmul(G[2 + c][:, :], pT[:, e % 2, f * P:(f + 1) * P],
                                                w[:, f, c * 512:(c + 1) * 512], start=(f == 0), stop=(f == 1))
                    last.then_inc(down_done, 1)

            pe.wait_ge(pre_half, 2)
            with pe.Fori(0, DEPTH) as l:
                fills[0] = 0
                pe.wait_ge(par, 16 * 13)
                nc.tensor.transpose(G[0][:, 0:N_ROWS], prow[:, :], ident[0:N_ROWS, 0:N_ROWS]).then_inc(par_turned, 1)
                pe.wait_ge(pcol_ready, 1)
                norm_turns(0)
                pe.wait_ge(nlo_done, KT)
                for c in range(len(P_CHUNKS)):
                    rows_chunk(c, c * UNITS_K, P_CHUNKS[c][2], hT_hi, hT_lo)
                    if c >= 1:
                        chunk_turns(c - 1)
                    if c == 1:
                        index_logits()
                chunk_turns(len(P_CHUNKS) - 1)
                pe.wait_ge(t_free, P_FILLS)
                for br_ in branches:
                    attention(br_)
                for group in dense_groups([("y", 2)]):
                    dense_step(group)
                pe.wait_ge(g_free, 4 * OUT_CHUNK)
                for c in range(2):
                    rows_chunk(OUT_CHUNK + c, unit_at[("out", c, 0)], 512, hT_hi, hT_lo)
                pe.wait_ge(g_free, 4 * N_CHUNKS)
                norm_turns(1)
                pe.wait_ge(nlo_done, 2 * KT)
                pe.wait_ge(wr_split, 1)
                for t in range(TT):
                    for kt in range(KT):
                        last = three(S[0][:, t * 20:(t + 1) * 20], hT_hi[:, kt, t * P:(t + 1) * P],
                                     hT_lo[:, kt, t * P:(t + 1) * P], wr_hi[:, kt, :], wr_lo[:, kt, :],
                                     kt == 0, kt == KT - 1)
                last.then_inc(log_done, 1)
                pe.wait_ge(picked, 1)
                for t in range(TT):
                    for u in range(t + 1):
                        last = nc.tensor.matmul(S[1][:, t * N_EXPERTS:(t + 1) * N_EXPERTS],
                                                upper[:, :] if u == t else ones[:, :], both[:, u, :],
                                                start=(u == 0), stop=(u == t))
                last.then_inc(counted, 1)
                pe.wait_ge(over_summed, 1)
                nc.tensor.matmul(S[0][:, 0:N_EXPERTS], ones[:, :], spilled[:, :], start=True, stop=True).then_inc(over_counted, 1)
                pe.wait_ge(over_known, 1)
                turn_gathered(0)
                for e in range(N_EXPERTS + 1):
                    if e < N_EXPERTS:
                        gate_up(e)
                    if e + 1 < N_EXPERTS:
                        turn_gathered(e + 1)
                    if e >= 1:
                        down(e - 1)
                    if e < N_EXPERTS:
                        turn_hidden(e)
                with pe.Fori(0, N_EXPERTS) as e:
                    over = pe.value_load(spilled_int[0:1, bass.ds(e, 1)], min_val=0, max_val=SEQ)
                    with pe.If(over > 0):
                        meet(pe, dense_start)
                        for n in range(UNITS_K):
                            pe.wait_ge(e_split, n + 1)
                            for t in range(4):
                                for kk in range(UNIT_KT):
                                    kt = n * UNIT_KT + kk
                                    last = three(G[t][:, :], w_hi[:, n % 2, kk, t * P:(t + 1) * P],
                                                 w_lo[:, n % 2, kk, t * P:(t + 1) * P], hT_hi[:, kt, :], hT_lo[:, kt, :],
                                                 kt == 0, kt == KT - 1)
                            last.then_inc(e_used, 1)
                        pe.wait_ge(e_used, UNITS_K)
                        pe.sem_inc(e_gu, 1)
                        pe.wait_ge(e_hid, 2)
                        for c in range(2):
                            n = UNITS_K + c
                            pe.wait_ge(e_split, n + 1)
                            for t in range(TT):
                                if c == 1:
                                    pe.wait_ge(e_free, t + 1)
                                for kk in range(FF // P):
                                    last = three(banks[4 + t][:, :], oT_hi[:, kk, t * P:(t + 1) * P],
                                                 oT_lo[:, kk, t * P:(t + 1) * P], w_hi[:, n % 2, kk, :],
                                                 w_lo[:, n % 2, kk, :], kk == 0, kk == FF // P - 1)
                                last.then_inc(e_down, 1)
                            if c == 0:
                                pe.wait_ge(e_down, TT)
                                pe.sem_inc(e_used, 1)
                        meet(pe, expert_end)
                meet(pe, layer_end)

        @block.scalar
        def _(act):
            def norm_rows(which):
                for t in range(TT):
                    if which + t:
                        act.wait_ge(ss_done, TT * which + t)
                    nc.scalar.activation(ptmp[:, 0:2, :].rearrange("p a n -> p (a n)"), X[:, t, :], ACT.Square,
                                         accum_out=row_ss[:, which, t:t + 1]).then_inc(ss_done, 1)

            def norm_hi(which, row):
                for dt in range(KT):
                    act.wait_ge(nt_done, KT * which + dt + 1)
                    gain = 1.0 if row is None else pcol[:, row + dt:row + dt + 1]
                    nc.scalar.activation(hT_hi[:, dt, :], G[dt % 4][:, :], ACT.Copy, scale=gain).then_inc(nhi_done, 1)

            n_sq = [0]
            n_copy = [0]
            fills = [0]

            def chunk_out(c):
                name = P_CHUNKS[c][0]
                fills_before = sum(T_BLOCKS[P_CHUNKS[m][0]] for m in range(c))
                for t in range(TT):
                    act.wait_ge(g_done, 4 * c + t + 1)
                    if t == 0 and fills_before and T_BLOCKS[name]:
                        act.wait_ge(t_done, fills_before)
                    ps = G[t]
                    if name == "Av":
                        nc.scalar.activation(av[:, t, :], ps[:, :], ACT.Copy).then_inc(g_free, 1)
                        continue
                    if name == "I":
                        nc.scalar.activation(ptmp[:, t, 384:448], ps[:, 0:64], ACT.Copy)
                        nc.scalar.activation(cv[:, t, :], ps[:, 64:128], ACT.Copy)
                        nc.scalar.activation(ptmp[:, t, 128:256], ps[:, 128:256], ACT.Copy)
                        nc.scalar.activation(ptmp[:, t, 256:384].rearrange("p (r d) -> p r d", r=4),
                                             ps[:, 256:288].unsqueeze(1).broadcast_to([P, 4, IDX_DIM]), ACT.Copy)
                        nc.scalar.activation(iw[:, t, :], ps[:, 288:292], ACT.Copy).then_inc(chunk_copied, 1)
                        w = 64
                    elif name == "Bkv":
                        nc.scalar.activation(bv[:, t, :], ps[:, 128:256], ACT.Copy)
                        nc.scalar.activation(ptmp[:, t, 256:384], ps[:, 0:128], ACT.Copy).then_inc(chunk_copied, 1)
                        w = 128
                    else:
                        nc.scalar.activation(ptmp[:, t, :], ps[:, :], ACT.Copy).then_inc(chunk_copied, 1)
                        w = 512
                    n_copy[0] += 1
                    if n_sq[0] >= 2:
                        act.wait_ge(reduced, n_sq[0] - 1)
                    nc.scalar.activation(sq[:, n_sq[0] % 2, 0:w], ps[:, 0:w], ACT.Square).then_inc(squared, 1)
                    n_sq[0] += 1
                    act.wait_ge(squared, n_sq[0])
                    act.wait_ge(chunk_copied, n_copy[0])
                    act.sem_inc(g_free, 1)

            def turned_out(c):
                name = P_CHUNKS[c][0]
                for b in range(T_BLOCKS[name]):
                    n = fills[0]
                    act.wait_ge(t_done, n + 1)
                    src = T[n % 2][:, :]
                    k_gain = {"A": 1, "B": 3, "C": 5}
                    if name == "I":
                        dst, gain = [(ckT, pcol[:, ROW_QK + 5:ROW_QK + 6]), (iqT, 1.0), (ikT[:, :], 1.0)][b]
                    elif name == "Bkv":
                        dst, gain = bkT[:, b, :], pcol[:, ROW_QK + 3:ROW_QK + 4]
                    elif name == "Ak":
                        dst, gain = akT[:, b, :], pcol[:, ROW_QK + 1:ROW_QK + 2]
                    else:
                        q = "ABC".index(name[0])
                        dst, gain = (aqT, bqT, cqT)[q][:, b, :], q_gain[:, q:q + 1]
                    nc.scalar.activation(dst, src, ACT.Copy, scale=gain).then_inc(t_free, 1)
                    fills[0] += 1

            def index_relu():
                n = 0
                for i in range(1, TT):
                    for h in range(IDX_HEADS):
                        act.wait_ge(idx_done, n + 1)
                        if n >= 4:
                            act.wait_ge(relu_used, n - 3)
                        nc.scalar.activation(probs[:, n % 4, 0:P * (i + 1)], S[n % 2][:, 0:P * (i + 1)],
                                             ACT.Relu).then_inc(relu_done, 1)
                        n += 1

            def load_bias(gh):
                act.dma_start(bias[:, gh % 2, :], bias_dram[gh]).then_inc(bias_in[gh % 2], 16)

            def exps(br_, j):
                h, i, _, nk, _ = br_.job(j)
                job = br_.first_job + j
                gh = br_.first_head + h
                act.wait_ge(soft_done, job + 1)
                if i == 0 and 1 <= gh < REL_HEADS - 1:
                    load_bias(gh + 1)
                st = j % 4
                for m in range(2 if br_.name == "A" else 1):
                    p = probs[:, 2 * (j % 2) + m, 0:nk] if br_.name == "A" else probs[:, j % 4, 0:nk]
                    last = nc.scalar.activation(p, p, ACT.Exp, bias=job_neg[:, st, m:m + 1],
                                                accum_out=job_sum[:, st, m:m + 1])
                if br_.name == "B":
                    last = nc.scalar.activation(job_sink[:, st:st + 1], sink_row[:, h:h + 1], ACT.Exp,
                                                bias=job_neg[:, st, 0:1])
                last.then_inc(exp_done, 1)

            def attention(br_):
                groups = dense_groups(br_.dense)
                for s in range(br_.slots):
                    if s < br_.jobs:
                        exps(br_, s)
                    if 0 <= s - br_.lag < br_.jobs:
                        j = s - br_.lag
                        _, _, _, nk, _ = br_.job(j)
                        act.wait_ge(t_done, br_.t_index[j] + 1)
                        if br_.first_job + j >= 2:
                            act.wait_ge(pv_done, br_.first_job + j - 1)
                        nc.scalar.activation(pT[:, j % 2, 0:nk], T[0][:, 0:nk], ACT.Copy).then_inc(t_free, 1)
                    b = br_.block_turned(s)
                    if b is not None:
                        act.wait_ge(t_done, br_.o_index[b] + 1)
                        if b == 0 and br_.n > 0:
                            act.wait_ge(g_done, 4 * (y_chunk(br_.n - 1, 1) + 1))
                        gain = sub_gain[:, 0:1] if br_.name == "A" else 1.0
                        nc.scalar.activation(oT_hi[:, b, :], T[0][:, :], ACT.Copy, scale=gain).then_inc(ohi_done, 1)
                    for g in br_.groups_of(s):
                        kind, n, c, _, t, _, _, last_of_bank, _ = groups[g]
                        if kind == "gate" and last_of_bank:
                            act.wait_ge(g_done, 4 * gate_chunk(n, c) + t + 1)
                            row = ROW_BGATE + n * KT + c * 4 + t
                            nc.scalar.activation(gT[:, c * 4 + t, :], G[t][:, :], ACT.Sigmoid,
                                                 bias=pcol[:, row:row + 1]).then_inc(g_free, 1)

            def et_out(e):
                act.wait_ge(et_turned, 2 * e + 1)
                if e >= 2:
                    act.wait_ge(gu_done, e - 1)
                nc.scalar.activation(et[:, e % 2, 0:512], S[0][:, :], ACT.Copy).then_inc(et_act, 1)

            def rows_down(e):
                act.wait_ge(down_done, 2 * e + 1)
                if e >= 4:
                    act.wait_ge(y_out[e % 4], 16 * (e // 4))
                nc.scalar.activation(xn[:, e % 4, 0:512], G[2][:, :], ACT.Copy).then_inc(y_act, 1)
                act.wait_ge(y_act, e + 1)
                act.wait_ge(y_dve, e + 1)
                act.dma_start(y_dram[e * CAPACITY:(e + 1) * CAPACITY, :], xn[:, e % 4, :]).then_inc(y_out[e % 4], 16)

            for a in range(2):
                act.wait_ge(pre_mm, a + 1)
                nc.scalar.activation(akT[0:REL_HEADS, a, 0:SPAN // 2], G[a][0:REL_HEADS, 0:SPAN // 2],
                                     ACT.Copy).then_inc(pre_row, 1)
            for h in range(REL_HEADS):
                act.wait_ge(pre_flip, h + 1)
                if h >= 2:
                    act.wait_ge(pre_out[h % 2], 16 * (h // 2))
                nc.scalar.activation(cqT[:, h % 2, :], S[h % 2][:, :], ACT.Copy).then_inc(pre_cp, 1)
            act.wait_ge(pre_half, 2)
            with act.Fori(0, DEPTH) as l:
                n_sq[0] = n_copy[0] = fills[0] = 0
                load_bias(0)
                load_bias(1)
                norm_rows(0)
                act.wait_ge(lam_summed, 1)
                nc.scalar.activation(lam_exp[:, :], lam_sum[:, :], ACT.Exp).then_inc(lam_exped, 1)
                act.wait_ge(gains_ready, 1)
                norm_hi(0, ROW_MIX)
                for c in range(len(P_CHUNKS)):
                    if c >= 1:
                        turned_out(c - 1)
                    chunk_out(c)
                    if c == 1:
                        index_relu()
                turned_out(len(P_CHUNKS) - 1)
                for br_ in branches:
                    attention(br_)
                act.wait_ge(g_free, 4 * OUT_CHUNK)
                act.dma_start(gain_row, layer_of(norm_ffn_g, l).broadcast_to([P, D_MODEL])).then_inc(gain_in, 16)
                act.dma_start(X[:, :, :], xs.rearrange("(t p) d -> p t d", p=P)).then_inc(x_back, 16)
                act.wait_ge(g_free, 4 * N_CHUNKS)
                norm_rows(1)
                act.wait_ge(xn_done, 2 * TT)
                act.dma_start(xn_dram.rearrange("(t p) d -> p t d", p=P), xn).then_inc(xn_out, 16)
                norm_hi(1, None)
                act.wait_ge(rexp_in, 1)
                nc.scalar.activation(rt[:, 0:2, :], rt[:, 0:2, :], ACT.Exp).then_inc(rexp_out, 1)
                et_out(0)
                for e in range(N_EXPERTS + 1):
                    if e < N_EXPERTS:
                        act.wait_ge(gu_done, e + 1)
                        if e >= 2:
                            act.wait_ge(hid_done, e - 1)
                        nc.scalar.activation(sq[:, e % 2, 0:FF], G[e % 2][:, 0:FF], ACT.Silu).then_inc(silu_done, 1)
                    if e + 1 < N_EXPERTS:
                        et_out(e + 1)
                    if e >= 1:
                        rows_down(e - 1)
                act.wait_ge(over_known, 1)
                with act.Fori(0, N_EXPERTS) as e:
                    over = act.value_load(spilled_int[0:1, bass.ds(e, 1)], min_val=0, max_val=SEQ)
                    with act.If(over > 0):
                        meet(act, dense_start)
                        act.wait_ge(e_gu, 1)
                        for f in range(2):
                            nc.scalar.activation(ptmp[:, f, :], G[f][:, :], ACT.Silu).then_inc(e_silu, 1)
                        meet(act, expert_end)
                meet(act, layer_end)

        @block.vector
        def _(v):
            links = [0]

            def link(ins):
                links[0] += 1
                ins.then_inc(dve, 1)
                v.wait_ge(dve, links[0])

            def norm_scale(which):
                v.wait_ge(ss_done, TT * (which + 1))
                nc.vector.tensor_scalar(row_ms[:, which, :], row_ss[:, which, :], 1.0 / D_MODEL, EPS, ALU.mult,
                                        ALU.add).then_inc(ms_done, 1)
                v.wait_ge(rs_done, which + 1)
                for t in range(TT):
                    if which == 0:
                        nc.vector.tensor_scalar(xn[:, t, :], X[:, t, :], row_rs[:, which, t:t + 1], None,
                                                ALU.mult).then_inc(xn_done, 1)
                    else:
                        nc.vector.scalar_tensor_tensor(xn[:, t, :], X[:, t, :], row_rs[:, which, t:t + 1], gain_row,
                                                       ALU.mult, ALU.mult).then_inc(xn_done, 1)

            def norm_lo(which, row):
                for dt in range(KT):
                    v.wait_ge(nhi_done, KT * which + dt + 1)
                    gain = 1.0 if row is None else pcol[:, row + dt:row + dt + 1]
                    nc.vector.scalar_tensor_tensor(hT_lo[:, dt, :], G[dt % 4][:, :], gain,
                                                   hT_hi[:, dt, :].bitcast(F32), ALU.mult,
                                                   ALU.subtract).then_inc(nlo_done, 1)

            n_red = [0]
            n_cms = [0]

            def chunk_stats(c):
                name = P_CHUNKS[c][0]
                heads = {"I": 1, "Bkv": 2}.get(name, 8)
                ss = head_ss[:, c % 2, 0:heads * TT].rearrange("p (t g) -> p t g", t=TT)
                for t in range(TT):
                    v.wait_ge(squared, n_red[0] + 1)
                    nc.vector.tensor_reduce(ss[:, t, :],
                                            sq[:, n_red[0] % 2, 0:heads * HD].rearrange("p (g d) -> p g d", d=HD),
                                            AX.X, ALU.add).then_inc(reduced, 1)
                    n_red[0] += 1
                v.wait_ge(reduced, n_red[0])
                nc.vector.tensor_scalar(head_ms[:, c % 2, 0:heads * TT], head_ss[:, c % 2, 0:heads * TT],
                                        1.0 / HD, EPS, ALU.mult, ALU.add).then_inc(cms_done, 1)
                n_cms[0] += 1

            def chunk_scale(c):
                name = P_CHUNKS[c][0]
                heads = {"I": 1, "Bkv": 2}.get(name, 8)
                v.wait_ge(crs_done, n_cms[0])
                v.wait_ge(chunk_copied, TT * n_cms[0])
                rs = head_rs[:, c % 2, 0:heads * TT]
                if heads == 8:
                    rows = ptmp[:, :, :].rearrange("p t (g d) -> p (t g) d", d=HD)
                    nc.vector.tensor_tensor(rows, rows, rs.unsqueeze(2).broadcast_to([P, 8 * TT, HD]),
                                            ALU.mult).then_inc(chunk_normed, 1)
                    return
                scale = rs.rearrange("p (t g) -> p t g", t=TT).unsqueeze(3).broadcast_to([P, TT, heads, HD])
                first = 384 if name == "I" else 256
                rows = ptmp[:, :, first:first + heads * HD].rearrange("p t (g d) -> p t g d", d=HD)
                for twin in range(2):
                    dst = ptmp[:, :, 0:heads * P].rearrange("p t (g r d) -> p t g r d", r=2, d=HD)[:, :, :, twin, :]
                    last = nc.vector.tensor_tensor(dst, rows, scale, ALU.mult)
                last.then_inc(chunk_normed, 1)

            block_at = {1: 0, 2: 2 * P, 3: 5 * P}

            def index_scores():
                w_scale = IDX_HEADS ** -0.5 * IDX_DIM ** -0.5
                link(nc.vector.tensor_scalar(iw[:, :, :], iw[:, :, :], w_scale, None, ALU.mult))
                n = 0
                for i in range(1, TT):
                    nk = P * (i + 1)
                    dst = score[:, block_at[i]:block_at[i] + nk]
                    for h in range(IDX_HEADS):
                        v.wait_ge(relu_done, n + 1)
                        w = iw[:, i, h:h + 1]
                        if h == 0:
                            nc.vector.tensor_scalar(dst, probs[:, n % 4, 0:nk], w, 0.0, ALU.mult,
                                                    ALU.add).then_inc(relu_used, 1)
                        else:
                            nc.vector.scalar_tensor_tensor(dst, probs[:, n % 4, 0:nk], w, dst, ALU.mult,
                                                           ALU.add).then_inc(relu_used, 1)
                        n += 1
                        v.wait_ge(relu_used, n)
                    link(nc.vector.memset(score[0:CHUNK, block_at[i] + nk - CHUNK:block_at[i] + nk], NEG))

            def top_round(i, r):
                nk = P * (i + 1)
                s = score[:, block_at[i]:block_at[i] + nk]
                link(nc.vector.max(top8[:, :], s))
                link(nc.vector.match_replace(s, top8[:, :], s, LOWEST))
                if r == TOP_K // 8 - 1:
                    link(nc.vector.tensor_scalar(s, s, TAKEN_BELOW, NEG, ALU.is_ge, ALU.mult))

            rounds = [(i, r) for i in range(1, TT) for r in range(TOP_K // 8)]

            def soft(br_, j):
                h, i, c0, nk, _ = br_.job(j)
                job, gh, st = br_.first_job + j, br_.first_head + h, j % 4
                tile_bias = bias[:, gh % 2, c0:c0 + nk]
                if i == 0:
                    v.wait_ge(bias_in[gh % 2], 16 * (gh // 2 + 1))
                if br_.name == "C" and i > 0:
                    link(nc.vector.tensor_tensor(bias_sel[:, 0:nk], tile_bias, score[:, block_at[i]:block_at[i] + nk],
                                                 ALU.add))
                    tile_bias = bias_sel[:, 0:nk]
                v.wait_ge(s_done, job + 1)
                if br_.name == "A":
                    if j >= 2:
                        v.wait_ge(t_done, br_.t_index[j - 2] + 1)
                    for m in range(2):
                        last = nc.vector.tensor_tensor_reduce(probs[:, 2 * (j % 2) + m, 0:nk], S[m][:, 0:nk],
                                                              tile_bias, 1.0, LOWEST, ALU.add, ALU.max,
                                                              job_max[:, st, m:m + 1])
                    link(last)
                    nc.vector.tensor_scalar(job_neg[:, st, :], job_max[:, st, :], -1.0, None,
                                            ALU.mult).then_inc(soft_done, 1)
                    return
                if j >= 4:
                    v.wait_ge(t_done, br_.t_index[j - 4] + 1)
                least = sink_row[:, h:h + 1] if br_.name == "B" else LOWEST
                link(nc.vector.tensor_tensor_reduce(probs[:, j % 4, 0:nk], S[j % 2][:, 0:nk], tile_bias, 1.0, least,
                                                    ALU.add, ALU.max, job_max[:, st, 0:1]))
                nc.vector.tensor_scalar(job_neg[:, st, 0:1], job_max[:, st, 0:1], -1.0, None,
                                        ALU.mult).then_inc(soft_done, 1)

            def post(br_, j):
                _, _, _, nk, _ = br_.job(j)
                job, st = br_.first_job + j, j % 4
                v.wait_ge(exp_done, job + 1)
                if br_.name == "A":
                    link(nc.vector.reciprocal(job_inv[:, st, :], job_sum[:, st, :]))
                    link(nc.vector.tensor_scalar(job_mix[:, st:st + 1], job_sum[:, st, 0:1], job_inv[:, st, 1:2],
                                                 neg_lam[:, 0:1], ALU.mult, ALU.mult))
                    nc.vector.scalar_tensor_tensor(probs[:, 2 * (j % 2), 0:nk], probs[:, 2 * (j % 2) + 1, 0:nk],
                                                   job_mix[:, st:st + 1], probs[:, 2 * (j % 2), 0:nk], ALU.mult,
                                                   ALU.add).then_inc(p_ready, 1)
                elif br_.name == "B":
                    link(nc.vector.tensor_tensor(job_den[:, st:st + 1], job_sum[:, st, 0:1], job_sink[:, st:st + 1],
                                                 ALU.add))
                    nc.vector.reciprocal(job_inv[:, st, 0:1], job_den[:, st:st + 1]).then_inc(p_ready, 1)
                else:
                    nc.vector.reciprocal(job_inv[:, st, 0:1], job_sum[:, st, 0:1]).then_inc(p_ready, 1)

            def rows_out(br_, j):
                h, i, _, _, _ = br_.job(j)
                job, st = br_.first_job + j, j % 4
                b = j // br_.per_block
                v.wait_ge(pv_done, job + 1)
                v.wait_ge(p_ready, job + 1)
                if j % br_.per_block == 0 and b >= 2:
                    v.wait_ge(t_done, br_.o_index[b - 2] + 1)
                w = P if br_.name == "A" else HD
                c0 = 0 if br_.name == "A" else HD * (h % 2)
                nc.vector.tensor_scalar(o_rows[:, b % 2, i, c0:c0 + w], O[:, (job % 4) * P:(job % 4) * P + w],
                                        job_inv[:, st, 0:1], None, ALU.mult).then_inc(o_free, 1)
                if br_.name == "A" and i == TT - 1:
                    v.wait_ge(o_free, job + 1)
                    for t in range(TT):
                        last = nc.vector.tensor_tensor_reduce(sq[:, 0, t * P:(t + 1) * P], o_rows[:, b % 2, t, :],
                                                              o_rows[:, b % 2, t, :], 1.0, 0.0, ALU.mult, ALU.add,
                                                              o_ss[:, b % 2, t:t + 1])
                    link(last)
                    nc.vector.tensor_scalar(o_ms[:, b % 2, :], o_ss[:, b % 2, :], 1.0 / P, EPS, ALU.mult,
                                            ALU.add).then_inc(oms_done, 1)

            def scale_rows(b):
                v.wait_ge(ors_done, b + 1)
                nc.vector.tensor_tensor(o_rows[:, b % 2], o_rows[:, b % 2],
                                        o_rs[:, b % 2, :].unsqueeze(2).broadcast_to([P, TT, P]),
                                        ALU.mult).then_inc(o_scaled, 1)

            def turned_lo(br_, b):
                n = 4 * br_.n + b
                v.wait_ge(ohi_done, 2 * n + 1)
                if br_.name == "A":
                    nc.vector.scalar_tensor_tensor(oT_lo[:, b, :], T[0][:, :], sub_gain[:, 0:1],
                                                   oT_hi[:, b, :].bitcast(F32), ALU.mult,
                                                   ALU.subtract).then_inc(ohi_done, 1)
                else:
                    nc.vector.tensor_tensor(oT_lo[:, b, :], T[0][:, :], oT_hi[:, b, :].bitcast(F32),
                                            ALU.subtract).then_inc(ohi_done, 1)
                v.wait_ge(ohi_done, 2 * n + 2)
                v.sem_inc(t_free, 1)

            def branch_out(n, c, t):
                dt = 4 * c + t
                k = y_chunk(n, c)
                v.wait_ge(g_done, 4 * k + t + 1)
                v.wait_ge(g_free, 4 * gate_chunk(n, c) + t + 1)
                if n == 0:
                    nc.vector.tensor_tensor(mixed[:, dt, :], G[t][:, :], gT[:, dt, :], ALU.mult).then_inc(g_free, 1)
                    return
                link(nc.vector.tensor_tensor(ytmp[:, :], G[t][:, :], gT[:, dt, :], ALU.mult))
                if n == 1:
                    nc.vector.tensor_tensor(mixed[:, dt, :], mixed[:, dt, :], ytmp[:, :], ALU.add).then_inc(g_free, 1)
                    v.wait_ge(g_free, 4 * k + t + 1)
                    return
                link(nc.vector.tensor_tensor(mixed[:, dt, :], mixed[:, dt, :], ytmp[:, :], ALU.add))
                link(nc.vector.tensor_copy(hT_hi[:, dt, :], mixed[:, dt, :]))
                nc.vector.tensor_tensor(hT_lo[:, dt, :], mixed[:, dt, :], hT_hi[:, dt, :].bitcast(F32),
                                        ALU.subtract).then_inc(g_free, 1)

            def attention(br_):
                groups = dense_groups(br_.dense)
                for s in range(br_.slots):
                    if s < br_.jobs:
                        soft(br_, s)
                    if 0 <= s - br_.lag - 1 < br_.jobs:
                        rows_out(br_, s - br_.lag - 1)
                    if br_.name == "A" and br_.block_scaled(s) is not None:
                        scale_rows(br_.block_scaled(s))
                    if br_.block_turned(s) is not None:
                        turned_lo(br_, br_.block_turned(s))
                    j = s - br_.lag + 1
                    if 0 <= j < br_.jobs:
                        post(br_, j)
                    for g in br_.groups_of(s):
                        kind, n, c, _, t, _, _, last_of_bank, _ = groups[g]
                        if kind == "y" and last_of_bank:
                            branch_out(n, c, t)

            def first_only(flags, n):
                taken = rt[:, 14, :].rearrange("p (t g) -> p t g", g=4)
                link(nc.vector.memset(taken, 0.0))
                link(nc.vector.tensor_copy(taken[:, :, 1:2], flags[:, :, 0:1]))
                link(nc.vector.tensor_tensor(taken[:, :, 2:3], flags[:, :, 0:1], flags[:, :, 1:2], ALU.max))
                link(nc.vector.tensor_tensor(taken[:, :, 3:4], taken[:, :, 2:3], flags[:, :, 2:3], ALU.max))
                link(nc.vector.tensor_tensor(flags, flags, taken, ALU.is_gt))

            def route():
                v.wait_ge(log_done, 1)
                link(nc.vector.tensor_tensor(logit[:, :, :], S[0][:, 0:TT * 20].rearrange("p (t n) -> p t n", t=TT),
                                             br[:, :].unsqueeze(1).broadcast_to([P, TT, 20]), ALU.add))
                four = lambda n: rt[:, n, :].rearrange("p (t g) -> p t g", g=4)
                one = lambda n: rt[:, n, 0:TT]
                wide = lambda n: one(n).unsqueeze(2).broadcast_to([P, TT, 4])
                gl = logit[:, :, 0:4]
                link(nc.vector.tensor_reduce(one(2), gl, AX.X, ALU.max))
                link(nc.vector.tensor_tensor(four(0), gl, wide(2), ALU.subtract))
                link(nc.vector.tensor_tensor(four(3), gl, wide(2), ALU.is_equal))
                first_only(four(3), 4)
                el = logit[:, :, 4:20].rearrange("p t (g e) -> p t e g", g=4)
                link(nc.vector.tensor_tensor(ein[:, :, :, :], el, four(3).unsqueeze(2).broadcast_to([P, TT, 4, 4]),
                                             ALU.mult))
                link(nc.vector.tensor_reduce(four(4), ein[:, :, :, :], AX.X, ALU.add))
                link(nc.vector.tensor_reduce(one(5), four(4), AX.X, ALU.max))
                link(nc.vector.tensor_tensor(four(6), four(4), wide(5), ALU.is_equal))
                first_only(four(6), 4)
                link(nc.vector.scalar_tensor_tensor(four(7), four(6), LOWEST, four(4), ALU.mult, ALU.add))
                link(nc.vector.tensor_reduce(one(8), four(7), AX.X, ALU.max))
                link(nc.vector.tensor_tensor(four(9), four(7), wide(8), ALU.is_equal))
                first_only(four(9), 4)
                link(nc.vector.memset(rt[:, 1, :], 0.0))
                nc.vector.tensor_tensor(rt[:, 1, 0:TT], one(8), one(5), ALU.subtract).then_inc(rexp_in, 1)
                for k, chosen in enumerate((four(6), four(9))):
                    dst = pick[:, k].rearrange("p t (g e) -> p t g e", g=4)
                    last = nc.vector.tensor_tensor(dst, four(3).unsqueeze(3).broadcast_to([P, TT, 4, 4]),
                                                   chosen.unsqueeze(2).broadcast_to([P, TT, 4, 4]), ALU.mult)
                link(last)
                nc.vector.tensor_tensor(both[:, :, :], pick[:, 0], pick[:, 1], ALU.add).then_inc(picked, 1)
                for k in range(2):
                    link(nc.vector.tensor_tensor(prod[:, :, :], pick[:, k],
                                                 eids[:, :].unsqueeze(1).broadcast_to([P, TT, N_EXPERTS]), ALU.mult))
                    link(nc.vector.tensor_reduce(eid[:, k], prod[:, :, :], AX.X, ALU.add))
                v.wait_ge(counted, 1)
                earlier = S[1][:, 0:TT * N_EXPERTS].rearrange("p (t e) -> p t e", t=TT)
                for k in range(2):
                    link(nc.vector.tensor_tensor(prod[:, :, :], pick[:, k], earlier, ALU.mult))
                    link(nc.vector.tensor_reduce(rank[:, k], prod[:, :, :], AX.X, ALU.add))
                link(nc.vector.tensor_scalar(fits[:, :, :], rank[:, :, :], float(CAPACITY), None, ALU.is_lt))
                link(nc.vector.scalar_tensor_tensor(row[:, :, :], rank[:, :, :], float(N_EXPERTS), eid[:, :, :],
                                                    ALU.mult, ALU.add))
                link(nc.vector.tensor_tensor(row[:, :, :], row[:, :, :], spill[:, :, :], ALU.subtract))
                link(nc.vector.tensor_tensor(row[:, :, :], row[:, :, :], fits[:, :, :], ALU.mult))
                link(nc.vector.tensor_tensor(row[:, :, :], row[:, :, :], spill[:, :, :], ALU.add))
                nc.vector.tensor_copy(table_row[:, :, :], row[:, :, :]).then_inc(rows_ready, 1)
                v.wait_ge(rows_ready, 1)
                link(nc.vector.tensor_scalar(left[:, :, :], fits[:, :, :], -1.0, 1.0, ALU.mult, ALU.add))
                for k in range(2):
                    last = nc.vector.tensor_tensor(pick_left[:, k], pick[:, k],
                                                   left[:, k].unsqueeze(2).broadcast_to([P, TT, N_EXPERTS]),
                                                   ALU.mult)
                link(last)
                nc.vector.tensor_reduce(spilled[:, :], pick_left[:, :, :, :].rearrange("p k t e -> p e (k t)"),
                                        AX.X, ALU.add).then_inc(over_summed, 1)
                link(nc.vector.scalar_tensor_tensor(row[:, :, :], eid[:, :, :], float(CAPACITY), rank[:, :, :],
                                                    ALU.mult, ALU.add))
                link(nc.vector.tensor_tensor(row[:, :, :], row[:, :, :], fits[:, :, :], ALU.mult))
                link(nc.vector.tensor_copy(y_row[:, :, :], row[:, :, :]))
                v.wait_ge(over_counted, 1)
                nc.vector.tensor_copy(spilled_int[:, :], S[0][:, 0:N_EXPERTS]).then_inc(over_known, 1)
                v.wait_ge(rexp_out, 1)
                link(nc.vector.tensor_reduce(one(10), four(0), AX.X, ALU.add))
                link(nc.vector.tensor_scalar(one(11), rt[:, 1, 0:TT], 1.0, None, ALU.add))
                link(nc.vector.tensor_tensor(one(12), one(10), one(11), ALU.mult))
                link(nc.vector.reciprocal(one(12), one(12)))
                link(nc.vector.tensor_tensor(one(13), one(12), rt[:, 1, 0:TT], ALU.mult))
                for k in range(2):
                    link(nc.vector.tensor_tensor(weight[:, k], one(12 + k), fits[:, k], ALU.mult))
                    link(nc.vector.tensor_tensor(left[:, k], one(12 + k), weight[:, k], ALU.subtract))

            def left_gates():
                for k in range(2):
                    link(nc.vector.tensor_tensor(pick[:, k], pick[:, k],
                                                 left[:, k].unsqueeze(2).broadcast_to([P, TT, N_EXPERTS]), ALU.mult))
                link(nc.vector.tensor_tensor(gate16[:, :, :].rearrange("p e t -> p t e"), pick[:, 0], pick[:, 1],
                                             ALU.add))

            def et_out(e):
                v.wait_ge(et_turned, 2 * e + 2)
                if e >= 2:
                    v.wait_ge(gu_done, e - 1)
                nc.vector.tensor_copy(et[:, e % 2, 512:1024], S[1][:, :]).then_inc(et_dve, 1)

            def experts():
                et_out(0)
                for e in range(N_EXPERTS + 1):
                    if e < N_EXPERTS:
                        v.wait_ge(silu_done, e + 1)
                        if e >= 2:
                            v.wait_ge(hid_turned, e - 1)
                        nc.vector.tensor_tensor(sq[:, e % 2, FF:2 * FF], sq[:, e % 2, 0:FF], G[e % 2][:, FF:2 * FF],
                                                ALU.mult).then_inc(hid_done, 1)
                    if e + 1 < N_EXPERTS:
                        et_out(e + 1)
                    if e >= 1:
                        v.wait_ge(down_done, 2 * e)
                        if e - 1 >= 4:
                            v.wait_ge(y_out[(e - 1) % 4], 16 * ((e - 1) // 4))
                        nc.vector.tensor_copy(xn[:, (e - 1) % 4, 512:1024], G[3][:, :]).then_inc(y_dve, 1)
                    if e < N_EXPERTS:
                        v.wait_ge(hid_turned, e + 1)
                        if e >= 2:
                            v.wait_ge(down_done, 2 * (e - 1))
                        nc.vector.tensor_copy(pT[:, e % 2, 0:FF], T[e % 2][:, 0:FF]).then_inc(hidT_done, 1)
                for t in range(TT):
                    v.wait_ge(y_back[t % 2], 32 * (t // 2 + 1))
                    for k in range(2):
                        nc.vector.scalar_tensor_tensor(X[:, t, :], xn[:, 2 * (t % 2) + k, :], weight[:, k, t:t + 1],
                                                       X[:, t, :], ALU.mult, ALU.add).then_inc(added, 1)
                        v.wait_ge(added, 2 * t + k + 1)

            for h in range(REL_HEADS):
                v.wait_ge(pre_cp, h + 1)
                last = nc.vector.memset(cqT[0:CHUNK, h % 2, SEQ - CHUNK:SEQ], NEG)
                if A_HEADS <= h < A_HEADS + B_HEADS:
                    last = nc.vector.memset(cqT[CHUNK:P, h % 2, SEQ - 2 * P:SEQ - 2 * P + CHUNK], NEG)
                last.then_inc(pre_set, 1)
            v.wait_ge(pre_half, 2)
            with v.Fori(0, DEPTH) as l:
                links[0] = n_red[0] = n_cms[0] = 0
                v.wait_ge(par_turned, 1)
                nc.vector.tensor_copy(pcol[:, :], G[0][:, 0:N_ROWS]).then_inc(pcol_ready, 1)
                norm_scale(0)
                v.wait_ge(par, 16 * 13)
                v.wait_ge(pcol_ready, 1)
                link(nc.vector.tensor_copy(wr_hi[:, :, :], wr[:, :, :]))
                nc.vector.tensor_tensor(wr_lo[:, :, :], wr[:, :, :], wr_hi[:, :, :].bitcast(F32),
                                        ALU.subtract).then_inc(wr_split, 1)
                for m in range(2):
                    last = nc.vector.tensor_tensor_reduce(sq[:, m, 0:HD], lam_rows[:, 2 * m * HD:(2 * m + 1) * HD],
                                                          lam_rows[:, (2 * m + 1) * HD:(2 * m + 2) * HD], 1.0, 0.0,
                                                          ALU.mult, ALU.add, lam_sum[:, m:m + 1])
                last.then_inc(lam_summed, 1)
                link(nc.vector.tensor_scalar(q_gain[:, :], pcol[:, ROW_QK:ROW_QK + 6:2], HD ** -0.5, None, ALU.mult))
                link(nc.vector.tensor_tensor(sub_gain[:, :], pcol[:, ROW_SUBLN:ROW_SUBLN + 1], lconst[:, 1:2],
                                             ALU.mult))
                v.wait_ge(lam_exped, 1)
                link(nc.vector.tensor_tensor(lam_dif[:, :], lam_exp[:, 1:2], lam_exp[:, 0:1], ALU.subtract))
                nc.vector.tensor_tensor(neg_lam[:, :], lam_dif[:, :], lconst[:, 0:1],
                                        ALU.subtract).then_inc(gains_ready, 1)
                v.wait_ge(gains_ready, 1)
                norm_lo(0, ROW_MIX)
                at = 0
                for c in range(len(P_CHUNKS)):
                    if P_CHUNKS[c][0] != "Av":
                        chunk_stats(c)
                    if c == 1:
                        index_scores()
                    if P_CHUNKS[c][0] != "Av":
                        chunk_scale(c)
                    if c >= 2:
                        n = -(-(len(rounds) - at) // (len(P_CHUNKS) - c))
                        for i, r in rounds[at:at + n]:
                            top_round(i, r)
                        at += n
                for br_ in branches:
                    attention(br_)
                for group in dense_groups([("y", 2)]):
                    if group[7]:
                        branch_out(2, group[2], group[4])
                v.wait_ge(x_back, 16)
                for c in range(2):
                    for t in range(TT):
                        v.wait_ge(g_done, 4 * (OUT_CHUNK + c) + t + 1)
                        rows = X[:, t, c * 512:(c + 1) * 512]
                        nc.vector.tensor_tensor(rows, G[t][:, :], rows, ALU.add).then_inc(g_free, 1)
                v.wait_ge(g_free, 4 * N_CHUNKS)
                v.wait_ge(gain_in, 16)
                norm_scale(1)
                norm_lo(1, None)
                route()
                experts()
                left_gates()
                with v.Fori(0, N_EXPERTS) as e:
                    over = v.value_load(spilled_int[0:1, bass.ds(e, 1)], min_val=0, max_val=SEQ)
                    with v.If(over > 0):
                        meet(v, dense_start)
                        nc.vector.tensor_copy(gate_cur[:, :], gate16[:, bass.ds(e, 1), :].rearrange("p a t -> p (a t)")
                                              ).then_inc(e_dve, 1)
                        for f in range(2):
                            v.wait_ge(e_silu, f + 1)
                            nc.vector.tensor_tensor(ptmp[:, 2 + f, :], ptmp[:, f, :], G[2 + f][:, :],
                                                    ALU.mult).then_inc(e_dve, 1)
                            v.wait_ge(e_dve, 2 + 2 * f)
                            nc.vector.tensor_copy(oT_hi[:, f, :], ptmp[:, 2 + f, :]).then_inc(e_dve, 1)
                            v.wait_ge(e_dve, 3 + 2 * f)
                            nc.vector.tensor_tensor(oT_lo[:, f, :], ptmp[:, 2 + f, :], oT_hi[:, f, :].bitcast(F32),
                                                    ALU.subtract).then_inc(e_hid, 1)
                        for c in range(2):
                            for t in range(TT):
                                v.wait_ge(e_down, TT * c + t + 1)
                                rows = X[:, t, c * 512:(c + 1) * 512]
                                nc.vector.scalar_tensor_tensor(rows, banks[4 + t][:, :], gate_cur[:, t:t + 1], rows,
                                                               ALU.mult, ALU.add).then_inc(e_free, 1)
                        meet(v, expert_end)
                meet(v, layer_end)


def distance_buckets():
    rel = np.arange(SPAN) - (SEQ - 1)
    half = N_BUCKETS // 2
    exact = half // 2
    n = np.abs(rel)
    n_f = np.maximum(n, 1).astype(np.float32)
    large = exact + (np.log(n_f / np.float32(exact)) / np.float32(math.log(MAX_DIST / exact))
                     * np.float32(half - exact)).astype(np.int32)
    large = np.minimum(large, half - 1)
    bucket = np.where(rel > 0, half, 0) + np.where(n < exact, n, large)
    return (bucket[None, :] == np.arange(N_BUCKETS)[:, None]).astype(np.float32)


_INS = ["x", "rel_bias", "norm_mix_g", "w_in", "qk_norm_g", "diff_lambda", "diff_subln_g", "sinks", "w_branch",
        "w_gate", "b_gate", "w_out", "norm_ffn_g", "w_router_group", "b_router_group", "w_router_expert",
        "b_router_expert", "w_ff_gate", "w_ff_up", "w_ff_down"]


def kernel(**inputs):
    import concourse.bacc as bacc
    from concourse.bass_utils import run_bass_kernel_spmd

    nc = bacc.Bacc("TRN2", target_bir_lowering=False, num_devices=1)
    arrays, args = {}, []
    constants = {
        "bucket_onehot": distance_buckets(),
        "identity": np.eye(P, dtype=np.float32),
        "flip": np.ascontiguousarray(np.eye(P, dtype=np.float32)[::-1]),
        "before": np.triu(np.ones((P, P), np.float32), 1),
        "expert_ids": np.tile(np.arange(N_EXPERTS, dtype=np.float32), (P, 1)),
        "token_ids": np.ascontiguousarray(np.arange(SEQ, dtype=np.int32).reshape(TT, P).T),
        "spill_rows": np.ascontiguousarray((N_EXPERTS * CAPACITY + np.arange(2 * SEQ, dtype=np.float32)
                                            ).reshape(2, TT, P).transpose(2, 0, 1)),
        "layer_consts": np.array([[i, 1.0 - i] for i in (0.8 - 0.6 * math.exp(-0.3 * l) for l in range(DEPTH))],
                                 np.float32),
    }
    for name in _INS + list(constants):
        a = np.ascontiguousarray(inputs[name] if name in inputs else constants[name])
        arrays[f"in_{name}"] = a
        args.append(nc.dram_tensor(f"in_{name}", a.shape, mybir.dt.from_np(a.dtype), kind="ExternalInput").ap())
    args.append(nc.dram_tensor("out_rows", (1, SEQ, D_MODEL), F32, kind="ExternalOutput").ap())
    hybrid_block(nc, *args)
    r = run_bass_kernel_spmd(nc, [arrays], core_ids=[0])
    return r.results[0]["out_rows"]
```

```python
import math
from contextlib import ExitStack

import numpy as np

import concourse.bass as bass
from concourse import mybir

F32 = mybir.dt.float32
F32R = mybir.dt.float32r
I32 = mybir.dt.int32
ALU = mybir.AluOpType
ACT = mybir.ActivationFunctionType
AX = mybir.AxisListType

P = 128
D_MODEL, SEQ, DEPTH = 1024, 512, 2
CHUNK, HD = 64, 64
A_HEADS, B_HEADS, B_KV, C_HEADS = 4, 8, 2, 8
IDX_HEADS, IDX_DIM = 4, 32
TOP_K = min(256, SEQ // 4)
N_BUCKETS, MAX_DIST = 32, 1024
REL_HEADS = A_HEADS + B_HEADS + C_HEADS
N_BRANCH, WIDTH = 3, 512
N_GROUPS, PER_GROUP = 4, 4
N_EXPERTS = N_GROUPS * PER_GROUP
FF = 256
EPS = 1e-6
NEG = -1e30
LOWEST = -3e38
TAKEN_BELOW = -2e38

TT = SEQ // P
KT = D_MODEL // P
RAW_SLOTS = 3
UNIT_KT = 2
SPAN = 640
CAPACITY = P
POW_AFTER = (3, 5, 7, 8)
CHUNK_ROUNDS = 4
SPARE = 3
MAX_OVER = 2 * SEQ // (CAPACITY + 1)
RING = 6
PIECES = 3

P_CHUNKS = [("I", 2816, 292), ("Aq", 0, 512), ("Ak", 512, 512), ("Bq", 1536, 512),
            ("Bkv", 2048, 256), ("Cq", 2304, 512), ("Av", 1024, 512)]
UNITS_K = KT // UNIT_KT
T_BLOCKS = {"I": 3, "Aq": 4, "Ak": 4, "Av": 0, "Bq": 4, "Bkv": 2, "Cq": 4}

ROW_MIX, ROW_FFN, ROW_BGATE, ROW_QK, ROW_SUBLN, N_ROWS = 0, 8, 16, 40, 46, 47


class Branch:

    def __init__(self, n, name, heads, lag, per_block, fill, first_head, first_job, first_fill, groups):
        self.n, self.name, self.heads, self.lag, self.per_block = n, name, heads, lag, per_block
        self.fill, self.first_head, self.first_job = fill, first_head, first_job
        self.jobs = heads * TT
        self.blocks = self.jobs // per_block
        self.slots = self.jobs + lag + 3
        self.t_index, self.o_index = {}, {}
        at = first_fill
        for s in range(self.slots):
            if 0 <= s - lag < self.jobs:
                self.t_index[s - lag] = at
                at += 1
            b = self.block_turned(s)
            if b is not None:
                self.o_index[b] = at
                at += 1
        self.end_fill = at
        self.dense = groups

    def block_turned(self, s):
        b, r = divmod(s - self.lag - 3 + 1, self.per_block)
        return b - 1 if r == 0 and 1 <= b <= self.blocks else None

    def block_scaled(self, s):
        b, r = divmod(s - self.lag - 2 + 1, self.per_block)
        return b - 1 if r == 0 and 1 <= b <= self.blocks else None

    def groups_of(self, s):
        total, over = self.fill * self.jobs, self.slots - SPARE
        return range(min(total, total * s // over), min(total, total * (s + 1) // over))

    def job(self, j):
        h, i = divmod(j, TT)
        if self.name == "B":
            tiles = [i - 1, i] if i else [0]
        else:
            tiles = list(range(i + 1))
        nk = P * len(tiles)
        return h, i, SEQ - nk, nk, tiles


def bias_start(h):
    return SEQ - 2 * P if A_HEADS <= h < A_HEADS + B_HEADS else 0


def gate_chunk(n, c):
    return len(P_CHUNKS) + 4 * n + c


def y_chunk(n, c):
    return len(P_CHUNKS) + 4 * n + 2 + c


OUT_CHUNK = len(P_CHUNKS) + 4 * N_BRANCH
N_CHUNKS = OUT_CHUNK + 2
GATE_GROUPS = 2 * 4 * KT
Y_GROUPS = 2 * 4 * (WIDTH // P)
P_FILLS = sum(T_BLOCKS.values())


def make_branches():
    a = Branch(0, "A", A_HEADS, 1, TT, 4, 0, 0, P_FILLS, [("gate", 0)])
    b = Branch(1, "B", B_HEADS, 3, 2 * TT, 3, A_HEADS, a.jobs, a.end_fill, [("y", 0), ("gate", 1)])
    c = Branch(2, "C", C_HEADS, 3, 2 * TT, 3, A_HEADS + B_HEADS, a.jobs + b.jobs, b.end_fill,
               [("y", 1), ("gate", 2)])
    return [a, b, c]


def dense_groups(dense):
    out = []
    for kind, n in dense:
        units = UNITS_K if kind == "gate" else WIDTH // P // UNIT_KT
        for c in range(2):
            for u in range(units):
                for t in range(4):
                    for k in range(UNIT_KT):
                        out.append((kind, n, c, u, t, k, u == 0 and k == 0,
                                    u == units - 1 and k == UNIT_KT - 1, t == 3 and k == UNIT_KT - 1))
    return out


def unit_list():
    out = [("in", i, u) for i in range(len(P_CHUNKS)) for u in range(UNITS_K)]
    for n in range(N_BRANCH):
        out += [("gate", n, c, u) for c in range(2) for u in range(UNITS_K)]
        out += [("y", n, c, u) for c in range(2) for u in range(WIDTH // P // UNIT_KT)]
    out += [("out", c, u) for c in range(2) for u in range(UNITS_K)]
    return out


def hybrid_block(nc, x, rel_bias, norm_mix_g, w_in, qk_norm_g, diff_lambda, diff_subln_g, sinks, w_branch,
                 w_gate, b_gate, w_out, norm_ffn_g, w_router_group, b_router_group, w_router_expert,
                 b_router_expert, w_ff_gate, w_ff_up, w_ff_down, bucket_onehot, identity, flip, before,
                 expert_ids, token_ids, slot_ids, layer_consts, out):
    units = unit_list()
    unit_at = {u: n for n, u in enumerate(units)}
    branches = make_branches()
    n_jobs = sum(b.jobs for b in branches)
    ctx = ExitStack()

    def sb(name, shape, dt=F32):
        return ctx.enter_context(nc.sbuf_tensor(name, shape, dt))

    def sem(name):
        return ctx.enter_context(nc.semaphore(name))

    with ctx:
        X = sb("X", [P, TT, D_MODEL])
        gT = X[:, :, :].rearrange("p t (a n) -> p (t a) n", a=2)
        hT_hi = sb("hT_hi", [P, KT, SEQ], F32R)
        hT_lo = sb("hT_lo", [P, KT, SEQ], F32R)
        raw = sb("raw", [P, RAW_SLOTS, UNIT_KT, 512])
        w_hi = sb("w_hi", [P, 2, UNIT_KT, 512], F32R)
        w_lo = sb("w_lo", [P, 2, UNIT_KT, 512], F32R)
        ptmp = sb("ptmp", [P, TT, 512])
        sq = sb("sq", [P, 2, 512])
        work = sb("work", [P, RING, 4, SEQ])
        aqT, akT, bqT, cqT, av = (work[:, i] for i in range(5))
        bkT, ckT, iqT = work[:, 5, 0:2], work[:, 5, 2], work[:, 5, 3]
        ikT = sb("ikT", [P, SEQ])
        bv = sb("bv", [P, TT, B_KV * HD])
        cv = sb("cv", [P, TT, HD])
        iw = sb("iw", [P, TT, IDX_HEADS])
        bias = sb("bias", [P, 2, SEQ])
        score = sb("score", [P, P * (2 + 3 + 4)])
        top8 = sb("top8", [P, 8])
        mixed = sb("mixed", [P, KT, SEQ])
        xn = mixed[:, :, :].rearrange("p (t a) n -> p t (a n)", a=2)
        ytmp = sb("ytmp", [P, SEQ])
        bias_sel = ytmp
        oT_hi = sb("oT_hi", [P, 4, SEQ], F32R)
        oT_lo = sb("oT_lo", [P, 4, SEQ], F32R)
        o_rows = sb("o_rows", [P, 2, TT, P])
        probs = sb("probs", [P, 4, SEQ])
        pT = sb("pT", [P, 2, SEQ])
        ident = sb("ident", [P, P])
        prow = sb("prow", [N_ROWS, P])
        pcol = sb("pcol", [P, N_ROWS])
        q_gain = sb("q_gain", [P, N_BRANCH])
        sub_gain = sb("sub_gain", [P, 1])
        lam_rows = sb("lam_rows", [P, 4 * HD])
        lam_sum = sb("lam_sum", [P, 2])
        lam_exp = sb("lam_exp", [P, 2])
        lam_dif = sb("lam_dif", [P, 1])
        neg_lam = sb("neg_lam", [P, 1])
        lconst = sb("lconst", [P, 2])
        sink_row = sb("sink_row", [P, B_HEADS])
        half_neg = sb("half_neg", [P, 32])
        row_ss = sb("row_ss", [P, 2, TT])
        row_ms = sb("row_ms", [P, 2, TT])
        row_rs = sb("row_rs", [P, 2, TT])
        head_ss = sb("head_ss", [P, 2, 32])
        head_ms = sb("head_ms", [P, 2, 32])
        head_rs = sb("head_rs", [P, 2, 32])
        o_ss = sb("o_ss", [P, 2, TT])
        o_ms = sb("o_ms", [P, 2, TT])
        o_rs = sb("o_rs", [P, 2, TT])
        job_max = sb("job_max", [P, 4, 2])
        job_neg = sb("job_neg", [P, 4, 2])
        job_sum = sb("job_sum", [P, 4, 2])
        job_sink = sb("job_sink", [P, 4])
        job_den = sb("job_den", [P, 4])
        job_inv = sb("job_inv", [P, 4, 2])
        job_mix = sb("job_mix", [P, 4])
        wr = sb("wr", [P, KT, 20])
        wr_hi = sb("wr_hi", [P, KT, 20], F32R)
        wr_lo = sb("wr_lo", [P, KT, 20], F32R)
        br = sb("br", [P, 20])
        gate_cur = sb("gate_cur", [P, TT])
        rt = score[:, 0:256].rearrange("p (a n) -> p a n", a=16)
        logit = score[:, 256:336].rearrange("p (t n) -> p t n", t=TT)
        ein = score[:, 336:400].rearrange("p (t g e) -> p t g e", t=TT, g=4)
        gate16 = score[:, 400:464].rearrange("p (e t) -> p e t", t=TT)
        pick = score[:, 464:592].rearrange("p (k t e) -> p k t e", k=2, t=TT)
        both = score[:, 592:656].rearrange("p (t e) -> p t e", t=TT)
        pick_left = score[:, 720:848].rearrange("p (k t e) -> p k t e", k=2, t=TT)
        pick_token = score[:, 848:976].rearrange("p (k t e) -> p k t e", k=2, t=TT)
        prod = score[:, 656:720].rearrange("p (t e) -> p t e", t=TT)
        upper = sb("upper", [P, P])
        ones = sb("ones", [P, P])
        eids = sb("eids", [P, N_EXPERTS])
        eids_up = sb("eids_up", [P, N_EXPERTS])
        tokens = sb("tokens", [P, TT])
        falling = sb("falling", [P, 4])
        rank = sb("rank", [P, 2, TT])
        eid = sb("eid", [P, 2, TT])
        fits = sb("fits", [P, 2, TT])
        row = sb("row", [P, 2, TT])
        y_row = sb("y_row", [P, 2, TT], I32)
        weight = sb("weight", [P, 2, TT])
        left = sb("left", [P, 2, TT])
        spilled = sb("spilled", [P, N_EXPERTS])
        over_list = sb("over_list", [P, 8], I32)
        over_expert = sb("over_expert", [P, 8], I32)
        slot_token = sb("slot_token", [P, N_EXPERTS], I32)

        gather_rows = probs[:, :, :].rearrange("p (b a) n -> p b (a n)", b=2)
        et = ptmp[:, :, :].rearrange("p (b a) n -> p b (a n)", b=2)
        gather_back = [xn[:, t, :] for t in range(TT)] + [gather_rows[:, 0, :], gather_rows[:, 1, :],
                                                          et[:, 0, :], et[:, 1, :]]
        slot_id = o_rows[:, 0, 0, :]
        slot_onehot = sq[:, :, :].rearrange("p a (t s) -> p a t s", s=CAPACITY)
        gain_row = bias[:, :, :].rearrange("p a n -> p (a n)")

        banks = [ctx.enter_context(nc.psum_tensor(f"bank{i}", [P, 512], F32)) for i in range(8)]
        G = banks[0:4]
        S = banks[4:6]
        T = banks[6:8]
        O = banks[7]

        xs = nc.dram_tensor("residual_dram", (SEQ, D_MODEL), F32, kind="Internal").ap()
        toep = nc.dram_tensor("toeplitz_dram", (REL_HEADS, SPAN), F32, kind="Internal").ap()
        bias_dram = nc.dram_tensor("bias_dram", (REL_HEADS, P, SEQ), F32, kind="Internal").ap()

        xn_dram = nc.dram_tensor("normed_dram", (SEQ, D_MODEL), F32, kind="Internal").ap()
        y_dram = nc.dram_tensor("expert_rows_dram", (N_EXPERTS * CAPACITY, D_MODEL), F32, kind="Internal").ap()

        pre_x = sem("pre_x")
        pre_c = sem("pre_c")
        pre_b = sem("pre_b")
        pre_mm = sem("pre_mm")
        pre_row = sem("pre_row")
        pre_toep = sem("pre_toep")
        pre_in = [sem(f"pre_in{i}") for i in range(4)]
        pre_flip = sem("pre_flip")
        pre_cp = sem("pre_cp")
        pre_set = sem("pre_set")
        pre_out = [sem(f"pre_out{i}") for i in range(4)]
        pre_half = sem("pre_half")
        pre_eids = sem("pre_eids")
        par = sem("par")
        row_par = sem("row_par")
        x_kept = sem("x_kept")
        raw_in = [sem(f"raw_in{i}") for i in range(RAW_SLOTS)]
        split_hi = sem("split_hi")
        split_done = sem("split_done")
        unit_used = sem("unit_used")
        par_turned = sem("par_turned")
        pcol_ready = sem("pcol_ready")
        lam_summed = sem("lam_summed")
        lam_exped = sem("lam_exped")
        gains_ready = sem("gains_ready")
        ss_act = sem("ss_act")
        ss_dve = sem("ss_dve")
        ms_done = sem("ms_done")
        rs_done = sem("rs_done")
        xn_done = sem("xn_done")
        nt_done = sem("nt_done")
        nhi_done = sem("nhi_done")
        nlo_done = sem("nlo_done")
        g_done = sem("g_done")
        g_free = sem("g_free")
        chunk_copied = sem("chunk_copied")
        squared = sem("squared")
        reduced = sem("reduced")
        cms_done = sem("cms_done")
        crs_done = sem("crs_done")
        chunk_normed = sem("chunk_normed")
        t_done = sem("t_done")
        t_free = sem("t_free")
        idx_done = sem("idx_done")
        relu_done = sem("relu_done")
        relu_used = sem("relu_used")
        s_done = sem("s_done")
        soft_done = sem("soft_done")
        exp_done = sem("exp_done")
        p_ready = sem("p_ready")
        pv_done = sem("pv_done")
        o_free = sem("o_free")
        oms_done = sem("oms_done")
        ors_done = sem("ors_done")
        o_scaled = sem("o_scaled")
        ohi_done = sem("ohi_done")
        bias_in = [sem("bias_in0"), sem("bias_in1")]
        x_back = sem("x_back")
        dve = sem("dve")
        wrhi_done = sem("wrhi_done")
        wr_split = sem("wr_split")
        log_done = sem("log_done")
        logT_done = sem("logT_done")
        logT_copied = sem("logT_copied")
        rexp_in = sem("rexp_in")
        rexp_out = sem("rexp_out")
        gain_in = sem("gain_in")
        xn_out = sem("xn_out")
        picked = sem("picked")
        counted = sem("counted")
        over_summed = sem("over_summed")
        over_counted = sem("over_counted")
        onehot_ready = sem("onehot_ready")
        over_known = sem("over_known")
        slots_in = sem("slots_in")
        slots_counted = sem("slots_counted")
        slots_known = sem("slots_known")
        piece_in = [sem(f"piece_in{i}") for i in range(RING)]
        first_half = sem("first_half")
        gathered = [sem("gathered0"), sem("gathered1")]
        et_turned = sem("et_turned")
        et_act = sem("et_act")
        et_dve = sem("et_dve")
        gu_done = sem("gu_done")
        silu_done = sem("silu_done")
        hid_done = sem("hid_done")
        hid_turned = sem("hid_turned")
        hidT_done = sem("hidT_done")
        down_done = sem("down_done")
        y_act = sem("y_act")
        y_dve = sem("y_dve")
        y_out = [sem(f"y_out{i}") for i in range(4)]
        y_back = [sem(f"y_back{t}") for t in range(TT)]
        added = sem("added")
        early_sems = [par, row_par, x_kept, *raw_in, split_hi, split_done, unit_used, par_turned, pcol_ready,
                      lam_summed, lam_exped, gains_ready, ss_act, ss_dve, ms_done, rs_done, xn_done, nt_done,
                      nhi_done, nlo_done, g_done, g_free, chunk_copied, squared, reduced, cms_done, crs_done,
                      chunk_normed, t_done, t_free, idx_done, relu_done, relu_used, s_done, soft_done, exp_done,
                      p_ready, pv_done, o_free, oms_done, ors_done, o_scaled, ohi_done, *bias_in, x_back, wrhi_done,
                      wr_split, log_done, logT_done, logT_copied, gain_in, xn_out, picked, counted, onehot_ready,
                      slots_in, slots_counted, slots_known]
        late_sems = [dve, rexp_in, rexp_out, over_summed, over_counted, over_known, *piece_in, first_half, *gathered,
                     et_turned, et_act, et_dve, gu_done, silu_done, hid_done, hid_turned, hidT_done, down_done, y_act,
                     y_dve, *y_out, *y_back, added]
        e_raw = [sem(f"e_raw{i}") for i in range(RAW_SLOTS)]
        e_hi = sem("e_hi")
        e_split = sem("e_split")
        e_used = sem("e_used")
        e_gu = sem("e_gu")
        e_silu = sem("e_silu")
        e_dve = sem("e_dve")
        e_hid = sem("e_hid")
        e_down = sem("e_down")
        e_free = sem("e_free")
        expert_sems = [*e_raw, e_hi, e_split, e_used, e_gu, e_silu, e_dve, e_hid, e_down, e_free]
        expert_end = [sem("expert_done"), sem("expert_go"), sem("expert_ack")]
        layer_end = [sem("layer_done"), sem("layer_go"), sem("layer_ack")]

        def meet_and_clear(sp, point, sems):
            meet_done, meet_go, meet_ack = point
            sp.wait_ge(meet_done, 4)
            for s in sems:
                sp.sem_clear(s)
            sp.sem_clear(meet_done)
            sp.sem_inc(meet_go, 1)
            sp.wait_ge(meet_ack, 4)
            sp.sem_clear(meet_go)
            sp.sem_clear(meet_ack)

        def meet(eng, point):
            meet_done, meet_go, meet_ack = point
            eng.drain()
            eng.sem_inc(meet_done, 1)
            eng.wait_ge(meet_go, 1)
            eng.sem_inc(meet_ack, 1)

        def layer_of(w, l):
            return w[bass.ds(l, 1)]

        def unit_source(unit, l):
            kind = unit[0]
            if kind == "in":
                _, c0, w = P_CHUNKS[unit[1]]
                src, u = layer_of(w_in, l)[:, :, c0:c0 + w], unit[2]
            elif kind == "gate":
                _, n, c, u = unit
                c0 = n * D_MODEL + c * 512
                src = layer_of(w_gate, l)[:, :, c0:c0 + 512]
            elif kind == "y":
                _, n, c, u = unit
                src = w_branch.rearrange("l n w d -> (l n) w d")[bass.ds(l * N_BRANCH + n, 1), :, c * 512:c * 512 + 512]
            else:
                _, c, u = unit
                src = layer_of(w_out, l)[:, :, c * 512:c * 512 + 512]
            src = src[:, u * UNIT_KT * P:(u + 1) * UNIT_KT * P, :]
            return src.rearrange("a (k p) n -> p (a k) n", p=P)

        chunk_names = list(dict.fromkeys(u[:-1] for u in units))

        def unit_end(n):
            k = chunk_names.index(units[n][:-1])
            if n + 1 == len(units) or units[n + 1][:-1] != units[n][:-1]:
                return True, 4 * (k + 1)
            return False, n + 1 - k

        E_UNITS = [("gu", u) for u in range(UNITS_K)] + [("down", c) for c in range(2)]

        def expert_raw_value(n):
            return sum(32 if E_UNITS[m][0] == "gu" else 16 for m in range(n % RAW_SLOTS, n + 1, RAW_SLOTS))

        block = ctx.enter_context(nc.Block())

        @block.sync
        def _(sp):
            sp.dma_start(probs[0:N_BUCKETS, 1, 0:REL_HEADS], rel_bias).then_inc(pre_b, 16)
            sp.dma_start(aqT[0:N_BUCKETS, 0:2, 0:SPAN // 2],
                         bucket_onehot.rearrange("b (a n) -> b a n", a=2)).then_inc(pre_b, 16)
            for dst, src in ((probs[:, 0, 0:P], flip), (ident[:, :], identity), (upper[:, :], before),
                             (eids[:, :], expert_ids), (tokens[:, :], token_ids)):
                sp.dma_start(dst, src).then_inc(pre_c, 16)
            sp.wait_ge(pre_row, 2)
            sp.dma_start(toep.rearrange("h (a n) -> h a n", a=2),
                         akT[0:REL_HEADS, 0:2, 0:SPAN // 2]).then_inc(pre_toep, 16)
            sp.wait_ge(pre_toep, 16)
            for h in range(REL_HEADS + 3):
                if h == 4:
                    sp.dma_start(X[:, :, :], x.rearrange("b (t p) d -> p (b t) d", p=P)).then_inc(pre_x, 16)
                if h < REL_HEADS:
                    if h >= 4:
                        sp.wait_ge(pre_flip, h - 3)
                    c0 = bias_start(h)
                    row = toep[h:h + 1, c0:SEQ]
                    shifted = bass.AP(row.tensor, row.offset, [[1, P], [1, SEQ - c0]])
                    sp.dma_start(bqT[:, h % 4, c0:SEQ], shifted).then_inc(pre_in[h % 4], 16)
                if h >= 3:
                    sp.wait_ge(pre_set, h - 2)
                    c0 = bias_start(h - 3)
                    sp.dma_start(bias_dram[h - 3, :, c0:SEQ],
                                 cqT[:, (h - 3) % 4, c0:SEQ]).then_inc(pre_out[(h - 3) % 4], 16)
            sp.wait_ge(pre_c, 16 * 5)
            sp.wait_ge(pre_x, 16)
            sp.sem_inc(pre_half, 1)
            with sp.Fori(0, DEPTH) as l:
                sp.dma_start(prow[ROW_MIX:ROW_MIX + 8, :],
                             layer_of(norm_mix_g, l).rearrange("a (r c) -> (a r) c", c=P)).then_inc(par, 16)
                sp.dma_start(prow[ROW_FFN:ROW_FFN + 8, :],
                             layer_of(norm_ffn_g, l).rearrange("a (r c) -> (a r) c", c=P)).then_inc(par, 16)
                sp.dma_start(prow[ROW_BGATE:ROW_BGATE + 24, :],
                             layer_of(b_gate, l).rearrange("a (r c) -> (a r) c", c=P)).then_inc(par, 16)
                for half in range(2):
                    sp.dma_start(prow[ROW_QK:ROW_QK + 6, half * HD:(half + 1) * HD],
                                 layer_of(qk_norm_g, l).rearrange("a n b d -> (a n b) d")).then_inc(par, 16)
                sp.dma_start(prow[ROW_SUBLN:ROW_SUBLN + 1, :], layer_of(diff_subln_g, l)).then_inc(par, 16)
                for unit in range(RAW_SLOTS):
                    w = P_CHUNKS[units[unit][1]][2]
                    sp.dma_start(raw[:, unit, :, 0:w], unit_source(units[unit], l)).then_inc(raw_in[unit], 16)
                sp.dma_start(lam_rows[:, :],
                             layer_of(diff_lambda, l).rearrange("a r d -> a (r d)").broadcast_to([P, 4 * HD])
                             ).then_inc(row_par, 16)
                sp.dma_start(sink_row[:, :], layer_of(sinks, l).broadcast_to([P, B_HEADS])).then_inc(row_par, 16)
                sp.dma_start(lconst[:, :], layer_of(layer_consts, l).broadcast_to([P, 2])).then_inc(row_par, 16)
                sp.dma_start(br[:, 0:4], layer_of(b_router_group, l).broadcast_to([P, 4])).then_inc(row_par, 16)
                sp.dma_start(br[:, 4:20], layer_of(b_router_expert, l).broadcast_to([P, 16])).then_inc(row_par, 16)
                sp.dma_start(wr[:, :, 0:4],
                             layer_of(w_router_group, l).rearrange("a (k p) n -> p (a k) n", p=P)).then_inc(row_par, 16)
                sp.dma_start(wr[:, :, 4:20],
                             layer_of(w_router_expert, l).rearrange("a (k p) n -> p (a k) n", p=P)).then_inc(row_par, 16)
                sp.dma_start(xs.rearrange("(t p) d -> p t d", p=P), X[:, :, :]).then_inc(x_kept, 16)
                for n in range(RAW_SLOTS, len(units)):
                    w = P_CHUNKS[units[n][1]][2] if units[n][0] == "in" else 512
                    sp.wait_ge(split_done, n - RAW_SLOTS + 1)
                    sp.dma_start(raw[:, n % RAW_SLOTS, :, 0:w],
                                 unit_source(units[n], l)).then_inc(raw_in[n % RAW_SLOTS], 16)
                for n in range(PIECES * N_EXPERTS):
                    e, part = divmod(n, PIECES)
                    if n == 0:
                        sp.wait_ge(pv_done, n_jobs)
                    if n >= RING:
                        used, per = ((first_half, 1), (gu_done, 1), (down_done, 2))[(n - RING) % PIECES]
                        sp.wait_ge(used, per * ((n - RING) // PIECES + 1))
                    slot = n % RING
                    if part < 2:
                        for half, w in enumerate((w_ff_gate, w_ff_up)):
                            src = layer_of(w, l)[:, e, part * 512:(part + 1) * 512, :]
                            sp.dma_start(work[:, slot, :, half * FF:(half + 1) * FF],
                                         src.rearrange("a (k p) n -> p (a k) n", p=P)).then_inc(piece_in[slot], 16)
                    else:
                        sp.dma_start(work[:, slot].rearrange("p (k c) n -> p k (c n)", k=2),
                                     layer_of(w_ff_down, l)[:, e].rearrange("a (k p) n -> p (a k) n", p=P)
                                     ).then_inc(piece_in[slot], 16)
                sp.wait_ge(down_done, 2 * 2)
                for s in early_sems:
                    sp.sem_clear(s)
                sp.wait_ge(over_known, 1)
                any_over = sp.value_load(over_list[0:1, 0:1], min_val=0, max_val=N_EXPERTS)
                with sp.If(any_over > 0):
                    with sp.Fori(0, MAX_OVER) as i:
                        over = sp.value_load(over_list[0:1, bass.ds(i, 1)], min_val=0, max_val=N_EXPERTS)
                        with sp.If(over > 0):
                            e = sp.value_load(over_expert[0:1, bass.ds(i, 1)], min_val=0, max_val=N_EXPERTS - 1)
                            le = l * N_EXPERTS + e
                            for n, (kind, u) in enumerate(E_UNITS):
                                if n >= RAW_SLOTS:
                                    sp.wait_ge(e_split, n - RAW_SLOTS + 1)
                                dst = raw[:, n % RAW_SLOTS]
                                if kind == "gu":
                                    for half, w in enumerate((w_ff_gate, w_ff_up)):
                                        src = w.rearrange("l e d f -> (l e) d f")[bass.ds(le, 1),
                                                                                  u * UNIT_KT * P:(u + 1) * UNIT_KT * P, :]
                                        sp.dma_start(dst[:, :, half * FF:(half + 1) * FF],
                                                     src.rearrange("a (k p) n -> p (a k) n", p=P)
                                                     ).then_inc(e_raw[n % RAW_SLOTS], 16)
                                else:
                                    src = w_ff_down.rearrange("l e f d -> (l e) f d")[bass.ds(le, 1), :, u * 512:u * 512 + 512]
                                    sp.dma_start(dst, src.rearrange("a (k p) n -> p (a k) n", p=P)
                                                 ).then_inc(e_raw[n % RAW_SLOTS], 16)
                            meet_and_clear(sp, expert_end, expert_sems)
                meet_and_clear(sp, layer_end, late_sems)
            sp.dma_start(out.rearrange("b (t p) d -> p (b t) d", p=P), X[:, :, :]).then_inc(pre_x, 16)
            sp.wait_ge(pre_x, 32)

        @block.gpsimd
        def _(pool):
            nc.gpsimd.memset(ones[:, :], 1.0)
            nc.gpsimd.memset(half_neg[:, :], -0.5).then_inc(pre_half, 1)

            def pow_step(dst, src, n):
                return nc.gpsimd.tensor_tensor(dst, src, half_neg[:, 0:n], ALU.pow)

            def split(n):
                w = P_CHUNKS[units[n][1]][2] if units[n][0] == "in" else 512
                slot, two = n % RAW_SLOTS, n % 2
                pool.wait_ge(raw_in[slot], 16 * (n // RAW_SLOTS + 1))
                if n >= 2:
                    last_of_chunk, value = unit_end(n - 2)
                    pool.wait_ge(g_done if last_of_chunk else unit_used, value)
                nc.gpsimd.tensor_scalar(w_hi[:, two, :, 0:w], raw[:, slot, :, 0:w], 1.0, 0.0,
                                        ALU.mult, ALU.add).then_inc(split_hi, 1)
                pool.wait_ge(split_hi, n + 1)
                nc.gpsimd.tensor_tensor(w_lo[:, two, :, 0:w], raw[:, slot, :, 0:w],
                                        w_hi[:, two, :, 0:w].bitcast(F32), ALU.subtract).then_inc(split_done, 1)

            pool.wait_ge(pre_half, 2)
            normed = [i for i, (name, _, _) in enumerate(P_CHUNKS) if name != "Av"]
            with pool.Fori(0, DEPTH) as l:
                pool.wait_ge(ms_done, 1)
                pow_step(row_rs[:, 0, :], row_ms[:, 0, :], TT).then_inc(rs_done, 1)
                split(0)
                split(1)
                n_gate0 = unit_at[("gate", 0, 0, 0)]
                powed = 0
                for n in range(2, len(units)):
                    split(n)
                    if n < n_gate0 + 4 and n % UNITS_K == 1 and n // UNITS_K - 1 in normed:
                        c = n // UNITS_K - 1
                        w = 8 * TT if P_CHUNKS[c][0] in ("Aq", "Ak", "Bq", "Cq") else 2 * TT
                        if P_CHUNKS[c][0] == "I":
                            w = TT
                        pool.wait_ge(cms_done, normed.index(c) + 1)
                        pow_step(head_rs[:, c % 2, 0:w], head_ms[:, c % 2, 0:w], w).then_inc(crs_done, 1)
                    for b in range(4):
                        if n == n_gate0 + POW_AFTER[b]:
                            pool.wait_ge(oms_done, b + 1)
                            pow_step(o_rs[:, b % 2, :], o_ms[:, b % 2, :], TT).then_inc(ors_done, 1)
                pool.wait_ge(ms_done, 2)
                pow_step(row_rs[:, 1, :], row_ms[:, 1, :], TT).then_inc(rs_done, 1)
                pool.wait_ge(slots_known, 1)
                pool.wait_ge(xn_out, 16)
                for e in range(N_EXPERTS):
                    if e >= 2:
                        pool.wait_ge(et_turned, 2 * (e - 1))
                    nc.gpsimd.indirect_dma_start(
                        out=gather_rows[:, e % 2, :], out_offset=None, in_=xn_dram,
                        in_offset=bass.IndirectOffsetOnAxis(ap=slot_token[:, e:e + 1], axis=0)
                    ).then_inc(gathered[e % 2], 16)
                for i in range(4):
                    pool.wait_ge(y_out[i], 16 * N_EXPERTS // 4)
                for t in range(TT):
                    for k in range(2):
                        nc.gpsimd.indirect_dma_start(
                            out=gather_back[2 * t + k], out_offset=None, in_=y_dram,
                            in_offset=bass.IndirectOffsetOnAxis(ap=y_row[:, k, t:t + 1], axis=0)
                        ).then_inc(y_back[t], 16)
                pool.wait_ge(over_known, 1)
                any_over = pool.value_load(over_list[0:1, 0:1], min_val=0, max_val=N_EXPERTS)
                with pool.If(any_over > 0):
                    with pool.Fori(0, MAX_OVER) as i:
                        over = pool.value_load(over_list[0:1, bass.ds(i, 1)], min_val=0, max_val=N_EXPERTS)
                        with pool.If(over > 0):
                            for n in range(len(E_UNITS)):
                                slot, two = n % RAW_SLOTS, n % 2
                                pool.wait_ge(e_raw[slot], expert_raw_value(n))
                                if n >= 2:
                                    pool.wait_ge(e_used, n - 1)
                                nc.gpsimd.tensor_scalar(w_hi[:, two], raw[:, slot], 1.0, 0.0,
                                                        ALU.mult, ALU.add).then_inc(e_hi, 1)
                                pool.wait_ge(e_hi, n + 1)
                                nc.gpsimd.tensor_tensor(w_lo[:, two], raw[:, slot], w_hi[:, two].bitcast(F32),
                                                        ALU.subtract).then_inc(e_split, 1)
                            meet(pool, expert_end)
                pool.drain()
                pool.dma_reset()
                meet(pool, layer_end)

        @block.tensor
        def _(pe):
            def three(out_ap, s_hi, s_lo, m_hi, m_lo, start, stop):
                nc.tensor.matmul(out_ap, s_hi, m_lo, start=start, stop=False)
                nc.tensor.matmul(out_ap, s_lo, m_hi, start=False, stop=False)
                return nc.tensor.matmul(out_ap, s_hi, m_hi, start=False, stop=stop)

            pe.wait_ge(pre_b, 16 * 2)
            for a in range(2):
                nc.tensor.matmul(G[a][0:REL_HEADS, 0:SPAN // 2], probs[0:N_BUCKETS, 1, 0:REL_HEADS],
                                 aqT[0:N_BUCKETS, a, 0:SPAN // 2], start=True, stop=True).then_inc(pre_mm, 1)
            pe.wait_ge(pre_c, 16 * 5)
            for h in range(REL_HEADS):
                pe.wait_ge(pre_in[h % 4], 16 * (h // 4 + 1))
                if h >= 4:
                    pe.wait_ge(pre_cp, h - 3)
                c0 = bias_start(h)
                nc.tensor.matmul(banks[4 + h % 4][:, c0:SEQ], probs[:, 0, 0:P], bqT[:, h % 4, c0:SEQ],
                                 start=True, stop=True).then_inc(pre_flip, 1)

            def norm_turns(which, after=None):
                for dt in range(KT):
                    pe.wait_ge(xn_done, TT * (2 * which + 1 + dt // 4))
                    if dt >= 4:
                        pe.wait_ge(nlo_done, KT * which + dt - 3)
                    for t in range(TT):
                        last = nc.tensor.transpose(G[dt % 4][:, t * P:(t + 1) * P],
                                                   xn[:, t, dt * P:(dt + 1) * P], ident[:, :])
                    last.then_inc(nt_done, 1)
                    if after is not None and dt >= 3:
                        after(dt - 3)
                if after is not None:
                    for kt in range(KT - 3, KT):
                        after(kt)

            def rows_chunk(k, first_unit, width, lhs_hi, lhs_lo, between=None):
                out_banks = banks[4:8] if k == OUT_CHUNK else G
                for u in range(UNITS_K):
                    n = first_unit + u
                    pe.wait_ge(split_done, n + 1)
                    if k == OUT_CHUNK:
                        pe.wait_ge(g_free, 4 * y_chunk(N_BRANCH - 1, 0) + UNIT_KT * (u + 1))
                    for t in range(TT):
                        if between is not None:
                            between(u, t)
                        if u == 0 and k > 0 and k != OUT_CHUNK:
                            pe.wait_ge(g_free, 4 * (k - 1 if k < OUT_CHUNK else k - 2) + t + 1)
                        for kk in range(UNIT_KT):
                            kt = u * UNIT_KT + kk
                            last = three(out_banks[t][:, 0:width], lhs_hi[:, kt, t * P:(t + 1) * P],
                                         lhs_lo[:, kt, t * P:(t + 1) * P], w_hi[:, n % 2, kk, 0:width],
                                         w_lo[:, n % 2, kk, 0:width], kt == 0, kt == KT - 1)
                        if u == UNITS_K - 1 and t < TT - 1:
                            last.then_inc(g_done, 1)
                    if u < UNITS_K - 1:
                        last.then_inc(unit_used, 1)
                last.then_inc(g_done, 1)

            fills = [0]

            def chunk_turns(c):
                name = P_CHUNKS[c][0]
                if T_BLOCKS[name]:
                    pe.wait_ge(chunk_normed, sum(1 for m in range(c + 1) if T_BLOCKS[P_CHUNKS[m][0]]))
                for b in range(T_BLOCKS[name]):
                    n = fills[0]
                    if n >= 2:
                        pe.wait_ge(t_free, n - 1)
                    for t in range(TT):
                        last = nc.tensor.transpose(T[n % 2][:, t * P:(t + 1) * P],
                                                   ptmp[:, t, b * P:(b + 1) * P], ident[:, :])
                    last.then_inc(t_done, 1)
                    fills[0] += 1

            def index_logit(n):
                i, h = 1 + n // IDX_HEADS, n % IDX_HEADS
                if n == 0:
                    pe.wait_ge(t_free, T_BLOCKS["I"])
                if n >= 2:
                    pe.wait_ge(relu_done, n - 1)
                r = slice(IDX_DIM * h, IDX_DIM * (h + 1))
                nc.tensor.matmul(S[n % 2][:, 0:P * (i + 1)], iqT[r, i * P:(i + 1) * P],
                                 ikT[r, 0:P * (i + 1)], start=True, stop=True).then_inc(idx_done, 1)

            def dense_step(group):
                kind, n, c, u, t, kk, first, last_of_bank, last_of_unit = group
                unit = unit_at[(kind, n, c, u)]
                k = gate_chunk(n, c) if kind == "gate" else y_chunk(n, c)
                if t == 0 and kk == 0:
                    pe.wait_ge(split_done, unit + 1)
                    if kind == "y" and c == 0 and u == 0:
                        pe.wait_ge(ohi_done, 2 * 4 * (n + 1))
                if first:
                    pe.wait_ge(g_free, 4 * (k - 1) + t + 1)
                hi, lo = (hT_hi, hT_lo) if kind == "gate" else (oT_hi, oT_lo)
                kt = u * UNIT_KT + kk
                last = three(G[t][:, :], w_hi[:, unit % 2, kk, t * P:(t + 1) * P],
                             w_lo[:, unit % 2, kk, t * P:(t + 1) * P], hi[:, kt, :], lo[:, kt, :], first,
                             last_of_bank)
                if last_of_bank:
                    last.then_inc(g_done, 1)
                elif last_of_unit:
                    last.then_inc(unit_used, 1)

            def scores(br_, j):
                h, i, _, nk, tiles = br_.job(j)
                k0 = tiles[0] * P
                job = br_.first_job + j
                if br_.name == "A":
                    if job:
                        pe.wait_ge(soft_done, job)
                    for m in range(2):
                        r = slice(HD * m, HD * (m + 1))
                        last = nc.tensor.matmul(S[m][:, 0:nk], aqT[r, h, i * P:(i + 1) * P],
                                                akT[r, h, k0:k0 + nk], start=True, stop=True)
                else:
                    pe.wait_ge(soft_done, br_.first_job + max(j - 1, 0))
                    r = slice(HD * (h % 2), HD * (h % 2 + 1))
                    q, k = (bqT, bkT[:, h // (B_HEADS // B_KV), :]) if br_.name == "B" else (cqT, ckT)
                    last = nc.tensor.matmul(S[j % 2][:, 0:nk], q[r, h // 2, i * P:(i + 1) * P],
                                            k[r, k0:k0 + nk], start=True, stop=True)
                last.then_inc(s_done, 1)

            def prob_of(br_, j):
                return probs[:, 2 * (j % 2), :] if br_.name == "A" else probs[:, j % 4, :]

            def turn_probs(br_, j):
                _, _, _, nk, tiles = br_.job(j)
                pe.wait_ge(p_ready, br_.first_job + j + 1)
                pe.wait_ge(t_free, br_.t_index[j])
                for b in range(len(tiles)):
                    last = nc.tensor.transpose(T[0][:, b * P:(b + 1) * P],
                                               prob_of(br_, j)[:, b * P:(b + 1) * P], ident[:, :])
                last.then_inc(t_done, 1)

            def times_values(br_, j):
                h, _, _, _, tiles = br_.job(j)
                job = br_.first_job + j
                pe.wait_ge(t_free, br_.t_index[j] + 1)
                if job:
                    pe.wait_ge(o_free, job)
                for b, kt in enumerate(tiles):
                    if br_.name == "A":
                        v = av[:, kt, h * P:(h + 1) * P]
                    elif br_.name == "B":
                        g = h // (B_HEADS // B_KV)
                        v = bv[:, kt, g * HD:(g + 1) * HD]
                    else:
                        v = cv[:, kt, :]
                    w = v.shape[-1]
                    last = nc.tensor.matmul(O[:, (job % 4) * P:(job % 4) * P + w], pT[:, j % 2, b * P:(b + 1) * P], v,
                                            start=(b == 0), stop=(b == len(tiles) - 1))
                last.then_inc(pv_done, 1)

            def turn_rows(br_, b):
                if br_.name == "A":
                    pe.wait_ge(o_scaled, b + 1)
                else:
                    pe.wait_ge(o_free, br_.first_job + br_.per_block * (b + 1))
                pe.wait_ge(t_free, br_.o_index[b])
                for t in range(TT):
                    last = nc.tensor.transpose(T[0][:, t * P:(t + 1) * P], o_rows[:, b % 2, t, :], ident[:, :])
                last.then_inc(t_done, 1)

            def attention(br_):
                groups = dense_groups(br_.dense)
                for s in range(br_.slots):
                    if s < br_.jobs:
                        scores(br_, s)
                    if 0 <= s - br_.lag < br_.jobs:
                        turn_probs(br_, s - br_.lag)
                    if 0 <= s - br_.lag - 1 < br_.jobs:
                        times_values(br_, s - br_.lag - 1)
                    if br_.block_turned(s) is not None:
                        turn_rows(br_, br_.block_turned(s))
                    for g in br_.groups_of(s):
                        dense_step(groups[g])

            def turn_gathered(e):
                pe.wait_ge(gathered[e % 2], 16 * (e // 2 + 1))
                if e >= 1:
                    pe.wait_ge(et_act, e)
                    pe.wait_ge(et_dve, e)
                for a in range(2):
                    for q in range(4):
                        dt = 4 * a + q
                        last = nc.tensor.transpose(S[a][:, q * P:(q + 1) * P],
                                                   gather_rows[:, e % 2, dt * P:(dt + 1) * P], ident[:, :])
                    last.then_inc(et_turned, 1)

            def gate_up(e):
                pe.wait_ge(et_act, e + 1)
                pe.wait_ge(et_dve, e + 1)
                if e >= 2:
                    pe.wait_ge(hid_done, e - 1)
                for part in range(2):
                    n = PIECES * e + part
                    pe.wait_ge(piece_in[n % RING], 32 * (n // RING + 1))
                    for kk in range(4):
                        kt = 4 * part + kk
                        last = nc.tensor.matmul(G[e % 2][:, :], et[:, e % 2, kt * P:(kt + 1) * P],
                                                work[:, n % RING, kk, :], start=(kt == 0), stop=(kt == KT - 1))
                    last.then_inc(first_half if part == 0 else gu_done, 1)

            def turn_hidden(e):
                pe.wait_ge(hid_done, e + 1)
                if e >= 2:
                    pe.wait_ge(hidT_done, e - 1)
                for f in range(2):
                    last = nc.tensor.transpose(T[e % 2][:, f * P:(f + 1) * P],
                                               sq[:, e % 2, FF + f * P:FF + (f + 1) * P], ident[:, :])
                last.then_inc(hid_turned, 1)

            def down(e):
                n = PIECES * e + 2
                pe.wait_ge(hidT_done, e + 1)
                pe.wait_ge(piece_in[n % RING], 16 * (n // RING + 1))
                w = work[:, n % RING].rearrange("p (k c) n -> p k (c n)", k=2)
                for c in range(2):
                    if e >= 1:
                        pe.wait_ge((y_act, y_dve)[c], e)
                    for f in range(2):
                        last = nc.tensor.matmul(G[2 + c][:, :], pT[:, e % 2, f * P:(f + 1) * P],
                                                w[:, f, c * 512:(c + 1) * 512], start=(f == 0), stop=(f == 1))
                    last.then_inc(down_done, 1)

            pe.wait_ge(pre_half, 2)
            with pe.Fori(0, DEPTH) as l:
                fills[0] = 0
                pe.wait_ge(par, 16 * 6)
                nc.tensor.transpose(T[1][:, 0:N_ROWS], prow[:, :], ident[0:N_ROWS, 0:N_ROWS]).then_inc(par_turned, 1)
                norm_turns(0)
                pe.wait_ge(nlo_done, KT)
                for c in range(len(P_CHUNKS)):
                    def between(u, t, c=c):
                        if c >= 1 and u == 2 and t == 0:
                            chunk_turns(c - 1)
                        if c == 1 and u == 3:
                            index_logit(t)
                        if c == 2 and u < 2:
                            index_logit(4 + 4 * u + t)
                    rows_chunk(c, c * UNITS_K, P_CHUNKS[c][2], hT_hi, hT_lo, between)
                pe.wait_ge(t_free, P_FILLS)
                for br_ in branches:
                    attention(br_)
                for group in dense_groups([("y", 2)]):
                    dense_step(group)
                for c in range(2):
                    rows_chunk(OUT_CHUNK + c, unit_at[("out", c, 0)], 512, hT_hi, hT_lo)
                pe.wait_ge(g_free, 4 * N_CHUNKS)
                pe.wait_ge(wr_split, 1)

                def router_step(kt):
                    pe.wait_ge(nlo_done, KT + kt + 1)
                    last = three(S[0][0:20, :], wr_hi[:, kt, :], wr_lo[:, kt, :], hT_hi[:, kt, :], hT_lo[:, kt, :],
                                 kt == 0, kt == KT - 1)
                    if kt == KT - 1:
                        last.then_inc(logT_done, 1)
                norm_turns(1, router_step)
                pe.wait_ge(logT_copied, 1)
                for t in range(TT):
                    last = nc.tensor.transpose(T[0][:, t * 20:(t + 1) * 20], ytmp[0:20, t * P:(t + 1) * P],
                                               ident[0:20, 0:20])
                last.then_inc(log_done, 1)
                pe.wait_ge(picked, 1)
                for t in range(TT):
                    for u in range(t + 1):
                        last = nc.tensor.matmul(S[1][:, t * N_EXPERTS:(t + 1) * N_EXPERTS],
                                                upper[:, :] if u == t else ones[:, :], both[:, u, :],
                                                start=(u == 0), stop=(u == t))
                last.then_inc(counted, 1)
                pe.wait_ge(onehot_ready, 1)
                for k in range(2):
                    for t in range(TT):
                        last = nc.tensor.matmul(S[0][:, 0:N_EXPERTS], slot_onehot[:, k, t, :], pick_token[:, k, t, :],
                                                start=(k + t == 0), stop=(k == 1 and t == TT - 1))
                last.then_inc(slots_counted, 1)
                pe.wait_ge(slots_known, 1)
                turn_gathered(0)
                for e in range(N_EXPERTS + 1):
                    if e < N_EXPERTS:
                        gate_up(e)
                    if e == 0:
                        pe.wait_ge(over_summed, 1)
                        nc.tensor.matmul(T[1][:, 0:N_EXPERTS], ones[:, :], spilled[:, :], start=True,
                                         stop=True).then_inc(over_counted, 1)
                    if e == 1:
                        pe.wait_ge(over_known, 1)
                    if e + 1 < N_EXPERTS:
                        turn_gathered(e + 1)
                    if e >= 1:
                        down(e - 1)
                    if e < N_EXPERTS:
                        turn_hidden(e)
                pe.wait_ge(y_act, N_EXPERTS)
                pe.wait_ge(y_dve, N_EXPERTS)
                any_over = pe.value_load(over_list[0:1, 0:1], min_val=0, max_val=N_EXPERTS)
                with pe.If(any_over > 0):
                    with pe.Fori(0, MAX_OVER) as i:
                        over = pe.value_load(over_list[0:1, bass.ds(i, 1)], min_val=0, max_val=N_EXPERTS)
                        with pe.If(over > 0):
                            for n in range(UNITS_K):
                                pe.wait_ge(e_split, n + 1)
                                for t in range(4):
                                    for kk in range(UNIT_KT):
                                        kt = n * UNIT_KT + kk
                                        last = three(G[t][:, :], w_hi[:, n % 2, kk, t * P:(t + 1) * P],
                                                     w_lo[:, n % 2, kk, t * P:(t + 1) * P], hT_hi[:, kt, :], hT_lo[:, kt, :],
                                                     kt == 0, kt == KT - 1)
                                last.then_inc(e_used, 1)
                            pe.wait_ge(e_used, UNITS_K)
                            pe.sem_inc(e_gu, 1)
                            pe.wait_ge(e_hid, 2)
                            for c in range(2):
                                n = UNITS_K + c
                                pe.wait_ge(e_split, n + 1)
                                for t in range(TT):
                                    if c == 1:
                                        pe.wait_ge(e_free, t + 1)
                                    for kk in range(FF // P):
                                        last = three(banks[4 + t][:, :], oT_hi[:, kk, t * P:(t + 1) * P],
                                                     oT_lo[:, kk, t * P:(t + 1) * P], w_hi[:, n % 2, kk, :],
                                                     w_lo[:, n % 2, kk, :], kk == 0, kk == FF // P - 1)
                                    last.then_inc(e_down, 1)
                                if c == 0:
                                    pe.wait_ge(e_down, TT)
                                    pe.sem_inc(e_used, 1)
                            meet(pe, expert_end)
                meet(pe, layer_end)

        @block.scalar
        def _(act):
            def norm_rows(which):
                for t in range(2):
                    if which + t:
                        act.wait_ge(ss_act, 2 * which + t)
                    if which:
                        act.wait_ge(g_free, 4 * (N_CHUNKS - 1) + t + 1)
                    nc.scalar.activation(ptmp[:, 0:2, :].rearrange("p a n -> p (a n)"), X[:, t, :], ACT.Square,
                                         accum_out=row_ss[:, which, t:t + 1]).then_inc(ss_act, 1)

            def norm_hi(which, row):
                for dt in range(KT):
                    act.wait_ge(nt_done, KT * which + dt + 1)
                    gain = 1.0 if row is None else pcol[:, row + dt:row + dt + 1]
                    nc.scalar.activation(hT_hi[:, dt, :], G[dt % 4][:, :], ACT.Copy, scale=gain).then_inc(nhi_done, 1)

            n_sq = [0]
            n_copy = [0]
            fills = [0]

            def chunk_out(c):
                name = P_CHUNKS[c][0]
                fills_before = sum(T_BLOCKS[P_CHUNKS[m][0]] for m in range(c))
                for t in range(TT):
                    act.wait_ge(g_done, 4 * c + t + 1)
                    if t == 0 and fills_before and T_BLOCKS[name]:
                        act.wait_ge(t_done, fills_before)
                    ps = G[t]
                    if name == "Av":
                        nc.scalar.activation(av[:, t, :], ps[:, :], ACT.Copy).then_inc(g_free, 1)
                        continue
                    if name == "I":
                        nc.scalar.activation(ptmp[:, t, 384:448], ps[:, 0:64], ACT.Copy)
                        nc.scalar.activation(cv[:, t, :], ps[:, 64:128], ACT.Copy)
                        nc.scalar.activation(ptmp[:, t, 128:256], ps[:, 128:256], ACT.Copy)
                        nc.scalar.activation(ptmp[:, t, 256:384].rearrange("p (r d) -> p r d", r=4),
                                             ps[:, 256:288].unsqueeze(1).broadcast_to([P, 4, IDX_DIM]), ACT.Copy)
                        nc.scalar.activation(iw[:, t, :], ps[:, 288:292], ACT.Copy).then_inc(chunk_copied, 1)
                        w = 64
                    elif name == "Bkv":
                        nc.scalar.activation(bv[:, t, :], ps[:, 128:256], ACT.Copy)
                        nc.scalar.activation(ptmp[:, t, 256:384], ps[:, 0:128], ACT.Copy).then_inc(chunk_copied, 1)
                        w = 128
                    else:
                        nc.scalar.activation(ptmp[:, t, :], ps[:, :], ACT.Copy).then_inc(chunk_copied, 1)
                        w = 512
                    n_copy[0] += 1
                    if n_sq[0] >= 2:
                        act.wait_ge(reduced, n_sq[0] - 1)
                    nc.scalar.activation(sq[:, n_sq[0] % 2, 0:w], ps[:, 0:w], ACT.Square).then_inc(squared, 1)
                    n_sq[0] += 1
                    act.wait_ge(squared, n_sq[0])
                    act.wait_ge(chunk_copied, n_copy[0])
                    act.sem_inc(g_free, 1)

            def turned_out(c):
                name = P_CHUNKS[c][0]
                for b in range(T_BLOCKS[name]):
                    n = fills[0]
                    act.wait_ge(t_done, n + 1)
                    src = T[n % 2][:, :]
                    k_gain = {"A": 1, "B": 3, "C": 5}
                    if name == "I":
                        dst, gain = [(ckT, pcol[:, ROW_QK + 5:ROW_QK + 6]), (iqT, 1.0), (ikT[:, :], 1.0)][b]
                    elif name == "Bkv":
                        dst, gain = bkT[:, b, :], pcol[:, ROW_QK + 3:ROW_QK + 4]
                    elif name == "Ak":
                        dst, gain = akT[:, b, :], pcol[:, ROW_QK + 1:ROW_QK + 2]
                    else:
                        q = "ABC".index(name[0])
                        dst, gain = (aqT, bqT, cqT)[q][:, b, :], q_gain[:, q:q + 1]
                    nc.scalar.activation(dst, src, ACT.Copy, scale=gain).then_inc(t_free, 1)
                    fills[0] += 1

            def index_relu(n):
                nk = P * (2 + n // IDX_HEADS)
                act.wait_ge(idx_done, n + 1)
                if n >= 4:
                    act.wait_ge(relu_used, n - 3)
                nc.scalar.activation(probs[:, n % 4, 0:nk], S[n % 2][:, 0:nk], ACT.Relu).then_inc(relu_done, 1)

            def load_bias(gh):
                c0 = bias_start(gh)
                act.dma_start(bias[:, gh % 2, c0:SEQ], bias_dram[gh, :, c0:SEQ]).then_inc(bias_in[gh % 2], 16)

            def exps(br_, j):
                h, i, _, nk, _ = br_.job(j)
                job = br_.first_job + j
                gh = br_.first_head + h
                act.wait_ge(soft_done, job + 1)
                if i == 0 and 1 <= gh < REL_HEADS - 1:
                    load_bias(gh + 1)
                st = j % 4
                for m in range(2 if br_.name == "A" else 1):
                    p = probs[:, 2 * (j % 2) + m, 0:nk] if br_.name == "A" else probs[:, j % 4, 0:nk]
                    last = nc.scalar.activation(p, p, ACT.Exp, bias=job_neg[:, st, m:m + 1],
                                                accum_out=job_sum[:, st, m:m + 1])
                if br_.name == "B":
                    last = nc.scalar.activation(job_sink[:, st:st + 1], sink_row[:, h:h + 1], ACT.Exp,
                                                bias=job_neg[:, st, 0:1])
                last.then_inc(exp_done, 1)

            def attention(br_):
                groups = dense_groups(br_.dense)
                for s in range(br_.slots):
                    if s < br_.jobs:
                        exps(br_, s)
                    if 0 <= s - br_.lag < br_.jobs:
                        j = s - br_.lag
                        _, _, _, nk, _ = br_.job(j)
                        act.wait_ge(t_done, br_.t_index[j] + 1)
                        if br_.first_job + j >= 2:
                            act.wait_ge(pv_done, br_.first_job + j - 1)
                        nc.scalar.activation(pT[:, j % 2, 0:nk], T[0][:, 0:nk], ACT.Copy).then_inc(t_free, 1)
                    b = br_.block_turned(s)
                    if b is not None:
                        act.wait_ge(t_done, br_.o_index[b] + 1)
                        if b == 0 and br_.n > 0:
                            act.wait_ge(g_done, 4 * (y_chunk(br_.n - 1, 1) + 1))
                        gain = sub_gain[:, 0:1] if br_.name == "A" else 1.0
                        nc.scalar.activation(oT_hi[:, b, :], T[0][:, :], ACT.Copy, scale=gain).then_inc(ohi_done, 1)
                    for g in br_.groups_of(s):
                        kind, n, c, _, t, _, _, last_of_bank, _ = groups[g]
                        if kind == "gate" and last_of_bank:
                            if n == 0 and c == 0 and t == 0:
                                act.wait_ge(x_kept, 16)
                            act.wait_ge(g_done, 4 * gate_chunk(n, c) + t + 1)
                            row = ROW_BGATE + n * KT + c * 4 + t
                            nc.scalar.activation(gT[:, c * 4 + t, :], G[t][:, :], ACT.Sigmoid,
                                                 bias=pcol[:, row:row + 1]).then_inc(g_free, 1)

            def et_out(e):
                act.wait_ge(et_turned, 2 * e + 1)
                if e >= 2:
                    act.wait_ge(gu_done, e - 1)
                nc.scalar.activation(et[:, e % 2, 0:512], S[0][:, :], ACT.Copy).then_inc(et_act, 1)

            def rows_down(e):
                act.wait_ge(down_done, 2 * e + 1)
                if e >= 4:
                    act.wait_ge(y_out[e % 4], 16 * (e // 4))
                nc.scalar.activation(xn[:, e % 4, 0:512], G[2][:, :], ACT.Copy).then_inc(y_act, 1)
                act.wait_ge(y_act, e + 1)
                act.wait_ge(y_dve, e + 1)
                act.dma_start(y_dram[e * CAPACITY:(e + 1) * CAPACITY, :], xn[:, e % 4, :]).then_inc(y_out[e % 4], 16)

            for a in range(2):
                act.wait_ge(pre_mm, a + 1)
                nc.scalar.activation(akT[0:REL_HEADS, a, 0:SPAN // 2], G[a][0:REL_HEADS, 0:SPAN // 2],
                                     ACT.Copy).then_inc(pre_row, 1)
            for h in range(REL_HEADS):
                act.wait_ge(pre_flip, h + 1)
                if h >= 4:
                    act.wait_ge(pre_out[h % 4], 16 * (h // 4))
                c0 = bias_start(h)
                nc.scalar.activation(cqT[:, h % 4, c0:SEQ], banks[4 + h % 4][:, c0:SEQ],
                                     ACT.Copy).then_inc(pre_cp, 1)
            act.wait_ge(pre_half, 2)
            with act.Fori(0, DEPTH) as l:
                n_sq[0] = n_copy[0] = fills[0] = 0
                norm_rows(0)
                act.wait_ge(par_turned, 1)
                nc.scalar.activation(pcol[:, :], T[1][:, 0:N_ROWS], ACT.Copy).then_inc(pcol_ready, 1)
                for i in range(4):
                    act.wait_ge(pre_out[i], 16 * REL_HEADS // 4)
                load_bias(0)
                load_bias(1)
                act.wait_ge(pcol_ready, 1)
                norm_hi(0, ROW_MIX)
                act.wait_ge(lam_summed, 1)
                nc.scalar.activation(lam_exp[:, :], lam_sum[:, :], ACT.Exp).then_inc(lam_exped, 1)
                act.wait_ge(gains_ready, 1)
                for c in range(len(P_CHUNKS)):
                    if c >= 1:
                        turned_out(c - 1)
                    for n in range(4 if c == 1 else 0):
                        index_relu(n)
                    chunk_out(c)
                    for n in range(4, 12 if c == 1 else 4):
                        index_relu(n)
                for br_ in branches:
                    attention(br_)
                act.wait_ge(g_free, 4 * OUT_CHUNK)
                act.dma_start(gain_row, layer_of(norm_ffn_g, l).broadcast_to([P, D_MODEL])).then_inc(gain_in, 16)
                act.dma_start(slot_id, slot_ids).then_inc(slots_in, 16)
                act.dma_start(X[:, :, :], xs.rearrange("(t p) d -> p t d", p=P)).then_inc(x_back, 16)
                norm_rows(1)
                act.wait_ge(xn_done, 4 * TT)
                act.dma_start(xn_dram.rearrange("(t p) d -> p t d", p=P), xn).then_inc(xn_out, 16)
                norm_hi(1, None)
                et_out(0)
                act.wait_ge(rexp_in, 1)
                nc.scalar.activation(rt[:, 0:2, :], rt[:, 0:2, :], ACT.Exp).then_inc(rexp_out, 1)
                for e in range(N_EXPERTS + 1):
                    if e < N_EXPERTS:
                        act.wait_ge(gu_done, e + 1)
                        if e >= 2:
                            act.wait_ge(hid_done, e - 1)
                        nc.scalar.activation(sq[:, e % 2, 0:FF], G[e % 2][:, 0:FF], ACT.Silu).then_inc(silu_done, 1)
                    if e + 1 < N_EXPERTS:
                        et_out(e + 1)
                    if e >= 1:
                        rows_down(e - 1)
                act.wait_ge(over_known, 1)
                act.wait_ge(added, 2 * TT)
                any_over = act.value_load(over_list[0:1, 0:1], min_val=0, max_val=N_EXPERTS)
                with act.If(any_over > 0):
                    with act.Fori(0, MAX_OVER) as i:
                        over = act.value_load(over_list[0:1, bass.ds(i, 1)], min_val=0, max_val=N_EXPERTS)
                        with act.If(over > 0):
                            act.wait_ge(e_gu, 1)
                            for f in range(2):
                                nc.scalar.activation(ptmp[:, f, :], G[f][:, :], ACT.Silu).then_inc(e_silu, 1)
                            meet(act, expert_end)
                meet(act, layer_end)

        @block.vector
        def _(v):
            links = [0]

            def link(ins):
                links[0] += 1
                ins.then_inc(dve, 1)
                v.wait_ge(dve, links[0])

            def norm_scale(which):
                for t in range(2, TT):
                    if which + t > 2:
                        v.wait_ge(ss_dve, 2 * which + t - 2)
                    nc.vector.tensor_tensor_reduce(ptmp[:, 2:4, :].rearrange("p a n -> p (a n)"), X[:, t, :],
                                                   X[:, t, :], 1.0, 0.0, ALU.mult, ALU.add,
                                                   row_ss[:, which, t:t + 1]).then_inc(ss_dve, 1)
                v.wait_ge(ss_act, 2 * (which + 1))
                v.wait_ge(ss_dve, 2 * (which + 1))
                nc.vector.tensor_scalar(row_ms[:, which, :], row_ss[:, which, :], 1.0 / D_MODEL, EPS, ALU.mult,
                                        ALU.add).then_inc(ms_done, 1)
                v.wait_ge(rs_done, which + 1)
                for c in range(2):
                    for t in range(TT):
                        rows, src = xn[:, t, c * 512:(c + 1) * 512], X[:, t, c * 512:(c + 1) * 512]
                        if which == 0:
                            nc.vector.tensor_scalar(rows, src, row_rs[:, which, t:t + 1], None,
                                                    ALU.mult).then_inc(xn_done, 1)
                        else:
                            nc.vector.scalar_tensor_tensor(rows, src, row_rs[:, which, t:t + 1],
                                                           gain_row[:, c * 512:(c + 1) * 512], ALU.mult,
                                                           ALU.mult).then_inc(xn_done, 1)

            def norm_lo(which, row):
                for dt in range(KT):
                    v.wait_ge(nhi_done, KT * which + dt + 1)
                    gain = 1.0 if row is None else pcol[:, row + dt:row + dt + 1]
                    nc.vector.scalar_tensor_tensor(hT_lo[:, dt, :], G[dt % 4][:, :], gain,
                                                   hT_hi[:, dt, :].bitcast(F32), ALU.mult,
                                                   ALU.subtract).then_inc(nlo_done, 1)

            n_red = [0]
            n_cms = [0]

            def chunk_stats(c):
                name = P_CHUNKS[c][0]
                heads = {"I": 1, "Bkv": 2}.get(name, 8)
                ss = head_ss[:, c % 2, 0:heads * TT].rearrange("p (t g) -> p t g", t=TT)
                for t in range(TT):
                    v.wait_ge(squared, n_red[0] + 1)
                    nc.vector.tensor_reduce(ss[:, t, :],
                                            sq[:, n_red[0] % 2, 0:heads * HD].rearrange("p (g d) -> p g d", d=HD),
                                            AX.X, ALU.add).then_inc(reduced, 1)
                    n_red[0] += 1
                v.wait_ge(reduced, n_red[0])
                nc.vector.tensor_scalar(head_ms[:, c % 2, 0:heads * TT], head_ss[:, c % 2, 0:heads * TT],
                                        1.0 / HD, EPS, ALU.mult, ALU.add).then_inc(cms_done, 1)
                n_cms[0] += 1

            def chunk_scale(c):
                name = P_CHUNKS[c][0]
                heads = {"I": 1, "Bkv": 2}.get(name, 8)
                v.wait_ge(crs_done, n_cms[0])
                v.wait_ge(chunk_copied, TT * n_cms[0])
                rs = head_rs[:, c % 2, 0:heads * TT]
                if heads == 8:
                    rows = ptmp[:, :, :].rearrange("p t (g d) -> p (t g) d", d=HD)
                    nc.vector.tensor_tensor(rows, rows, rs.unsqueeze(2).broadcast_to([P, 8 * TT, HD]),
                                            ALU.mult).then_inc(chunk_normed, 1)
                    return
                scale = rs.rearrange("p (t g) -> p t g", t=TT).unsqueeze(3).broadcast_to([P, TT, heads, HD])
                first = 384 if name == "I" else 256
                rows = ptmp[:, :, first:first + heads * HD].rearrange("p t (g d) -> p t g d", d=HD)
                for twin in range(2):
                    dst = ptmp[:, :, 0:heads * P].rearrange("p t (g r d) -> p t g r d", r=2, d=HD)[:, :, :, twin, :]
                    last = nc.vector.tensor_tensor(dst, rows, scale, ALU.mult)
                last.then_inc(chunk_normed, 1)

            block_at = {1: 0, 2: 2 * P, 3: 5 * P}

            def index_score(i):
                if i == 1:
                    w_scale = IDX_HEADS ** -0.5 * IDX_DIM ** -0.5
                    link(nc.vector.tensor_scalar(iw[:, :, :], iw[:, :, :], w_scale, None, ALU.mult))
                nk = P * (i + 1)
                dst = score[:, block_at[i]:block_at[i] + nk]
                for h in range(IDX_HEADS):
                    n = IDX_HEADS * (i - 1) + h
                    v.wait_ge(relu_done, n + 1)
                    w = iw[:, i, h:h + 1]
                    if h == 0:
                        nc.vector.tensor_scalar(dst, probs[:, n % 4, 0:nk], w, 0.0, ALU.mult,
                                                ALU.add).then_inc(relu_used, 1)
                    else:
                        nc.vector.scalar_tensor_tensor(dst, probs[:, n % 4, 0:nk], w, dst, ALU.mult,
                                                       ALU.add).then_inc(relu_used, 1)
                    v.wait_ge(relu_used, n + 1)
                link(nc.vector.memset(score[0:CHUNK, block_at[i] + nk - CHUNK:block_at[i] + nk], NEG))

            def top_round(i, r):
                nk = P * (i + 1)
                s = score[:, block_at[i]:block_at[i] + nk]
                link(nc.vector.max(top8[:, :], s))
                link(nc.vector.match_replace(s, top8[:, :], s, LOWEST))
                if r == TOP_K // 8 - 1:
                    link(nc.vector.tensor_scalar(s, s, TAKEN_BELOW, NEG, ALU.is_ge, ALU.mult))

            at_round = [0]
            rounds = [(i, r) for i in range(1, TT) for r in range(TOP_K // 8)]

            def soft(br_, j):
                h, i, c0, nk, _ = br_.job(j)
                job, gh, st = br_.first_job + j, br_.first_head + h, j % 4
                tile_bias = bias[:, gh % 2, c0:c0 + nk]
                if i == 0:
                    v.wait_ge(bias_in[gh % 2], 16 * (gh // 2 + 1))
                if br_.name == "C" and i > 0:
                    link(nc.vector.tensor_tensor(bias_sel[:, 0:nk], tile_bias, score[:, block_at[i]:block_at[i] + nk],
                                                 ALU.add))
                    tile_bias = bias_sel[:, 0:nk]
                v.wait_ge(s_done, job + 1)
                if br_.name == "A":
                    if j >= 2:
                        v.wait_ge(t_done, br_.t_index[j - 2] + 1)
                    for m in range(2):
                        last = nc.vector.tensor_tensor_reduce(probs[:, 2 * (j % 2) + m, 0:nk], S[m][:, 0:nk],
                                                              tile_bias, 1.0, LOWEST, ALU.add, ALU.max,
                                                              job_max[:, st, m:m + 1])
                    link(last)
                    nc.vector.tensor_scalar(job_neg[:, st, :], job_max[:, st, :], -1.0, None,
                                            ALU.mult).then_inc(soft_done, 1)
                    return
                if j >= 4:
                    v.wait_ge(t_done, br_.t_index[j - 4] + 1)
                least = sink_row[:, h:h + 1] if br_.name == "B" else LOWEST
                link(nc.vector.tensor_tensor_reduce(probs[:, j % 4, 0:nk], S[j % 2][:, 0:nk], tile_bias, 1.0, least,
                                                    ALU.add, ALU.max, job_max[:, st, 0:1]))
                nc.vector.tensor_scalar(job_neg[:, st, 0:1], job_max[:, st, 0:1], -1.0, None,
                                        ALU.mult).then_inc(soft_done, 1)

            def post(br_, j):
                _, _, _, nk, _ = br_.job(j)
                job, st = br_.first_job + j, j % 4
                v.wait_ge(exp_done, job + 1)
                if br_.name == "A":
                    link(nc.vector.reciprocal(job_inv[:, st, :], job_sum[:, st, :]))
                    link(nc.vector.tensor_scalar(job_mix[:, st:st + 1], job_sum[:, st, 0:1], job_inv[:, st, 1:2],
                                                 neg_lam[:, 0:1], ALU.mult, ALU.mult))
                    nc.vector.scalar_tensor_tensor(probs[:, 2 * (j % 2), 0:nk], probs[:, 2 * (j % 2) + 1, 0:nk],
                                                   job_mix[:, st:st + 1], probs[:, 2 * (j % 2), 0:nk], ALU.mult,
                                                   ALU.add).then_inc(p_ready, 1)
                elif br_.name == "B":
                    link(nc.vector.tensor_tensor(job_den[:, st:st + 1], job_sum[:, st, 0:1], job_sink[:, st:st + 1],
                                                 ALU.add))
                    nc.vector.reciprocal(job_inv[:, st, 0:1], job_den[:, st:st + 1]).then_inc(p_ready, 1)
                else:
                    nc.vector.reciprocal(job_inv[:, st, 0:1], job_sum[:, st, 0:1]).then_inc(p_ready, 1)

            def rows_out(br_, j):
                h, i, _, _, _ = br_.job(j)
                job, st = br_.first_job + j, j % 4
                b = j // br_.per_block
                v.wait_ge(pv_done, job + 1)
                v.wait_ge(p_ready, job + 1)
                if j % br_.per_block == 0 and b >= 2:
                    v.wait_ge(t_done, br_.o_index[b - 2] + 1)
                w = P if br_.name == "A" else HD
                c0 = 0 if br_.name == "A" else HD * (h % 2)
                nc.vector.tensor_scalar(o_rows[:, b % 2, i, c0:c0 + w], O[:, (job % 4) * P:(job % 4) * P + w],
                                        job_inv[:, st, 0:1], None, ALU.mult).then_inc(o_free, 1)
                if br_.name == "A" and i == TT - 1:
                    v.wait_ge(o_free, job + 1)
                    for t in range(TT):
                        last = nc.vector.tensor_tensor_reduce(sq[:, 0, t * P:(t + 1) * P], o_rows[:, b % 2, t, :],
                                                              o_rows[:, b % 2, t, :], 1.0, 0.0, ALU.mult, ALU.add,
                                                              o_ss[:, b % 2, t:t + 1])
                    link(last)
                    nc.vector.tensor_scalar(o_ms[:, b % 2, :], o_ss[:, b % 2, :], 1.0 / P, EPS, ALU.mult,
                                            ALU.add).then_inc(oms_done, 1)

            def scale_rows(b):
                v.wait_ge(ors_done, b + 1)
                nc.vector.tensor_tensor(o_rows[:, b % 2], o_rows[:, b % 2],
                                        o_rs[:, b % 2, :].unsqueeze(2).broadcast_to([P, TT, P]),
                                        ALU.mult).then_inc(o_scaled, 1)

            def turned_lo(br_, b):
                n = 4 * br_.n + b
                v.wait_ge(ohi_done, 2 * n + 1)
                if br_.name == "A":
                    nc.vector.scalar_tensor_tensor(oT_lo[:, b, :], T[0][:, :], sub_gain[:, 0:1],
                                                   oT_hi[:, b, :].bitcast(F32), ALU.mult,
                                                   ALU.subtract).then_inc(ohi_done, 1)
                else:
                    nc.vector.tensor_tensor(oT_lo[:, b, :], T[0][:, :], oT_hi[:, b, :].bitcast(F32),
                                            ALU.subtract).then_inc(ohi_done, 1)
                v.wait_ge(ohi_done, 2 * n + 2)
                v.sem_inc(t_free, 1)

            def branch_out(n, c, t):
                dt = 4 * c + t
                k = y_chunk(n, c)
                v.wait_ge(g_done, 4 * k + t + 1)
                v.wait_ge(g_free, 4 * gate_chunk(n, c) + t + 1)
                if n == 0:
                    nc.vector.tensor_tensor(mixed[:, dt, :], G[t][:, :], gT[:, dt, :], ALU.mult).then_inc(g_free, 1)
                    return
                link(nc.vector.tensor_tensor(ytmp[:, :], G[t][:, :], gT[:, dt, :], ALU.mult))
                if n == 1:
                    nc.vector.tensor_tensor(mixed[:, dt, :], mixed[:, dt, :], ytmp[:, :], ALU.add).then_inc(g_free, 1)
                    v.wait_ge(g_free, 4 * k + t + 1)
                    return
                link(nc.vector.tensor_tensor(mixed[:, dt, :], mixed[:, dt, :], ytmp[:, :], ALU.add))
                link(nc.vector.tensor_copy(hT_hi[:, dt, :], mixed[:, dt, :]))
                nc.vector.tensor_tensor(hT_lo[:, dt, :], mixed[:, dt, :], hT_hi[:, dt, :].bitcast(F32),
                                        ALU.subtract).then_inc(g_free, 1)

            def attention(br_):
                groups = dense_groups(br_.dense)
                for s in range(br_.slots):
                    if s < br_.jobs:
                        soft(br_, s)
                    if 0 <= s - br_.lag - 1 < br_.jobs:
                        rows_out(br_, s - br_.lag - 1)
                    if br_.name == "A" and br_.block_scaled(s) is not None:
                        scale_rows(br_.block_scaled(s))
                    if br_.block_turned(s) is not None:
                        turned_lo(br_, br_.block_turned(s))
                    j = s - br_.lag + 1
                    if 0 <= j < br_.jobs:
                        post(br_, j)
                    for g in br_.groups_of(s):
                        kind, n, c, _, t, _, _, last_of_bank, _ = groups[g]
                        if kind == "y" and last_of_bank:
                            branch_out(n, c, t)
                    if br_.name == "B" and at_round[0] < len(rounds):
                        top_round(*rounds[at_round[0]])
                        at_round[0] += 1

            def first_only(flags):
                order = rt[:, 14, :].rearrange("p (t g) -> p t g", g=4)
                last = rt[:, 15, 0:TT]
                link(nc.vector.tensor_tensor(order, flags, falling[:, :].unsqueeze(1).broadcast_to([P, TT, 4]), ALU.mult))
                link(nc.vector.tensor_reduce(last, order, AX.X, ALU.max))
                link(nc.vector.tensor_tensor(flags, order, last.unsqueeze(2).broadcast_to([P, TT, 4]), ALU.is_equal))

            def route():
                v.wait_ge(logT_done, 1)
                nc.vector.tensor_copy(ytmp[0:20, :], S[0][0:20, :]).then_inc(logT_copied, 1)
                v.wait_ge(log_done, 1)
                link(nc.vector.tensor_tensor(logit[:, :, :], T[0][:, 0:TT * 20].rearrange("p (t n) -> p t n", t=TT),
                                             br[:, :].unsqueeze(1).broadcast_to([P, TT, 20]), ALU.add))
                four = lambda n: rt[:, n, :].rearrange("p (t g) -> p t g", g=4)
                one = lambda n: rt[:, n, 0:TT]
                wide = lambda n: one(n).unsqueeze(2).broadcast_to([P, TT, 4])
                gl = logit[:, :, 0:4]
                link(nc.vector.tensor_reduce(one(2), gl, AX.X, ALU.max))
                link(nc.vector.tensor_tensor(four(3), gl, wide(2), ALU.is_equal))
                first_only(four(3))
                el = logit[:, :, 4:20].rearrange("p t (g e) -> p t e g", g=4)
                link(nc.vector.tensor_tensor(ein[:, :, :, :], el, four(3).unsqueeze(2).broadcast_to([P, TT, 4, 4]),
                                             ALU.mult))
                link(nc.vector.tensor_reduce(four(4), ein[:, :, :, :], AX.X, ALU.add))
                link(nc.vector.tensor_reduce(one(5), four(4), AX.X, ALU.max))
                link(nc.vector.tensor_tensor(four(6), four(4), wide(5), ALU.is_equal))
                first_only(four(6))
                link(nc.vector.scalar_tensor_tensor(four(7), four(6), LOWEST, four(4), ALU.mult, ALU.add))
                link(nc.vector.tensor_reduce(one(8), four(7), AX.X, ALU.max))
                link(nc.vector.tensor_tensor(four(9), four(7), wide(8), ALU.is_equal))
                first_only(four(9))
                for k, chosen in enumerate((four(6), four(9))):
                    dst = pick[:, k].rearrange("p t (g e) -> p t g e", g=4)
                    last = nc.vector.tensor_tensor(dst, four(3).unsqueeze(3).broadcast_to([P, TT, 4, 4]),
                                                   chosen.unsqueeze(2).broadcast_to([P, TT, 4, 4]), ALU.mult)
                link(last)
                nc.vector.tensor_tensor(both[:, :, :], pick[:, 0], pick[:, 1], ALU.add).then_inc(picked, 1)
                v.wait_ge(counted, 1)
                earlier = S[1][:, 0:TT * N_EXPERTS].rearrange("p (t e) -> p t e", t=TT)
                for k in range(2):
                    link(nc.vector.tensor_tensor(prod[:, :, :], pick[:, k], earlier, ALU.mult))
                    link(nc.vector.tensor_reduce(rank[:, k], prod[:, :, :], AX.X, ALU.add))
                v.wait_ge(slots_in, 16)
                for k in range(2):
                    for t in range(TT):
                        last = nc.vector.tensor_scalar(slot_onehot[:, k, t, :], slot_id, rank[:, k, t:t + 1], None,
                                                       ALU.is_equal)
                    last = nc.vector.tensor_tensor(pick_token[:, k], pick[:, k],
                                                   tokens[:, :].unsqueeze(2).broadcast_to([P, TT, N_EXPERTS]),
                                                   ALU.mult)
                last.then_inc(onehot_ready, 1)
                v.wait_ge(slots_counted, 1)
                nc.vector.tensor_copy(slot_token[:, :], S[0][:, 0:N_EXPERTS]).then_inc(slots_known, 1)

            def route_rest():
                four = lambda n: rt[:, n, :].rearrange("p (t g) -> p t g", g=4)
                one = lambda n: rt[:, n, 0:TT]
                wide = lambda n: one(n).unsqueeze(2).broadcast_to([P, TT, 4])
                link(nc.vector.tensor_tensor(four(0), logit[:, :, 0:4], wide(2), ALU.subtract))
                link(nc.vector.memset(rt[:, 1, :], 0.0))
                nc.vector.tensor_tensor(rt[:, 1, 0:TT], one(8), one(5), ALU.subtract).then_inc(rexp_in, 1)
                for k in range(2):
                    link(nc.vector.tensor_tensor(prod[:, :, :], pick[:, k],
                                                 eids[:, :].unsqueeze(1).broadcast_to([P, TT, N_EXPERTS]), ALU.mult))
                    link(nc.vector.tensor_reduce(eid[:, k], prod[:, :, :], AX.X, ALU.add))
                link(nc.vector.tensor_scalar(fits[:, :, :], rank[:, :, :], float(CAPACITY), None, ALU.is_lt))
                link(nc.vector.tensor_scalar(left[:, :, :], fits[:, :, :], -1.0, 1.0, ALU.mult, ALU.add))
                for k in range(2):
                    last = nc.vector.tensor_tensor(pick_left[:, k], pick[:, k],
                                                   left[:, k].unsqueeze(2).broadcast_to([P, TT, N_EXPERTS]),
                                                   ALU.mult)
                link(last)
                nc.vector.tensor_reduce(spilled[:, :], pick_left[:, :, :, :].rearrange("p k t e -> p e (k t)"),
                                        AX.X, ALU.add).then_inc(over_summed, 1)
                link(nc.vector.scalar_tensor_tensor(row[:, :, :], eid[:, :, :], float(CAPACITY), rank[:, :, :],
                                                    ALU.mult, ALU.add))
                link(nc.vector.tensor_tensor(row[:, :, :], row[:, :, :], fits[:, :, :], ALU.mult))
                link(nc.vector.tensor_copy(y_row[:, :, :], row[:, :, :]))
                v.wait_ge(over_counted, 1)
                link(nc.vector.scalar_tensor_tensor(spilled[:, :], T[1][:, 0:N_EXPERTS], 0.5, eids_up[:, :],
                                                    ALU.is_gt, ALU.mult))
                link(nc.vector.max(top8[:, :], spilled[:, :]))
                nc.vector.tensor_copy(over_list[:, :], top8[:, :])
                nc.vector.tensor_scalar(over_expert[:, :], top8[:, :], 1.0, None, ALU.subtract).then_inc(over_known, 1)
                v.wait_ge(rexp_out, 1)
                link(nc.vector.tensor_reduce(one(10), rt[:, 0, :].rearrange("p (t g) -> p t g", g=4), AX.X, ALU.add))
                link(nc.vector.tensor_scalar(one(11), rt[:, 1, 0:TT], 1.0, None, ALU.add))
                link(nc.vector.tensor_tensor(one(12), one(10), one(11), ALU.mult))
                link(nc.vector.reciprocal(one(12), one(12)))
                link(nc.vector.tensor_tensor(one(13), one(12), rt[:, 1, 0:TT], ALU.mult))
                for k in range(2):
                    link(nc.vector.tensor_tensor(weight[:, k], one(12 + k), fits[:, k], ALU.mult))
                    link(nc.vector.tensor_tensor(left[:, k], one(12 + k), weight[:, k], ALU.subtract))

            def left_gates():
                for k in range(2):
                    link(nc.vector.tensor_tensor(pick[:, k], pick[:, k],
                                                 left[:, k].unsqueeze(2).broadcast_to([P, TT, N_EXPERTS]), ALU.mult))
                link(nc.vector.tensor_tensor(gate16[:, :, :].rearrange("p e t -> p t e"), pick[:, 0], pick[:, 1],
                                             ALU.add))

            def et_out(e):
                v.wait_ge(et_turned, 2 * e + 2)
                if e >= 2:
                    v.wait_ge(gu_done, e - 1)
                nc.vector.tensor_copy(et[:, e % 2, 512:1024], S[1][:, :]).then_inc(et_dve, 1)

            def experts():
                et_out(0)
                route_rest()
                for e in range(N_EXPERTS + 1):
                    if e < N_EXPERTS:
                        v.wait_ge(silu_done, e + 1)
                        if e >= 2:
                            v.wait_ge(hid_turned, e - 1)
                        nc.vector.tensor_tensor(sq[:, e % 2, FF:2 * FF], sq[:, e % 2, 0:FF], G[e % 2][:, FF:2 * FF],
                                                ALU.mult).then_inc(hid_done, 1)
                    if e + 1 < N_EXPERTS:
                        et_out(e + 1)
                    if e >= 1:
                        v.wait_ge(down_done, 2 * e)
                        if e - 1 >= 4:
                            v.wait_ge(y_out[(e - 1) % 4], 16 * ((e - 1) // 4))
                        nc.vector.tensor_copy(xn[:, (e - 1) % 4, 512:1024], G[3][:, :]).then_inc(y_dve, 1)
                    if e < N_EXPERTS:
                        v.wait_ge(hid_turned, e + 1)
                        if e >= 2:
                            v.wait_ge(down_done, 2 * (e - 1))
                        nc.vector.tensor_copy(pT[:, e % 2, 0:FF], T[e % 2][:, 0:FF]).then_inc(hidT_done, 1)
                for t in range(TT):
                    v.wait_ge(y_back[t], 32)
                    for k in range(2):
                        nc.vector.scalar_tensor_tensor(X[:, t, :], gather_back[2 * t + k], weight[:, k, t:t + 1],
                                                       X[:, t, :], ALU.mult, ALU.add).then_inc(added, 1)
                        v.wait_ge(added, 2 * t + k + 1)

            v.wait_ge(pre_c, 16 * 5)
            for g in range(4):
                nc.vector.memset(falling[:, g:g + 1], float(4 - g))
            nc.vector.tensor_scalar(eids_up[:, :], eids[:, :], 1.0, None, ALU.add).then_inc(pre_eids, 1)
            v.wait_ge(pre_eids, 1)
            for h in range(REL_HEADS):
                v.wait_ge(pre_cp, h + 1)
                last = nc.vector.memset(cqT[0:CHUNK, h % 4, SEQ - CHUNK:SEQ], NEG)
                if A_HEADS <= h < A_HEADS + B_HEADS:
                    last = nc.vector.memset(cqT[CHUNK:P, h % 4, SEQ - 2 * P:SEQ - 2 * P + CHUNK], NEG)
                last.then_inc(pre_set, 1)
            v.wait_ge(pre_half, 2)
            with v.Fori(0, DEPTH) as l:
                links[0] = n_red[0] = n_cms[0] = 0
                norm_scale(0)
                v.wait_ge(pcol_ready, 1)
                norm_lo(0, ROW_MIX)
                v.wait_ge(row_par, 16 * 7)
                link(nc.vector.tensor_copy(wr_hi[:, :, :], wr[:, :, :]))
                nc.vector.tensor_tensor(wr_lo[:, :, :], wr[:, :, :], wr_hi[:, :, :].bitcast(F32),
                                        ALU.subtract).then_inc(wr_split, 1)
                for m in range(2):
                    last = nc.vector.tensor_tensor_reduce(sq[:, m, 0:HD], lam_rows[:, 2 * m * HD:(2 * m + 1) * HD],
                                                          lam_rows[:, (2 * m + 1) * HD:(2 * m + 2) * HD], 1.0, 0.0,
                                                          ALU.mult, ALU.add, lam_sum[:, m:m + 1])
                last.then_inc(lam_summed, 1)
                link(nc.vector.tensor_scalar(q_gain[:, :], pcol[:, ROW_QK:ROW_QK + 6:2], HD ** -0.5, None, ALU.mult))
                link(nc.vector.tensor_tensor(sub_gain[:, :], pcol[:, ROW_SUBLN:ROW_SUBLN + 1], lconst[:, 1:2],
                                             ALU.mult))
                v.wait_ge(lam_exped, 1)
                link(nc.vector.tensor_tensor(lam_dif[:, :], lam_exp[:, 1:2], lam_exp[:, 0:1], ALU.subtract))
                nc.vector.tensor_tensor(neg_lam[:, :], lam_dif[:, :], lconst[:, 0:1],
                                        ALU.subtract).then_inc(gains_ready, 1)
                v.wait_ge(gains_ready, 1)
                at = 0
                for c in range(len(P_CHUNKS)):
                    if c == 1:
                        index_score(1)
                    if P_CHUNKS[c][0] != "Av":
                        chunk_stats(c)
                    if P_CHUNKS[c][0] != "Av":
                        chunk_scale(c)
                    if c == 1:
                        index_score(2)
                        index_score(3)
                    if c >= 2:
                        for i, r in rounds[at:at + CHUNK_ROUNDS]:
                            top_round(i, r)
                        at += CHUNK_ROUNDS
                at_round[0] = at
                for br_ in branches:
                    attention(br_)
                for group in dense_groups([("y", 2)]):
                    if group[7]:
                        branch_out(2, group[2], group[4])
                v.wait_ge(x_back, 16)
                for c in range(2):
                    for t in range(TT):
                        v.wait_ge(g_done, 4 * (OUT_CHUNK + c) + t + 1)
                        rows = X[:, t, c * 512:(c + 1) * 512]
                        src = banks[4 + t] if c == 0 else G[t]
                        nc.vector.tensor_tensor(rows, src[:, :], rows, ALU.add).then_inc(g_free, 1)
                v.wait_ge(g_free, 4 * N_CHUNKS)
                v.wait_ge(gain_in, 16)
                norm_scale(1)
                norm_lo(1, None)
                route()
                experts()
                any_over = v.value_load(over_list[0:1, 0:1], min_val=0, max_val=N_EXPERTS)
                with v.If(any_over > 0):
                    left_gates()
                    with v.Fori(0, MAX_OVER) as i:
                        over = v.value_load(over_list[0:1, bass.ds(i, 1)], min_val=0, max_val=N_EXPERTS)
                        with v.If(over > 0):
                            e = v.value_load(over_expert[0:1, bass.ds(i, 1)], min_val=0, max_val=N_EXPERTS - 1)
                            nc.vector.tensor_copy(gate_cur[:, :], gate16[:, bass.ds(e, 1), :].rearrange("p a t -> p (a t)")
                                                  ).then_inc(e_dve, 1)
                            for f in range(2):
                                v.wait_ge(e_silu, f + 1)
                                nc.vector.tensor_tensor(ptmp[:, 2 + f, :], ptmp[:, f, :], G[2 + f][:, :],
                                                        ALU.mult).then_inc(e_dve, 1)
                                v.wait_ge(e_dve, 2 + 2 * f)
                                nc.vector.tensor_copy(oT_hi[:, f, :], ptmp[:, 2 + f, :]).then_inc(e_dve, 1)
                                v.wait_ge(e_dve, 3 + 2 * f)
                                nc.vector.tensor_tensor(oT_lo[:, f, :], ptmp[:, 2 + f, :], oT_hi[:, f, :].bitcast(F32),
                                                        ALU.subtract).then_inc(e_hid, 1)
                            for c in range(2):
                                for t in range(TT):
                                    v.wait_ge(e_down, TT * c + t + 1)
                                    rows = X[:, t, c * 512:(c + 1) * 512]
                                    nc.vector.scalar_tensor_tensor(rows, banks[4 + t][:, :], gate_cur[:, t:t + 1], rows,
                                                                   ALU.mult, ALU.add).then_inc(e_free, 1)
                            meet(v, expert_end)
                meet(v, layer_end)


def distance_buckets():
    rel = np.arange(SPAN) - (SEQ - 1)
    half = N_BUCKETS // 2
    exact = half // 2
    n = np.abs(rel)
    n_f = np.maximum(n, 1).astype(np.float32)
    large = exact + (np.log(n_f / np.float32(exact)) / np.float32(math.log(MAX_DIST / exact))
                     * np.float32(half - exact)).astype(np.int32)
    large = np.minimum(large, half - 1)
    bucket = np.where(rel > 0, half, 0) + np.where(n < exact, n, large)
    return (bucket[None, :] == np.arange(N_BUCKETS)[:, None]).astype(np.float32)


_INS = ["x", "rel_bias", "norm_mix_g", "w_in", "qk_norm_g", "diff_lambda", "diff_subln_g", "sinks", "w_branch",
        "w_gate", "b_gate", "w_out", "norm_ffn_g", "w_router_group", "b_router_group", "w_router_expert",
        "b_router_expert", "w_ff_gate", "w_ff_up", "w_ff_down"]


def kernel(**inputs):
    import concourse.bacc as bacc
    from concourse.bass_utils import run_bass_kernel_spmd

    nc = bacc.Bacc("TRN2", target_bir_lowering=False, num_devices=1)
    arrays, args = {}, []
    constants = {
        "bucket_onehot": distance_buckets(),
        "identity": np.eye(P, dtype=np.float32),
        "flip": np.ascontiguousarray(np.eye(P, dtype=np.float32)[::-1]),
        "before": np.triu(np.ones((P, P), np.float32), 1),
        "expert_ids": np.tile(np.arange(N_EXPERTS, dtype=np.float32), (P, 1)),
        "token_ids": np.ascontiguousarray(np.arange(SEQ, dtype=np.float32).reshape(TT, P).T),
        "slot_ids": np.tile(np.arange(CAPACITY, dtype=np.float32), (P, 1)),
        "layer_consts": np.array([[i, 1.0 - i] for i in (0.8 - 0.6 * math.exp(-0.3 * l) for l in range(DEPTH))],
                                 np.float32),
    }
    for name in _INS + list(constants):
        a = np.ascontiguousarray(inputs[name] if name in inputs else constants[name])
        arrays[f"in_{name}"] = a
        args.append(nc.dram_tensor(f"in_{name}", a.shape, mybir.dt.from_np(a.dtype), kind="ExternalInput").ap())
    args.append(nc.dram_tensor("out_rows", (1, SEQ, D_MODEL), F32, kind="ExternalOutput").ap())
    hybrid_block(nc, *args)
    r = run_bass_kernel_spmd(nc, [arrays], core_ids=[0])
    return r.results[0]["out_rows"]
```
